# Optimizing a Trainium2 kernel written in Bass

```python
import math
import jax, jax.numpy as jnp
from jax import lax
import numpy as np

D_MODEL = 1024
BATCH = 1
SEQ = 256
DEPTH = 2

SC_GROUPS = 8
SC_WIDTH = 512
SC_WIDTH_CONV = 3
CF_GROUPS = 8
CF_WIDTH = 512
CF_WIDTH_CONV = 31
EV_IN = 3 * SC_WIDTH + 2 * CF_WIDTH
EV_OUT_IN = SC_WIDTH + CF_WIDTH

LRU_HEADS = 8
LRU_WIDTH = 512
LRU_BLOCK = LRU_WIDTH // LRU_HEADS
LRU_CONV = 4
LRU_C = 8.0
DIL_PATTERNS = ((128, 1), (512, 4), (2048, 16))
N_DIL_GROUPS = len(DIL_PATTERNS)
DIL_HEADS = 4
DIL_HEAD_DIM = 64
DIL_OUT = DIL_HEADS * DIL_HEAD_DIM
DIL_QKV = N_DIL_GROUPS * DIL_OUT
ATTN_BLOCK = 128
OD_IN = 2 * LRU_WIDTH + 3 * DIL_QKV
OD_OUT_IN = LRU_WIDTH + DIL_OUT

D_FF = 2816
FFN_CONV = 3

N_EVEN = (DEPTH + 1) // 2
N_ODD = DEPTH // 2
EPS = 1e-6


def rmsnorm(x, g):
    xf = x.astype(jnp.float32)
    y = xf * lax.rsqrt(jnp.mean(xf * xf, axis=-1, keepdims=True) + EPS)
    return (y * g.astype(jnp.float32)).astype(x.dtype)

def layernorm(x, g, b):
    xf = x.astype(jnp.float32)
    mu = jnp.mean(xf, axis=-1, keepdims=True)
    var = jnp.mean(jnp.square(xf - mu), axis=-1, keepdims=True)
    y = (xf - mu) * lax.rsqrt(var + EPS) * g.astype(jnp.float32) + b.astype(jnp.float32)
    return y.astype(x.dtype)

def causal_dwconv(x, w):
    K, C = w.shape
    return lax.conv_general_dilated(
        x, w[:, None, :].astype(x.dtype), window_strides=(1,), padding=[(K - 1, 0)],
        dimension_numbers=("NWC", "WIO", "NWC"), feature_group_count=C)

def even_mixer(h, w_in, sc_conv_w, cf_conv_w, cf_conv_b, cf_ln_g, cf_ln_b, w_out):
    z = h @ w_in
    sc_b, sc_c, sc_x, cf_a, cf_g = jnp.split(
        z, [SC_WIDTH, 2 * SC_WIDTH, 3 * SC_WIDTH, 3 * SC_WIDTH + CF_WIDTH], axis=-1)
    y_sc = sc_b * causal_dwconv(sc_c * sc_x, sc_conv_w)
    u = cf_a * jax.nn.sigmoid(cf_g)
    u = causal_dwconv(u, cf_conv_w) + cf_conv_b
    u = jax.nn.silu(layernorm(u, cf_ln_g, cf_ln_b))
    return jnp.concatenate([y_sc, u], axis=-1) @ w_out

def rg_lru(xc, w_a, b_a, w_x, b_x, lam):
    B, S, W = xc.shape
    xb = xc.reshape(B, S, LRU_HEADS, LRU_BLOCK)
    r = jax.nn.sigmoid(jnp.einsum("bshi,hij->bshj", xb, w_a).reshape(B, S, W) + b_a)
    i = jax.nn.sigmoid(jnp.einsum("bshi,hij->bshj", xb, w_x).reshape(B, S, W) + b_x)
    log_a = -LRU_C * r.astype(jnp.float32) * jax.nn.softplus(-lam.astype(jnp.float32))
    a = jnp.exp(log_a)
    mult = jnp.sqrt(-jnp.expm1(2.0 * log_a))
    bt = mult * (i * xc).astype(jnp.float32)

    def combine(left, right):
        a1, b1 = left
        a2, b2 = right
        return a1 * a2, a2 * b1 + b2

    _, hs = lax.associative_scan(combine, (a, bt), axis=1)
    return hs.astype(xc.dtype)

def dilated_group_attention(q, k, v, window, dilation):
    B, S, H, Dh = q.shape
    L = S // dilation
    nb = -(-L // ATTN_BLOCK)
    Lp = nb * ATTN_BLOCK
    span = window // dilation

    def strided(t):
        t = t.reshape(B, L, dilation, H, Dh).transpose(0, 2, 1, 3, 4)
        t = jnp.pad(t, ((0, 0), (0, 0), (0, Lp - L), (0, 0), (0, 0)))
        return t.reshape(B, dilation, nb, ATTN_BLOCK, H, Dh)

    def with_prev(t):
        prev = jnp.pad(t[:, :, :-1], ((0, 0), (0, 0), (1, 0), (0, 0), (0, 0), (0, 0)))
        return jnp.concatenate([prev, t], axis=3)

    qb = strided(q)
    kk = with_prev(strided(k))
    vv = with_prev(strided(v))
    s = jnp.einsum("brnqhd,brnkhd->brnhqk", qb, kk).astype(jnp.float32)
    qi = jnp.arange(ATTN_BLOCK)[:, None]
    kj = jnp.arange(2 * ATTN_BLOCK)[None, :]
    steps = ATTN_BLOCK + qi - kj
    band = (steps >= 0) & (steps <= span)
    blk_idx = jnp.arange(nb)[:, None, None]
    mask = band[None] & ((blk_idx > 0) | (kj >= ATTN_BLOCK)[None])
    s = jnp.where(mask[None, None, :, None], s, -jnp.inf)
    m = jnp.max(s, axis=-1, keepdims=True)
    p = jnp.exp(s - m)
    den = jnp.sum(p, axis=-1, keepdims=True)
    o = jnp.einsum("brnhqk,brnkhd->brnqhd", p, vv.astype(jnp.float32))
    o = o / jnp.swapaxes(den, 3, 4)
    lse = jnp.swapaxes((m + jnp.log(den))[..., 0], 3, 4)
    o = o.reshape(B, dilation, Lp, H, Dh)[:, :, :L].transpose(0, 2, 1, 3, 4).reshape(B, S, H, Dh)
    lse = lse.reshape(B, dilation, Lp, H)[:, :, :L].transpose(0, 2, 1, 3).reshape(B, S, H)
    return o, lse

def dilated_attention(q, k, v, q_norm_g, k_norm_g):
    B, S, _ = q.shape
    shp = (B, S, N_DIL_GROUPS, DIL_HEADS, DIL_HEAD_DIM)
    qn = rmsnorm(q.reshape(shp), q_norm_g) * (DIL_HEAD_DIM ** -0.5)
    kn = rmsnorm(k.reshape(shp), k_norm_g)
    vr = v.reshape(shp)
    outs, lses = [], []
    for g, (window, dilation) in enumerate(DIL_PATTERNS):
        o, lse = dilated_group_attention(qn[:, :, g], kn[:, :, g], vr[:, :, g], window, dilation)
        outs.append(o)
        lses.append(lse)
    o = jnp.stack(outs)
    wts = jax.nn.softmax(jnp.stack(lses), axis=0)
    out = jnp.einsum("gbsh,gbshd->bshd", wts, o)
    return out.reshape(B, S, DIL_OUT).astype(q.dtype)

def odd_mixer(h, w_in, lru_conv_w, lru_conv_b, lru_wa, lru_ba, lru_wx, lru_bx, lru_lam,
              q_norm_g, k_norm_g, w_out):
    z = h @ w_in
    lru_x, lru_gate, q, k, v = jnp.split(
        z, [LRU_WIDTH, 2 * LRU_WIDTH, 2 * LRU_WIDTH + DIL_QKV, 2 * LRU_WIDTH + 2 * DIL_QKV], axis=-1)
    xc = causal_dwconv(lru_x, lru_conv_w) + lru_conv_b
    y_lru = rg_lru(xc, lru_wa, lru_ba, lru_wx, lru_bx, lru_lam) * jax.nn.gelu(lru_gate)
    y_att = dilated_attention(q, k, v, q_norm_g, k_norm_g)
    return jnp.concatenate([y_lru, y_att], axis=-1) @ w_out

def conv_glu_ffn(h, w_gate, w_up, conv_w, conv_b, w_down):
    g = causal_dwconv(h @ w_gate, conv_w) + conv_b
    return (jax.nn.silu(g) * (h @ w_up)) @ w_down

def first_inputs(seed: int = 0) -> dict:
    key = jax.random.key(seed)
    ks = iter(jax.random.split(key, 40))
    f32 = jnp.float32

    def nrm(shape, fan_in):
        return jax.random.normal(next(ks), shape, f32) * (fan_in ** -0.5)

    def gain(shape):
        return 1.0 + 0.05 * jax.random.normal(next(ks), shape, f32)

    def bias(shape):
        return 0.01 * jax.random.normal(next(ks), shape, f32)

    u = jax.random.uniform(next(ks), (N_ODD, LRU_WIDTH), f32, minval=0.9, maxval=0.999)
    a0 = u ** (1.0 / LRU_C)
    lam = jnp.log(a0) - jnp.log1p(-a0)

    return {
        "x": jax.random.normal(next(ks), (BATCH, SEQ, D_MODEL), f32),
        "mix_norm_g": gain((DEPTH, D_MODEL)),
        "ffn_norm_g": gain((DEPTH, D_MODEL)),
        "ev_w_in": nrm((N_EVEN, D_MODEL, EV_IN), D_MODEL),
        "ev_sc_conv_w": nrm((N_EVEN, SC_WIDTH_CONV, SC_WIDTH), SC_WIDTH_CONV),
        "ev_cf_conv_w": nrm((N_EVEN, CF_WIDTH_CONV, CF_WIDTH), CF_WIDTH_CONV),
        "ev_cf_conv_b": bias((N_EVEN, CF_WIDTH)),
        "ev_cf_ln_g": gain((N_EVEN, CF_WIDTH)),
        "ev_cf_ln_b": bias((N_EVEN, CF_WIDTH)),
        "ev_w_out": nrm((N_EVEN, EV_OUT_IN, D_MODEL), EV_OUT_IN),
        "od_w_in": nrm((N_ODD, D_MODEL, OD_IN), D_MODEL),
        "od_lru_conv_w": nrm((N_ODD, LRU_CONV, LRU_WIDTH), LRU_CONV),
        "od_lru_conv_b": bias((N_ODD, LRU_WIDTH)),
        "od_lru_wa": nrm((N_ODD, LRU_HEADS, LRU_BLOCK, LRU_BLOCK), LRU_BLOCK),
        "od_lru_ba": bias((N_ODD, LRU_WIDTH)),
        "od_lru_wx": nrm((N_ODD, LRU_HEADS, LRU_BLOCK, LRU_BLOCK), LRU_BLOCK),
        "od_lru_bx": bias((N_ODD, LRU_WIDTH)),
        "od_lru_lam": lam,
        "od_q_norm_g": gain((N_ODD, DIL_HEAD_DIM)),
        "od_k_norm_g": gain((N_ODD, DIL_HEAD_DIM)),
        "od_w_out": nrm((N_ODD, OD_OUT_IN, D_MODEL), OD_OUT_IN),
        "ffn_w_gate": nrm((DEPTH, D_MODEL, D_FF), D_MODEL),
        "ffn_w_up": nrm((DEPTH, D_MODEL, D_FF), D_MODEL),
        "ffn_conv_w": nrm((DEPTH, FFN_CONV, D_FF), FFN_CONV),
        "ffn_conv_b": bias((DEPTH, D_FF)),
        "ffn_w_down": nrm((DEPTH, D_FF, D_MODEL), D_FF),
    }

def first_block(x, mix_norm_g, ffn_norm_g,
              ev_w_in, ev_sc_conv_w, ev_cf_conv_w, ev_cf_conv_b, ev_cf_ln_g, ev_cf_ln_b, ev_w_out,
              od_w_in, od_lru_conv_w, od_lru_conv_b, od_lru_wa, od_lru_ba, od_lru_wx, od_lru_bx,
              od_lru_lam, od_q_norm_g, od_k_norm_g, od_w_out,
              ffn_w_gate, ffn_w_up, ffn_conv_w, ffn_conv_b, ffn_w_down):
    for layer in range(DEPTH):
        j = layer // 2
        h = rmsnorm(x, mix_norm_g[layer])
        if layer % 2 == 0:
            x = x + even_mixer(h, ev_w_in[j], ev_sc_conv_w[j], ev_cf_conv_w[j], ev_cf_conv_b[j],
                               ev_cf_ln_g[j], ev_cf_ln_b[j], ev_w_out[j])
        else:
            x = x + odd_mixer(h, od_w_in[j], od_lru_conv_w[j], od_lru_conv_b[j], od_lru_wa[j],
                              od_lru_ba[j], od_lru_wx[j], od_lru_bx[j], od_lru_lam[j],
                              od_q_norm_g[j], od_k_norm_g[j], od_w_out[j])
        h = rmsnorm(x, ffn_norm_g[layer])
        x = x + conv_glu_ffn(h, ffn_w_gate[layer], ffn_w_up[layer], ffn_conv_w[layer],
                             ffn_conv_b[layer], ffn_w_down[layer])
    return x


N_HEADS = 8
HEAD_DIM = 128
N_KV_HEADS = 2
Q_PER_KV = N_HEADS // N_KV_HEADS
ATTN_WIDTH = N_HEADS * HEAD_DIM
KV_WIDTH = N_KV_HEADS * HEAD_DIM
IDX_HEADS = 8
IDX_DIM = 64
TOPK_MAX = 256
Q_BLOCK = 128
ROPE_THETA = 500000.0
ROPE_FRACTION = 4

SSD_EXPAND = 2
SSD_INNER = SSD_EXPAND * D_MODEL
SSD_HEAD_DIM = 64
SSD_HEADS = SSD_INNER // SSD_HEAD_DIM
SSD_GROUPS = 4
SSD_HEADS_PER_GROUP = SSD_HEADS // SSD_GROUPS
SSD_STATE = 128
SSD_CONV = 4
SSD_CHUNK = 128
SSD_CONV_DIM = SSD_INNER + 2 * SSD_GROUPS * SSD_STATE

FFN_DIM = 2816
NORM_EPS = 1e-6

IN_SPLITS = (ATTN_WIDTH, KV_WIDTH, KV_WIDTH, IDX_HEADS * IDX_DIM, IDX_DIM, IDX_HEADS,
             SSD_INNER, SSD_CONV_DIM, SSD_HEADS, D_MODEL, D_MODEL)
IN_COLS = (ATTN_WIDTH + 2 * KV_WIDTH + IDX_HEADS * IDX_DIM + IDX_DIM + IDX_HEADS
           + SSD_INNER + SSD_CONV_DIM + SSD_HEADS + 2 * D_MODEL)


def rms_norm(x, w):
    xf = x.astype(jnp.float32)
    y = xf * lax.rsqrt(jnp.mean(xf * xf, axis=-1, keepdims=True) + NORM_EPS)
    return (y * w.astype(jnp.float32)).astype(x.dtype)

def rope_tables(seq, rot_dim):
    inv = ROPE_THETA ** (-jnp.arange(0, rot_dim, 2, dtype=jnp.float32) / rot_dim)
    ang = jnp.arange(seq, dtype=jnp.float32)[:, None] * inv[None, :]
    return jnp.cos(ang), jnp.sin(ang)

def apply_partial_rope(t, cos, sin):
    half = cos.shape[-1]
    rot = 2 * half
    c = cos[None, :, None, :]
    s = sin[None, :, None, :]
    tf = t[..., :rot].astype(jnp.float32)
    x1, x2 = tf[..., :half], tf[..., half:]
    r = jnp.concatenate([x1 * c - x2 * s, x2 * c + x1 * s], axis=-1).astype(t.dtype)
    return jnp.concatenate([r, t[..., rot:]], axis=-1)

def causal_dwconv_2(u, w, b):
    width = w.shape[0]
    seq = u.shape[1]
    up = jnp.pad(u, ((0, 0), (width - 1, 0), (0, 0)))
    out = b
    for j in range(width):
        out = out + up[:, j:j + seq] * w[j]
    return out

def dsa_attention(q, k, v, q_idx, k_idx, w_idx):
    bsz, seq = q.shape[0], q.shape[1]
    topk = min(TOPK_MAX, seq // 4)
    n_blk = seq // Q_BLOCK
    kv = jnp.concatenate([k, v], axis=-1)
    k_idx_f = k_idx.astype(jnp.float32)
    kpos = jnp.arange(seq)
    scale = HEAD_DIM ** -0.5

    def block(i):
        t0 = i * Q_BLOCK
        sl = lambda a: lax.dynamic_slice_in_dim(a, t0, Q_BLOCK, axis=1)
        qpos = t0 + jnp.arange(Q_BLOCK)
        qi = sl(q_idx).astype(jnp.float32)
        wi = sl(w_idx).astype(jnp.float32)
        rel = jax.nn.relu(jnp.einsum('bqhd,bsd->bqhs', qi, k_idx_f))
        score = jnp.einsum('bqhs,bqh->bqs', rel, wi)
        causal = kpos[None, :] <= qpos[:, None]
        score = jnp.where(causal[None], score, -jnp.inf)
        _, sel = lax.top_k(score, topk)
        valid = sel <= qpos[None, :, None]
        kv_sel = jax.vmap(lambda a, ix: a[ix])(kv, sel)
        k_sel, v_sel = kv_sel[..., :HEAD_DIM], kv_sel[..., HEAD_DIM:]
        qb = sl(q).reshape(bsz, Q_BLOCK, N_KV_HEADS, Q_PER_KV, HEAD_DIM)
        logits = jnp.einsum('bqhgd,bqkhd->bqhgk', qb, k_sel).astype(jnp.float32) * scale
        logits = jnp.where(valid[:, :, None, None, :], logits, -jnp.inf)
        p = jax.nn.softmax(logits, axis=-1).astype(v.dtype)
        o = jnp.einsum('bqhgk,bqkhd->bqhgd', p, v_sel)
        return o.reshape(bsz, Q_BLOCK, ATTN_WIDTH)

    out = lax.map(block, jnp.arange(n_blk))
    return out.transpose(1, 0, 2, 3).reshape(bsz, seq, ATTN_WIDTH)

def ssd_scan(xdt, adt, bm, cm):
    bsz, seq = xdt.shape[0], xdt.shape[1]
    nc = seq // SSD_CHUNK
    X = xdt.reshape(bsz, nc, SSD_CHUNK, SSD_GROUPS, SSD_HEADS_PER_GROUP, SSD_HEAD_DIM)
    Bc = bm.reshape(bsz, nc, SSD_CHUNK, SSD_GROUPS, SSD_STATE)
    Cc = cm.reshape(bsz, nc, SSD_CHUNK, SSD_GROUPS, SSD_STATE)
    A = adt.reshape(bsz, nc, SSD_CHUNK, SSD_GROUPS, SSD_HEADS_PER_GROUP).transpose(0, 3, 4, 1, 2)
    A_cs = jnp.cumsum(A, axis=-1)
    tril = jnp.tril(jnp.ones((SSD_CHUNK, SSD_CHUNK), dtype=bool))
    seg = A_cs[..., :, None] - A_cs[..., None, :]
    Lmat = jnp.exp(jnp.where(tril, seg, -jnp.inf))
    CB = jnp.einsum('bclgn,bcsgn->bcgls', Cc, Bc)
    y_diag = jnp.einsum('bcgls,bgecls,bcsgep->bclgep', CB, Lmat, X)
    decay_states = jnp.exp(A_cs[..., -1:] - A_cs)
    states = jnp.einsum('bclgn,bgecl,bclgep->bcgepn', Bc, decay_states, X)
    chunk_decay = jnp.exp(A_cs[..., -1])

    def step(h, inp):
        s_c, d_c = inp
        return h * d_c[..., None, None] + s_c, h

    h0 = jnp.zeros(states.shape[:1] + states.shape[2:], states.dtype)
    _, states_in = lax.scan(step, h0, (states.transpose(1, 0, 2, 3, 4, 5), chunk_decay.transpose(3, 0, 1, 2)))
    states_in = states_in.transpose(1, 0, 2, 3, 4, 5)
    y_off = jnp.einsum('bclgn,bcgepn,bgecl->bclgep', Cc, states_in, jnp.exp(A_cs))
    return (y_diag + y_off).reshape(bsz, seq, SSD_HEADS, SSD_HEAD_DIM)

def mamba2_branch(z, xbc, dt_raw, conv_w, conv_b, dt_bias, a_log, d_skip, norm_w):
    bsz, seq = z.shape[0], z.shape[1]
    xbc = jax.nn.silu(causal_dwconv_2(xbc, conv_w, conv_b))
    gn = SSD_GROUPS * SSD_STATE
    xs = xbc[..., :SSD_INNER].reshape(bsz, seq, SSD_HEADS, SSD_HEAD_DIM)
    bm = xbc[..., SSD_INNER:SSD_INNER + gn].reshape(bsz, seq, SSD_GROUPS, SSD_STATE)
    cm = xbc[..., SSD_INNER + gn:].reshape(bsz, seq, SSD_GROUPS, SSD_STATE)
    dt = jax.nn.softplus(dt_raw.astype(jnp.float32) + dt_bias.astype(jnp.float32))
    A = -jnp.exp(a_log.astype(jnp.float32))
    y = ssd_scan(xs * dt[..., None], dt * A, bm, cm) + xs * d_skip[:, None]
    y = y.reshape(bsz, seq, SSD_INNER) * jax.nn.silu(z.astype(jnp.float32))
    yg = y.astype(jnp.float32).reshape(bsz, seq, SSD_GROUPS, SSD_INNER // SSD_GROUPS)
    yg = yg * lax.rsqrt(jnp.mean(yg * yg, axis=-1, keepdims=True) + NORM_EPS)
    y = yg.reshape(bsz, seq, SSD_INNER) * norm_w.astype(jnp.float32)
    return y.astype(z.dtype)

def hybrid_mixer(h, w_in, ssd_conv_w, ssd_conv_b, ssd_dt_bias, ssd_a_log, ssd_d, ssd_norm_w,
                 w_proj_attn, w_proj_ssd, w_out):
    bsz, seq = h.shape[0], h.shape[1]
    proj = h @ w_in
    offsets = np.cumsum(np.array(IN_SPLITS))[:-1].tolist()
    (q, k, v, qi, ki, wi, z, xbc, dt_raw, g_attn, g_ssd) = jnp.split(proj, offsets, axis=-1)
    cos_a, sin_a = rope_tables(seq, HEAD_DIM // ROPE_FRACTION)
    cos_i, sin_i = rope_tables(seq, IDX_DIM // ROPE_FRACTION)
    q = apply_partial_rope(q.reshape(bsz, seq, N_HEADS, HEAD_DIM), cos_a, sin_a)
    k = apply_partial_rope(k.reshape(bsz, seq, N_KV_HEADS, HEAD_DIM), cos_a, sin_a)
    v = v.reshape(bsz, seq, N_KV_HEADS, HEAD_DIM)
    qi = apply_partial_rope(qi.reshape(bsz, seq, IDX_HEADS, IDX_DIM), cos_i, sin_i)
    ki = apply_partial_rope(ki.reshape(bsz, seq, 1, IDX_DIM), cos_i, sin_i)[:, :, 0]
    a = dsa_attention(q, k, v, qi, ki, wi)
    b = mamba2_branch(z, xbc, dt_raw, ssd_conv_w, ssd_conv_b, ssd_dt_bias, ssd_a_log, ssd_d, ssd_norm_w)
    merged = jax.nn.sigmoid(g_attn) * (a @ w_proj_attn) + jax.nn.sigmoid(g_ssd) * (b @ w_proj_ssd)
    return merged @ w_out

def conv_glu_ffn_2(h, w_up, conv_w, conv_b, w_down):
    u = causal_dwconv_2(h @ w_up, conv_w, conv_b)
    gate, val = u[..., :FFN_DIM], u[..., FFN_DIM:]
    return (jax.nn.silu(gate) * val) @ w_down

def second_inputs(seed: int = 0) -> dict:
    key = jax.random.key(seed)
    ks = jax.random.split(key, 20)
    nrm = lambda k, shape, s: jax.random.normal(k, shape, jnp.float32) * s
    x = nrm(ks[0], (BATCH, SEQ, D_MODEL), 1.0)
    norm_mix_w = 1.0 + nrm(ks[1], (DEPTH, D_MODEL), 0.02)
    w_in = nrm(ks[2], (DEPTH, D_MODEL, IN_COLS), D_MODEL ** -0.5)
    ssd_conv_w = nrm(ks[3], (DEPTH, SSD_CONV, SSD_CONV_DIM), SSD_CONV ** -0.5)
    ssd_conv_b = nrm(ks[4], (DEPTH, SSD_CONV_DIM), 0.01)
    u = jax.random.uniform(ks[5], (DEPTH, SSD_HEADS), jnp.float32)
    dt0 = jnp.exp(u * (math.log(0.1) - math.log(0.001)) + math.log(0.001))
    ssd_dt_bias = dt0 + jnp.log(-jnp.expm1(-dt0))
    ssd_a_log = jnp.log(jax.random.uniform(ks[6], (DEPTH, SSD_HEADS), jnp.float32, minval=1.0, maxval=16.0))
    ssd_d = 1.0 + nrm(ks[7], (DEPTH, SSD_HEADS), 0.1)
    ssd_norm_w = 1.0 + nrm(ks[8], (DEPTH, SSD_INNER), 0.02)
    w_proj_attn = nrm(ks[9], (DEPTH, ATTN_WIDTH, D_MODEL), ATTN_WIDTH ** -0.5)
    w_proj_ssd = nrm(ks[10], (DEPTH, SSD_INNER, D_MODEL), SSD_INNER ** -0.5)
    w_out = nrm(ks[11], (DEPTH, D_MODEL, D_MODEL), D_MODEL ** -0.5)
    norm_ffn_w = 1.0 + nrm(ks[12], (DEPTH, D_MODEL), 0.02)
    ffn_w_up = nrm(ks[13], (DEPTH, D_MODEL, 2 * FFN_DIM), D_MODEL ** -0.5)
    ffn_conv_w = nrm(ks[14], (DEPTH, FFN_CONV, 2 * FFN_DIM), FFN_CONV ** -0.5)
    ffn_conv_b = nrm(ks[15], (DEPTH, 2 * FFN_DIM), 0.01)
    ffn_w_down = nrm(ks[16], (DEPTH, FFN_DIM, D_MODEL), FFN_DIM ** -0.5)
    norm_final_w = 1.0 + nrm(ks[17], (D_MODEL,), 0.02)
    return {'x': x, 'norm_mix_w': norm_mix_w, 'w_in': w_in, 'ssd_conv_w': ssd_conv_w,
            'ssd_conv_b': ssd_conv_b, 'ssd_dt_bias': ssd_dt_bias, 'ssd_a_log': ssd_a_log,
            'ssd_d': ssd_d, 'ssd_norm_w': ssd_norm_w, 'w_proj_attn': w_proj_attn,
            'w_proj_ssd': w_proj_ssd, 'w_out': w_out, 'norm_ffn_w': norm_ffn_w,
            'ffn_w_up': ffn_w_up, 'ffn_conv_w': ffn_conv_w, 'ffn_conv_b': ffn_conv_b,
            'ffn_w_down': ffn_w_down, 'norm_final_w': norm_final_w}

def second_block(x, norm_mix_w, w_in, ssd_conv_w, ssd_conv_b, ssd_dt_bias, ssd_a_log, ssd_d, ssd_norm_w,
              w_proj_attn, w_proj_ssd, w_out, norm_ffn_w, ffn_w_up, ffn_conv_w, ffn_conv_b,
              ffn_w_down, norm_final_w):
    for l in range(DEPTH):
        h = rms_norm(x, norm_mix_w[l])
        x = x + hybrid_mixer(h, w_in[l], ssd_conv_w[l], ssd_conv_b[l], ssd_dt_bias[l], ssd_a_log[l],
                             ssd_d[l], ssd_norm_w[l], w_proj_attn[l], w_proj_ssd[l], w_out[l])
        h = rms_norm(x, norm_ffn_w[l])
        x = x + conv_glu_ffn_2(h, ffn_w_up[l], ffn_conv_w[l], ffn_conv_b[l], ffn_w_down[l])
    return rms_norm(x, norm_final_w)


def setup_inputs(seed=0):
    out = dict(first_inputs(seed))
    for name, value in second_inputs(seed + 1).items():
        if name != "x":
            out[name + "_2"] = value
    return out


def reference(
    x, mix_norm_g, ffn_norm_g, ev_w_in, ev_sc_conv_w, ev_cf_conv_w, ev_cf_conv_b, ev_cf_ln_g,
    ev_cf_ln_b, ev_w_out, od_w_in, od_lru_conv_w, od_lru_conv_b, od_lru_wa, od_lru_ba,
    od_lru_wx, od_lru_bx, od_lru_lam, od_q_norm_g, od_k_norm_g, od_w_out, ffn_w_gate, ffn_w_up,
    ffn_conv_w, ffn_conv_b, ffn_w_down, norm_mix_w_2, w_in_2, ssd_conv_w_2, ssd_conv_b_2,
    ssd_dt_bias_2, ssd_a_log_2, ssd_d_2, ssd_norm_w_2, w_proj_attn_2, w_proj_ssd_2, w_out_2,
    norm_ffn_w_2, ffn_w_up_2, ffn_conv_w_2, ffn_conv_b_2, ffn_w_down_2, norm_final_w_2,
):
    x = first_block(
        x, mix_norm_g, ffn_norm_g, ev_w_in, ev_sc_conv_w, ev_cf_conv_w, ev_cf_conv_b,
        ev_cf_ln_g, ev_cf_ln_b, ev_w_out, od_w_in, od_lru_conv_w, od_lru_conv_b, od_lru_wa,
        od_lru_ba, od_lru_wx, od_lru_bx, od_lru_lam, od_q_norm_g, od_k_norm_g, od_w_out,
        ffn_w_gate, ffn_w_up, ffn_conv_w, ffn_conv_b, ffn_w_down,
    )
    return second_block(
        x, norm_mix_w_2, w_in_2, ssd_conv_w_2, ssd_conv_b_2, ssd_dt_bias_2, ssd_a_log_2,
        ssd_d_2, ssd_norm_w_2, w_proj_attn_2, w_proj_ssd_2, w_out_2, norm_ffn_w_2, ffn_w_up_2,
        ffn_conv_w_2, ffn_conv_b_2, ffn_w_down_2, norm_final_w_2,
    )


_drawn_inputs = setup_inputs


def setup_inputs(seed=0):
    import zlib

    import numpy as np

    out = dict(_drawn_inputs(seed))
    spreads = {}
    factors = {'ev_cf_conv_b': 2.984,
     'ev_cf_ln_b': 5.711,
     'od_lru_ba': 8.0,
     'od_lru_bx': 8.0,
     'od_q_norm_g': 7.817,
     'od_k_norm_g': 8.0,
     'ffn_conv_b': 5.003,
     'norm_mix_w_2': 2.769,
     'ssd_conv_b_2': 7.348,
     'ssd_norm_w_2': 5.156,
     'norm_ffn_w_2': 3.585,
     'ffn_conv_b_2': 7.187,
     'norm_final_w_2': 8.061,
     'ssd_d_2': 4.177}
    for name, (base, spread) in spreads.items():
        noise = np.random.default_rng([zlib.crc32(name.encode()), seed]).standard_normal(out[name].shape)
        drawn = base * np.exp(spread * noise) if base else spread * noise
        out[name] = __import__('jax').numpy.asarray(drawn.astype(out[name].dtype))
    for name, factor in factors.items():
        out[name] = (out[name] * factor).astype(out[name].dtype)
    return out
```

```python
from contextlib import ExitStack

import numpy as np

import concourse.bass as bass
from concourse import mybir

F32 = mybir.dt.float32
ALU = mybir.AluOpType
ACT = mybir.ActivationFunctionType
AX_X = mybir.AxisListType.X

P = 128
T = 256
D = 1024
DC = D // P
RING = 4
KC = 8
EPS = 1e-6
NEG = -1.0e30
TAKEN = -3.0e38

SC = CF = LRU = 512
NC4 = SC // P
SC_TAPS, CF_TAPS, LRU_TAPS, FFN_TAPS = 3, 31, 4, 3
DIL = ((128, 1), (512, 4), (2048, 16))
DIL_G, DIL_H, DIL_D = 3, 4, 64
DIL_W = DIL_G * DIL_H * DIL_D
FF = 2816
FC = FF // P
DOWN_GROUPS = ((0, 8), (8, 8), (16, 6))

NH, HD, NKV = 8, 128, 2
QPK = NH // NKV
IH, ID = 8, 64
TOPK = min(256, T // 4)
XI = 2048
XCH = XI // P
SH, SG, SN = 32, 4, 128
XBC = XI + 2 * SG * SN
XBC_CH = XBC // P
SSD_TAPS = 4
ROPE_THETA, ROPE_FRACTION = 500000.0, 4
IN_SPLITS = (NH * HD, NKV * HD, NKV * HD, IH * ID, ID, IH, XI, XBC, SH, D, D)

FIRST = [("ev_cf", 4), ("ev_sc", 4), ("ev_b", 2), ("ev_out", 4), ("up0", FC), ("down0", 12),
         ("od_lru", 4), ("od_qk", 6), ("od_v", 3), ("od_out", 4), ("up1", FC), ("down1", 12)]
SECOND = [("kidt", 1), ("wi", 1), ("qi", 2), ("q", 4), ("k", 1), ("v", 1), ("xbc", 12), ("z", 8),
          ("gates", 8), ("pa", 4), ("ps", 8), ("out", 4), ("up", FC), ("down", 12)]


def starts(stages, at):
    where = {}
    for name, n in stages:
        where[name] = at
        at += n
    return where, at


AT, SECOND_AT = starts(FIRST, 0)
AT2, END2 = starts(SECOND, SECOND_AT)
PER_LAYER = END2 - SECOND_AT
assert PER_LAYER % RING == 0
WIDTH = {"od_out": 6 * 256, "wi": KC * IH}
COUNT = dict(FIRST + SECOND)


def columns(parts):
    where, at = {}, 0
    for name, n in parts:
        where[name] = at
        at += n
    return where, at


PCOL, P_FIRST = columns([
    ("mix_g0", DC), ("ffn_g0", DC), ("mix_g1", DC), ("ffn_g1", DC), ("sc_w", SC_TAPS * NC4),
    ("cf_w", CF_TAPS * NC4), ("cf_b", NC4), ("ln_g", NC4), ("ln_b", NC4), ("lru_w", LRU_TAPS * NC4),
    ("lru_b", NC4), ("lru_ba", NC4), ("lru_bx", NC4), ("lam", NC4), ("q_g", 1), ("k_g", 1),
    ("fw0", FFN_TAPS * FC), ("fb0", FC), ("fw1", FFN_TAPS * FC), ("fb1", FC), ("final_g", DC)])
PCOL2, P_LAYER = columns([
    ("mix_g", DC), ("ffn_g", DC), ("ssd_w", SSD_TAPS * XBC_CH), ("ssd_b", XBC_CH), ("ssd_norm", XCH),
    ("ssd_d", XCH), ("dt_bias", 1), ("a_log", 1), ("fw", FFN_TAPS * 2 * FC), ("fb", 2 * FC)])
NPARAM = P_FIRST + 2 * P_LAYER

CCOL, NCONST = columns([
    ("ident", P), ("mean1024", P), ("mean512", P), ("mean64", P), ("swap_attn", P), ("swap_idx", P),
    ("cos_attn", T), ("sin_attn", T), ("cos_idx", T), ("sin_idx", T),
    ("dil0", DIL_G * P), ("dil1", DIL_G * T), ("causal0", P), ("causal1", T), ("tril", T + P)])


class Semaphores:
    pass


class Slab:

    def __init__(self, sems, first, turns):
        self.sems, self.bank = sems, first % RING
        self.use = turns + first // RING
        self.number = turns * RING + first
        self.opening = isinstance(turns, int) and first + RING * turns < RING

    def wait_slot_read(self, eng):
        if not self.opening:
            eng.wait_ge(self.sems.lin_done, self.number - (RING - 1))

    def wait_landed(self, eng):
        eng.wait_ge(self.sems.w_landed[self.bank], (self.use + 1) * 16)

    def wait_bank_free(self, eng):
        if not self.opening:
            eng.wait_ge(self.sems.bank_free[self.bank], self.use)

    def wait_done(self, eng):
        eng.wait_ge(self.sems.lin_done, self.number + 1)

    def wait_released(self, eng):
        eng.wait_ge(self.sems.bank_free[self.bank], self.use + 1)


def each_slab(sems, eng, first, count, turns, body):
    whole = count // RING if count >= 2 * RING else 0
    if whole:
        with eng.Fori(0, whole) as i:
            for j in range(RING):
                body(Slab(sems, first + j, turns + i), i * RING + j, j)
    for n in range(whole * RING, count):
        body(Slab(sems, first + n, turns), n, n % RING)


class Chain:

    def __init__(self, eng, sem, base=0):
        self.eng, self.sem, self.base, self.n = eng, sem, base, 0

    def link(self, ins):
        self.n += 1
        ins.then_inc(self.sem, 1)
        self.eng.wait_ge(self.sem, self.base + self.n)





SOFTPLUS_LINKS = 14
LAM_LINKS = SOFTPLUS_LINKS + 2
DT_LINKS = SOFTPLUS_LINKS + 2
IX_LINKS = 2 * (IH + 1 + 2 * (TOPK // 8) + 2)


def build(nc, dram):
    ctx = ExitStack()
    with ctx:
        def sb(name, shape):
            return ctx.enter_context(nc.sbuf_tensor(name, shape, F32))

        def psum(name, shape):
            return ctx.enter_context(nc.psum_tensor(name, shape, F32))

        def sem(name):
            return ctx.enter_context(nc.semaphore(name))

        s = Semaphores()
        s.loaded = sem("loaded")
        s.pads = sem("pads")
        s.lin_done = sem("lin_done")
        s.norm_sq = sem("norm_sq")
        s.norm_sum = sem("norm_sum")
        s.norm_std = sem("norm_std")
        s.norm_rstd = sem("norm_rstd")
        s.h_ready = sem("h_ready")
        s.cf_sig = sem("cf_sig")
        s.cf_tap = sem("cf_tap")
        s.ln_mean = sem("ln_mean")
        s.ln_diff = sem("ln_diff")
        s.ln_sq = sem("ln_sq")
        s.ln_var = sem("ln_var")
        s.ln_std = sem("ln_std")
        s.ln_rstd = sem("ln_rstd")
        s.ln_scaled = sem("ln_scaled")
        s.u_ready = sem("u_ready")
        s.sc_chain = sem("sc_chain")
        s.y_sc = sem("y_sc")
        s.ffn_t0 = sem("ffn_t0")
        s.ffn_tap = sem("ffn_tap")
        s.ffn_silu = sem("ffn_silu")
        s.ffn2_t0 = sem("ffn2_t0")
        s.ffn2_tap = sem("ffn2_tap")
        s.ffn2_silu = sem("ffn2_silu")
        s.lru_t0 = sem("lru_t0")
        s.lru_tap = sem("lru_tap")
        s.lru_r = sem("lru_r")
        s.lru_i = sem("lru_i")
        s.lru_gates = sem("lru_gates")
        s.lru_a = sem("lru_a")
        s.lru_m2 = sem("lru_m2")
        s.lru_mult = sem("lru_mult")
        s.lru_chain = sem("lru_chain")
        s.lru_y = sem("lru_y")
        s.lam_chain = sem("lam_chain")
        s.lam_e = sem("lam_e")
        s.qk_sq = sem("qk_sq")
        s.qk_sum = sem("qk_sum")
        s.qk_std = sem("qk_std")
        s.qk_chain = sem("qk_chain")
        s.at_logits = sem("at_logits")
        s.at_masked = sem("at_masked")
        s.at_max = sem("at_max")
        s.at_exp = sem("at_exp")
        s.at_chain = sem("at_chain")
        s.at_p = sem("at_p")
        s.at_tr = sem("at_tr")
        s.at_pt = sem("at_pt")
        s.at_pv = sem("at_pv")
        s.at_out = sem("at_out")
        s.rope_rot = sem("rope_rot")
        s.rope_chain = sem("rope_chain")
        s.rope_done = sem("rope_done")
        s.dt_abs = sem("dt_abs")
        s.dt_e = sem("dt_e")
        s.dt_chain = sem("dt_chain")
        s.dt_tr = sem("dt_tr")
        s.dt_tok = sem("dt_tok")
        s.xbc_t0 = sem("xbc_t0")
        s.xbc_tap = sem("xbc_tap")
        s.xbc_silu = sem("xbc_silu")
        s.ix_mm = sem("ix_mm")
        s.ix_rel = sem("ix_rel")
        s.ix_chain = sem("ix_chain")
        s.da_logits = sem("da_logits")
        s.da_max = sem("da_max")
        s.da_exp = sem("da_exp")
        s.da_chain = sem("da_chain")
        s.da_p = sem("da_p")
        s.da_tr = sem("da_tr")
        s.da_pt = sem("da_pt")
        s.da_pv = sem("da_pv")
        s.da_out = sem("da_out")
        s.xt_tr = sem("xt_tr")
        s.xt_copied = sem("xt_copied")
        s.a_exp = sem("a_exp")
        s.ssd_cb = sem("ssd_cb")
        s.ssd_cbm = sem("ssd_cbm")
        s.ssd_abc = sem("ssd_abc")
        s.ssd_seg = sem("ssd_seg")
        s.ssd_exp = sem("ssd_exp")
        s.ssd_m = sem("ssd_m")
        s.ssd_y = sem("ssd_y")
        s.ssd_chain = sem("ssd_chain")
        s.ssd_ydone = sem("ssd_ydone")
        s.bn_sq = sem("bn_sq")
        s.bn_sum = sem("bn_sum")
        s.bn_std = sem("bn_std")
        s.bn_chain = sem("bn_chain")
        s.ps_chain = sem("ps_chain")
        s.final = sem("final")
        s.out_written = sem("out_written")
        s.w_landed = [sem(f"w_landed{i}") for i in range(RING)]
        s.bank_free = [sem(f"bank_free{i}") for i in range(RING)]

        x = sb("x", [P, DC, T])
        h = sb("h", [P, DC, T])
        sq = sb("sq", [P, DC, T])
        hid = sb("hid", [P, 3 * KC, T])
        wring = [sb(f"w{i}", [P, KC, 256]) for i in range(RING)]
        arena = sb("arena", [P, 89 * T])
        par = sb("par", [P, NPARAM, 1])
        cst = sb("cst", [P, NCONST])
        std = sb("std", [P, 2, 2 * T])
        rstd = sb("rstd", [P, 2, 2 * T])
        eps = sb("eps", [P, 1])
        acc = sb("acc", [P, 2, 2, T])
        sil = std[:, :, 0:T]
        score = arena[:, 64 * T:72 * T].rearrange("p (b n) -> p b n", b=2)
        pt = sb("pt", [P, 2, 6 * P])
        small = sb("small", [P, 64])

        lin = [psum(f"lin{i}", [P, 2, T]) for i in range(RING)]
        stat = psum("stat", [P, 2 * T])
        logit = psum("logit", [P, 4, T])
        tr = psum("tr", [P, 2 * T])

        def cut(at, chunks):
            return arena[:, at * T:(at + chunks) * T].rearrange("p (c t) -> p c t", t=T)

        u_pad = arena[:, 0:NC4 * (T + 30)].rearrange("p (c t) -> p c t", c=NC4)
        t_pad = arena[:, 5 * T:5 * T + NC4 * (T + 2)].rearrange("p (c t) -> p c t", c=NC4)
        cf_acc, sc_c, sc_x, sc_b, diff, sc_acc = (cut(10 + 4 * i, 4) for i in range(6))
        lru_xc, lru_gate, lru_r, lru_i, lru_a, lru_th, lru_m, lru_hs = (cut(4 * i, 4) for i in range(8))
        qn, kn = cut(32, 6), cut(38, 6)
        vt = arena[:, 44 * T:50 * T].rearrange("p (t n) -> p t n", t=2)
        qk_sq = cut(50, 4).rearrange("p (b c) t -> p b (c t)", b=2)
        gate_w = arena[:, 60 * T:64 * T].rearrange("p (c n) -> p c n", n=P)
        q2, k2, qi2, ki2 = cut(0, 8), cut(8, 2), cut(10, 4), cut(14, 1)
        v2 = cut(15, 2)
        xbc = cut(17, XBC_CH)
        zs = cut(41, XCH)
        xtok = arena[:, 57 * T:73 * T].rearrange("p (t n) -> p t n", t=2)
        gates = arena[:, 17 * T:33 * T].rearrange("p (m g t) -> p m g t", g=2, t=T)
        rope_raw = cut(73, 4).rearrange("p (b c) t -> p b c t", b=2)
        rope_t = cut(77, 4).rearrange("p (b c) t -> p b c t", b=2)
        ix_rel = cut(73, 8).rearrange("p (b c) t -> p b c t", b=2)
        ix_sc, ix_w = cut(81, 1), cut(82, 2)
        sel = cut(84, 2)
        dtb = cut(86, 3)
        seg = arena[:, 73 * T:76 * T].rearrange("p (b c) -> p b c", b=2)
        seg_e = arena[:, 76 * T:79 * T].rearrange("p (b c) -> p b c", b=2)
        m_buf = arena[:, 0:6 * T].rearrange("p (b c) -> p b c", b=4)
        cbm = arena[:, 6 * T:6 * T + T + P]
        y_raw = cut(79, 2)
        merged = sq
        dscr = rope_t.rearrange("p b c t -> p (b c) t")

        ident = cst[:, CCOL["ident"]:CCOL["ident"] + P]

        def const(name, n=P):
            return cst[:, CCOL[name]:CCOL[name] + n]

        def pcol(name, n=0):
            return par[:, PCOL[name] + n, :]

        def pcol2(l, name, n=0):
            return par[:, P_FIRST + PCOL2[name] + l * P_LAYER + n, :]

        def slabs(eng, stage, body, l=None):
            if l is None:
                each_slab(s, eng, AT[stage], COUNT[stage], 0, body)
            else:
                each_slab(s, eng, AT2[stage], COUNT[stage], l * (PER_LAYER // RING), body)

        def stage_released(eng, stage, l=None):
            at, turns = (AT[stage], 0) if l is None else (AT2[stage], l * (PER_LAYER // RING))
            for n in range(max(0, COUNT[stage] - RING), COUNT[stage]):
                Slab(s, at + n, turns).wait_released(eng)

        block = ctx.enter_context(nc.Block())

        @block.sync
        def _(sp):
            def stream(stage, l=None):
                width = WIDTH.get(stage, KC * 256)

                def body(slab, n, j):
                    slab.wait_slot_read(sp)
                    at = n if l is None else l * COUNT[stage] + n
                    slot = wring[slab.bank][:, :, :].rearrange("p k n -> p (k n)")
                    sp.dma_start(slot[:, 0:width], dram[stage][at, :, :]).then_inc(s.w_landed[slab.bank], 16)
                slabs(sp, stage, body, l)

            for stage, _n in FIRST:
                stream(stage)
            for l in range(2):
                for stage, _n in SECOND:
                    stream(stage, l)
            sp.wait_ge(s.final, 1)
            sp.dma_start(dram["result"], h[:, :, :]).then_inc(s.out_written, 16)
            sp.wait_ge(s.out_written, 16)

        @block.gpsimd
        def _(pool):
            nc.gpsimd.memset(eps[:, :], EPS)
            nc.gpsimd.memset(u_pad[:, :, 0:CF_TAPS - 1], 0.0)
            nc.gpsimd.memset(t_pad[:, :, 0:SC_TAPS - 1], 0.0).then_inc(s.pads, 1)

        @block.tensor
        def _(pe):
            def slab_products(slab, rhs, chunks=KC, stop_group=True):
                slab.wait_landed(pe)
                slab.wait_bank_free(pe)
                w = wring[slab.bank][:, :, :].rearrange("p k n -> p (k n)")[:, 0:chunks * 256]
                w = w.rearrange("p (k n) -> p k n", n=256)
                for half in range(2):
                    for k in range(chunks):
                        mm = nc.tensor.matmul(lin[slab.bank][:, half, :], w[:, k, half * P:half * P + P],
                                              rhs[:, k, :], start=(k == 0), stop=(k == chunks - 1))
                mm.then_inc(s.lin_done, 1)

            def slab_tokens(slab):
                slab.wait_landed(pe)
                slab.wait_bank_free(pe)
                for t in range(2):
                    for k in range(KC):
                        mm = nc.tensor.matmul(lin[slab.bank][:, t, :], h[:, k, t * P:t * P + P],
                                              wring[slab.bank][:, k, :], start=(k == 0), stop=(k == KC - 1))
                mm.then_inc(s.lin_done, 1)

            def products(stage, rhs, l=None, chunks=KC):
                slabs(pe, stage, lambda slab, n, j: slab_products(slab, rhs, chunks), l)

            def down(stage, l=None):
                at, turns = (AT[stage], 0) if l is None else (AT2[stage], l * (PER_LAYER // RING))
                for g, (c0, n) in enumerate(DOWN_GROUPS):
                    for j in range(4):
                        slab_products(Slab(s, at + 4 * g + j, turns), hid[:, c0:c0 + n, :], n)

            def norm_mean(n):
                pe.wait_ge(s.norm_sq, n + 1)
                for k in range(DC):
                    mm = nc.tensor.matmul(stat[:, 0:T], const("mean1024"), sq[:, k, :],
                                          start=(k == 0), stop=(k == DC - 1))
                mm.then_inc(s.norm_sum, 1)
                pe.wait_ge(s.h_ready, n + 1)

            pe.wait_ge(s.loaded, 64)
            norm_mean(0)
            products("ev_cf", h)
            products("ev_sc", h)
            products("ev_b", h)
            pe.wait_ge(s.cf_tap, CF_TAPS * NC4)
            for k in range(NC4):
                mm = nc.tensor.matmul(stat[:, 0:T], const("mean512"), cf_acc[:, k, :],
                                      start=(k == 0), stop=(k == NC4 - 1))
            mm.then_inc(s.ln_mean, 1)
            pe.wait_ge(s.ln_sq, 1)
            for k in range(NC4):
                mm = nc.tensor.matmul(stat[:, T:2 * T], const("mean512"), sq[:, k, :],
                                      start=(k == 0), stop=(k == NC4 - 1))
            mm.then_inc(s.ln_var, 1)
            pe.wait_ge(s.u_ready, 1)
            pe.wait_ge(s.y_sc, 1)
            products("ev_out", hid)
            norm_mean(1)
            products("up0", h)
            stage_released(pe, "up0")
            down("down0")

            norm_mean(2)
            products("od_lru", h)

            def qk_mean(n):
                pe.wait_ge(s.qk_sq, n + 1)
                if n >= 1:
                    pe.wait_ge(s.qk_std, n)
                nc.tensor.matmul(stat[:, :], const("mean64"), qk_sq[:, n % 2, :],
                                 start=True, stop=True).then_inc(s.qk_sum, 1)

            def qk_slab(slab, n, j):
                slab_products(slab, h)
                if n >= 1:
                    qk_mean(n - 1)
            slabs(pe, "od_qk", qk_slab)
            qk_mean(COUNT["od_qk"] - 1)
            slabs(pe, "od_v", lambda slab, n, j: slab_tokens(slab))
            stage_released(pe, "od_lru")
            pe.wait_ge(s.qk_std, COUNT["od_qk"])
            for c in range(NC4):
                mm = nc.tensor.matmul(logit[:, c, :], gate_w[:, c, :], lru_xc[:, c, :], start=True, stop=True)
            mm.then_inc(s.lru_gates, 1)
            for c in range(NC4):
                out = (stat, tr)[c // 2][:, (c % 2) * T:(c % 2 + 1) * T]
                mm = nc.tensor.matmul(out, gate_w[:, NC4 + c, :], lru_xc[:, c, :], start=True, stop=True)
            mm.then_inc(s.lru_gates, 1)
            stage_released(pe, "od_qk")
            pe.wait_ge(s.lru_r, 1)
            pe.wait_ge(s.lru_i, 1)
            stage_released(pe, "od_v")

            def at_logits(u):
                head, t = u // 2, u % 2
                lo = 64 * (head % 2)
                if u >= 1:
                    pe.wait_ge(s.at_masked, u)
                for g in range(DIL_G):
                    c = (g * DIL_H + head) // 2
                    mm = nc.tensor.matmul(logit[:, g, 0:(t + 1) * P], qn[lo:lo + 64, c, t * P:t * P + P],
                                          kn[lo:lo + 64, c, 0:(t + 1) * P], start=True, stop=True)
                mm.then_inc(s.at_logits, 1)

            at_logits(0)
            for u in range(2 * DIL_H):
                head, t = u // 2, u % 2
                lo = 64 * (head % 2)
                if u + 1 < 2 * DIL_H:
                    at_logits(u + 1)
                nb = DIL_G * (t + 1)
                pe.wait_ge(s.at_p, u + 1)
                if u >= 1:
                    pe.wait_ge(s.at_out, u)
                for b in range(nb):
                    where = tr[:, b * P:b * P + P] if b < 4 else stat[:, T + (b - 4) * P:T + (b - 3) * P]
                    g, st = b // (t + 1), b % (t + 1)
                    at = g * (t + 1) * P + st * P
                    mm = nc.tensor.transpose(where, score[:, u % 2, at:at + P], ident)
                mm.then_inc(s.at_tr, 1)
                pe.wait_ge(s.at_pt, u + 1)
                for b in range(nb):
                    g, st = b // (t + 1), b % (t + 1)
                    v_at = (g * DIL_H + head) * DIL_D
                    mm = nc.tensor.matmul(stat[lo:lo + 64, 0:P], vt[:, st, v_at:v_at + DIL_D],
                                          pt[:, u % 2, b * P:b * P + P], start=(b == 0), stop=(b == nb - 1))
                mm.then_inc(s.at_pv, 1)
            pe.wait_ge(s.at_out, 2 * DIL_H)
            pe.wait_ge(s.lru_y, 1)
            products("od_out", hid, chunks=6)
            norm_mean(3)
            products("up1", h)
            stage_released(pe, "up1")
            down("down1")

            def layer(l):
                norm_mean(4 + 2 * l)
                rope_unit = [0]

                def swap(which, n, stage, at=0):
                    r = rope_unit[0]
                    rope_unit[0] += 1
                    Slab(s, AT2[stage] + at, l * (PER_LAYER // RING)).wait_released(pe)
                    if r >= 1:
                        pe.wait_ge(s.rope_done, 8 * l + r)
                    nc.tensor.matmul(stat[:, 0:n], const(which),
                                     rope_raw[:, r % 2, :, :].rearrange("p c t -> p (c t)")[:, 0:n],
                                     start=True, stop=True).then_inc(s.rope_rot, 1)

                def kidt(slab, n, j):
                    slab.wait_landed(pe)
                    slab.wait_bank_free(pe)
                    w = wring[slab.bank]
                    for k in range(KC):
                        nc.tensor.matmul(lin[slab.bank][:, 0, :], w[:, k, 0:P], h[:, k, :],
                                         start=(k == 0), stop=(k == KC - 1))
                    for k in range(KC):
                        mm = nc.tensor.matmul(lin[slab.bank][0:SH, 1, :], w[:, k, P:P + SH], h[:, k, :],
                                              start=(k == 0), stop=(k == KC - 1))
                    mm.then_inc(s.lin_done, 1)
                slabs(pe, "kidt", kidt, l)

                def wi_slab(slab, n, j):
                    slab.wait_landed(pe)
                    slab.wait_bank_free(pe)
                    w = wring[slab.bank][:, :, :].rearrange("p k n -> p (k n)")
                    for t in range(2):
                        for k in range(KC):
                            mm = nc.tensor.matmul(lin[slab.bank][:, t, 0:IH], h[:, k, t * P:t * P + P],
                                                  w[:, k * IH:(k + 1) * IH], start=(k == 0), stop=(k == KC - 1))
                    mm.then_inc(s.lin_done, 1)
                slabs(pe, "wi", wi_slab, l)
                swap("swap_idx", T, "kidt")

                def roped(stage, which):
                    def body(slab, n, j):
                        slab_products(slab, h)
                        if n >= 1:
                            swap(which, 2 * T, stage, n - 1)
                    slabs(pe, stage, body, l)
                    swap(which, 2 * T, stage, COUNT[stage] - 1)
                roped("qi", "swap_idx")
                roped("q", "swap_attn")
                roped("k", "swap_attn")
                slabs(pe, "v", lambda slab, n, j: slab_tokens(slab), l)
                products("xbc", h, l)
                pe.wait_ge(s.rope_done, 8 * l + 8)
                pe.wait_ge(s.dt_chain, DT_LINKS * (l + 1))
                for i, row in enumerate((0, 2)):
                    for t in range(2):
                        mm = nc.tensor.transpose(tr[:, (2 * i + t) * SH:(2 * i + t + 1) * SH],
                                                 dtb[0:SH, row, t * P:t * P + P], ident[0:SH, 0:SH])
                mm.then_inc(s.dt_tr, 1)

                for b in range(4):
                    t, half = b // 2, b % 2
                    if b >= 1:
                        pe.wait_ge(s.ix_rel, 4 * l + b)
                    for i in range(4):
                        head = 4 * half + i
                        lo = 64 * (head % 2)
                        mm = nc.tensor.matmul(logit[:, 2 * (i % 2) + i // 2, 0:(t + 1) * P],
                                              qi2[lo:lo + 64, head // 2, t * P:t * P + P],
                                              ki2[lo:lo + 64, 0, 0:(t + 1) * P], start=True, stop=True)
                    mm.then_inc(s.ix_mm, 1)
                products("z", h, l)

                for u in range(4):
                    t, kv = u // 2, u % 2
                    n = (t + 1) * P
                    if u == 0:
                        pe.wait_ge(s.ix_rel, 4 * l + 4)
                    else:
                        pe.wait_ge(s.da_out, 4 * l + u)
                    for i in range(QPK):
                        mm = nc.tensor.matmul(logit[:, i, 0:n], q2[:, kv * QPK + i, t * P:t * P + P],
                                              k2[:, kv, 0:n], start=True, stop=True)
                    mm.then_inc(s.da_logits, 1)
                    pe.wait_ge(s.da_p, 4 * l + u + 1)
                    if u == 0:
                        pe.wait_ge(s.dt_tok, l + 1)
                    for st in range(t + 1):
                        for i in range(QPK):
                            mm = nc.tensor.transpose((tr, stat)[st][:, i * P:i * P + P],
                                                     score[:, u % 2, i * T + st * P:i * T + st * P + P], ident)
                    mm.then_inc(s.da_tr, 1)
                    pe.wait_ge(s.da_pt, 6 * l + (1, 2, 4, 6)[u])
                    for st in range(t + 1):
                        mm = nc.tensor.matmul(logit[:, 0:2, :].rearrange("p c t -> p (c t)"),
                                              v2[:, st, kv * P:kv * P + P], pt[:, st, 0:4 * P],
                                              start=(st == 0), stop=(st == t))
                    mm.then_inc(s.da_pv, 1)

                pe.wait_ge(s.xbc_silu, 12 * (l + 1))
                pe.wait_ge(s.da_out, 4 * l + 4)
                for b in range(8):
                    t, quad = b // 4, b % 4
                    if b >= 2:
                        pe.wait_ge(s.xt_copied, 8 * l + b - 1)
                    for i in range(4):
                        mm = nc.tensor.transpose((tr, stat)[b % 2][:, i * P:i * P + P],
                                                 xbc[:, 4 * quad + i, t * P:t * P + P], ident)
                    mm.then_inc(s.xt_tr, 1)
                pe.wait_ge(s.xt_copied, 8 * l + 8)

                def running_sums(c):
                    if c >= 2:
                        pe.wait_ge(s.ssd_seg, SH * l + 2 * c - 2)
                    for i in range(2):
                        mm = nc.tensor.matmul(logit[:, 2 * (c % 2) + i, :],
                                              ident[0:SH, 2 * c + i:2 * c + i + 1].to_broadcast([SH, P]),
                                              dtb[0:SH, 2, :], start=True, stop=True)
                    mm.then_inc(s.ssd_abc, 1)

                running_sums(0)
                for c in range(XCH):
                    where = (tr, stat)[c % 2]
                    if c >= 2:
                        pe.wait_ge(s.ssd_ydone, XCH * l + c - 1)
                    if c % 4 == 0:
                        g = c // 4
                        nc.tensor.matmul(where[:, 0:T], xbc[:, XCH + g, 0:P], xbc[:, XCH + SG + g, :],
                                         start=True, stop=True)
                        nc.tensor.matmul(where[:, T:T + P], xbc[:, XCH + g, P:T], xbc[:, XCH + SG + g, P:T],
                                         start=True, stop=True).then_inc(s.ssd_cb, 1)
                    if c + 1 < XCH:
                        running_sums(c + 1)
                    for head in (2 * c, 2 * c + 1):
                        lo = 64 * (head % 2)
                        pe.wait_ge(s.ssd_m, SH * l + head + 1)
                        nc.tensor.matmul(where[lo:lo + 64, 0:T], xtok[:, 0, head * 64:head * 64 + 64],
                                         m_buf[:, head % 4, 0:T], start=True, stop=False)
                        mm = nc.tensor.matmul(where[lo:lo + 64, P:T], xtok[:, 1, head * 64:head * 64 + 64],
                                              m_buf[:, head % 4, T:T + P], start=False, stop=True)
                    mm.then_inc(s.ssd_y, 1)
                products("gates", h, l)
                pe.wait_ge(s.ssd_ydone, XCH * (l + 1))
                for g in range(SG):
                    pe.wait_ge(s.bn_sq, SG * l + g + 1)
                    for k in range(4):
                        mm = nc.tensor.matmul((tr, stat)[g % 2][:, 0:T], const("mean512"),
                                              sq[:, 4 * (g % 2) + k, :], start=(k == 0), stop=(k == 3))
                    mm.then_inc(s.bn_sum, 1)
                products("pa", hid, l)
                pe.wait_ge(s.bn_chain, 2 * SG * (l + 1))
                at, turns = AT2["ps"], l * (PER_LAYER // RING)
                for n in range(8):
                    slab_products(Slab(s, at + n, turns), hid[:, 8 + 8 * (n // 4):16 + 8 * (n // 4), :])
                stage_released(pe, "ps", l)
                products("out", merged, l)
                norm_mean(5 + 2 * l)
                products("up", h, l)
                stage_released(pe, "up", l)
                down("down", l)

            for l in range(2):
                layer(l)
            pe.wait_ge(s.norm_sq, 9)
            for k in range(DC):
                mm = nc.tensor.matmul(stat[:, 0:T], const("mean1024"), sq[:, k, :],
                                      start=(k == 0), stop=(k == DC - 1))
            mm.then_inc(s.norm_sum, 1)

        @block.scalar
        def _(act):
            def norm(n):
                nc.scalar.activation(sq[:, :, :], x[:, :, :], ACT.Square).then_inc(s.norm_sq, 1)
                act.wait_ge(s.norm_sum, n + 1)
                nc.scalar.activation(std[:, 0, 0:T], stat[:, 0:T], ACT.Sqrt, bias=eps[:, :]).then_inc(s.norm_std, 1)

            def ffn(stage, f, l=None):
                def body(slab, n, j):
                    b = j % 2
                    bank = lin[slab.bank]
                    slab.wait_done(act)
                    if l is None:
                        nc.scalar.activation(acc[:, b, 0, :], bank[:, 0, :], ACT.Identity,
                                             bias=pcol(f"fb{f}", n), scale=pcol(f"fw{f}", 2 * FC + n)).then_inc(s.ffn_t0, 1)
                        act.wait_ge(s.ffn_tap, 2 * (f * FC + n) + 2)
                        nc.scalar.activation(sil[:, b, :], acc[:, b, 0, :], ACT.Silu).then_inc(s.ffn_silu, 1)
                    else:
                        for i in range(2):
                            ins = nc.scalar.activation(acc[:, b, i, :], bank[:, i, :], ACT.Identity,
                                                       bias=pcol2(l, "fb", i * FC + n),
                                                       scale=pcol2(l, "fw", 2 * 2 * FC + i * FC + n))
                        ins.then_inc(s.ffn2_t0, 1)
                        act.wait_ge(s.ffn2_tap, 4 * (l * FC + n) + 3)
                        nc.scalar.activation(sil[:, b, :], acc[:, b, 0, :], ACT.Silu).then_inc(s.ffn2_silu, 1)
                slabs(act, stage, body, l)

            act.dma_start(x[:, :, :], dram["x"]).then_inc(s.loaded, 16)
            act.dma_start(cst[:, :], dram["consts"]).then_inc(s.loaded, 16)
            act.dma_start(par[:, :, :], dram["params"].rearrange("p (n a) -> p n a", a=1)).then_inc(s.loaded, 16)
            act.dma_start(gate_w[:, :, :], dram["gate_w"]).then_inc(s.loaded, 16)
            act.wait_ge(s.loaded, 64)
            act.wait_ge(s.pads, 1)

            norm(0)

            def cf_gate(slab, n, j):
                slab.wait_done(act)
                nc.scalar.activation(sq[:, n, :], lin[slab.bank][:, 1, :], ACT.Sigmoid).then_inc(s.cf_sig, 1)
            slabs(act, "ev_cf", cf_gate)

            def sc_copy(slab, n, j):
                slab.wait_done(act)
                nc.scalar.activation(sc_c[:, n, :], lin[slab.bank][:, 0, :], ACT.Copy)
                nc.scalar.activation(sc_x[:, n, :], lin[slab.bank][:, 1, :], ACT.Copy).then_inc(s.bank_free[slab.bank], 1)
            slabs(act, "ev_sc", sc_copy)

            def b_copy(slab, n, j):
                slab.wait_done(act)
                nc.scalar.activation(sc_b[:, 2 * n:2 * n + 2, :], lin[slab.bank][:, :, :], ACT.Copy)\
                    .then_inc(s.bank_free[slab.bank], 1)
            slabs(act, "ev_b", b_copy)
            act.wait_ge(s.ln_diff, 1)
            nc.scalar.activation(sq[:, 0:NC4, :], diff[:, :, :], ACT.Square).then_inc(s.ln_sq, 1)
            act.wait_ge(s.ln_var, 1)
            nc.scalar.activation(std[:, 0, 0:T], stat[:, T:2 * T], ACT.Sqrt, bias=eps[:, :]).then_inc(s.ln_std, 1)
            act.wait_ge(s.ln_scaled, 1)
            for c in range(NC4):
                ins = nc.scalar.activation(hid[:, NC4 + c, :], diff[:, c, :], ACT.Silu,
                                           bias=pcol("ln_b", c), scale=pcol("ln_g", c))
            ins.then_inc(s.u_ready, 1)
            stage_released(act, "ev_out")
            norm(1)
            ffn("up0", 0)
            stage_released(act, "down0")

            norm(2)
            act.wait_ge(s.lam_chain, 1)
            nc.scalar.activation(small[:, 8:12], small[:, 4:8], ACT.Exp, scale=-1.0).then_inc(s.lam_e, 1)

            def lru_in(slab, n, j):
                slab.wait_done(act)
                nc.scalar.activation(lru_gate[:, n, :], lin[slab.bank][:, 1, :], ACT.Gelu_apprx_tanh)
                nc.scalar.activation(lru_xc[:, n, :], lin[slab.bank][:, 0, :], ACT.Identity,
                                     bias=pcol("lru_b", n), scale=pcol("lru_w", 3 * NC4 + n)).then_inc(s.lru_t0, 1)
            slabs(act, "od_lru", lru_in)

            def qk_square(slab, n, j):
                slab.wait_done(act)
                if n >= 2:
                    act.wait_ge(s.qk_sum, n - 1)
                nc.scalar.activation(qk_sq[:, n % 2, :], lin[slab.bank][:, :, :].rearrange("p c t -> p (c t)"),
                                     ACT.Square).then_inc(s.qk_sq, 1)
                if n >= 1:
                    qk_root(n - 1)

            def qk_root(n):
                act.wait_ge(s.qk_sum, n + 1)
                if n >= 2:
                    act.wait_ge(s.qk_chain, n - 1)
                nc.scalar.activation(std[:, n % 2, :], stat[:, :], ACT.Sqrt, bias=eps[:, :]).then_inc(s.qk_std, 1)
            slabs(act, "od_qk", qk_square)
            qk_root(COUNT["od_qk"] - 1)

            def v_copy(slab, n, j):
                slab.wait_done(act)
                nc.scalar.activation(vt[:, :, n * 256:(n + 1) * 256], lin[slab.bank][:, :, :], ACT.Copy)\
                    .then_inc(s.bank_free[slab.bank], 1)
            slabs(act, "od_v", v_copy)
            act.wait_ge(s.lru_gates, 1)
            for c in range(NC4):
                ins = nc.scalar.activation(lru_r[:, c, :], logit[:, c, :], ACT.Sigmoid, bias=pcol("lru_ba", c))
            ins.then_inc(s.lru_r, 1)
            act.wait_ge(s.lru_gates, 2)
            for c in range(NC4):
                ins = nc.scalar.activation(lru_i[:, c, :], (stat, tr)[c // 2][:, (c % 2) * T:(c % 2 + 1) * T],
                                           ACT.Sigmoid, bias=pcol("lru_bx", c))
            ins.then_inc(s.lru_i, 1)
            act.wait_ge(s.lru_r, 1)
            act.wait_ge(s.lam_chain, LAM_LINKS)
            for c in range(NC4):
                nc.scalar.activation(lru_th[:, c, :], lru_r[:, c, :], ACT.Tanh, scale=small[:, c:c + 1])
                ins = nc.scalar.activation(lru_a[:, c, :], lru_r[:, c, :], ACT.Exp, scale=small[:, c:c + 1])
            ins.then_inc(s.lru_a, 1)
            act.wait_ge(s.lru_m2, 1)
            nc.scalar.activation(lru_th[:, :, :], lru_m[:, :, :], ACT.Sqrt).then_inc(s.lru_mult, 1)

            for u in range(2 * DIL_H):
                head, t = u // 2, u % 2
                lo = 64 * (head % 2)
                n = DIL_G * (t + 1) * P
                act.wait_ge(s.at_max, u + 1)
                nc.scalar.activation(score[:, u % 2, 0:n], score[:, u % 2, 0:n], ACT.Exp,
                                     bias=small[:, 16 + u:17 + u], accum_out=small[:, 24 + u:25 + u]).then_inc(s.at_exp, 1)
                act.wait_ge(s.at_tr, u + 1)
                first = min(n, 4 * P)
                ins = nc.scalar.activation(pt[:, u % 2, 0:first], tr[:, 0:first], ACT.Copy)
                if n > first:
                    ins = nc.scalar.activation(pt[:, u % 2, first:n], stat[:, T:T + n - first], ACT.Copy)
                ins.then_inc(s.at_pt, 1)
                act.wait_ge(s.at_pv, u + 1)
                nc.scalar.activation(hid[lo:lo + 64, NC4 + head // 2, t * P:t * P + P], stat[lo:lo + 64, 0:P],
                                     ACT.Copy).then_inc(s.at_out, 1)
            stage_released(act, "od_out")
            norm(3)
            ffn("up1", 1)
            stage_released(act, "down1")

            def layer(l):
                norm(4 + 2 * l)
                rope_unit = [0]

                def raw_copy(slab, chunks):
                    r = rope_unit[0]
                    rope_unit[0] += 1
                    if r >= 2:
                        act.wait_ge(s.rope_done, 8 * l + r - 1)
                    return nc.scalar.activation(rope_raw[:, r % 2, 0:chunks, :], lin[slab.bank][:, 0:chunks, :], ACT.Copy)

                def kidt(slab, n, j):
                    slab.wait_done(act)
                    raw_copy(slab, 1)
                    nc.scalar.activation(dscr[0:SH, 2, :], lin[slab.bank][0:SH, 1, :], ACT.Identity,
                                         bias=pcol2(l, "dt_bias")[0:SH, :]).then_inc(s.bank_free[slab.bank], 1)
                    nc.scalar.activation(small[0:SH, 40:41], pcol2(l, "a_log")[0:SH, :], ACT.Exp).then_inc(s.a_exp, 1)
                slabs(act, "kidt", kidt, l)

                def wi_copy(slab, n, j):
                    slab.wait_done(act)
                    nc.scalar.activation(small[:, 42:58].rearrange("p (t h) -> p t h", t=2),
                                         lin[slab.bank][:, :, 0:IH], ACT.Copy).then_inc(s.bank_free[slab.bank], 1)
                slabs(act, "wi", wi_copy, l)
                act.wait_ge(s.dt_abs, l + 1)
                nc.scalar.activation(dscr[0:SH, 3, :], dscr[0:SH, 3, :], ACT.Exp, scale=-1.0).then_inc(s.dt_e, 1)

                def rope_copy(slab, n, j):
                    slab.wait_done(act)
                    raw_copy(slab, 2).then_inc(s.bank_free[slab.bank], 1)
                for stage in ("qi", "q", "k"):
                    slabs(act, stage, rope_copy, l)

                def v_copy2(slab, n, j):
                    slab.wait_done(act)
                    nc.scalar.activation(v2[:, :, :], lin[slab.bank][:, :, :], ACT.Copy).then_inc(s.bank_free[slab.bank], 1)
                slabs(act, "v", v_copy2, l)

                def xbc_conv(slab, n, j):
                    b = j % 2
                    slab.wait_done(act)
                    for i in range(2):
                        ins = nc.scalar.activation(acc[:, b, i, :], lin[slab.bank][:, i, :], ACT.Identity,
                                                   bias=pcol2(l, "ssd_b", 2 * n + i),
                                                   scale=pcol2(l, "ssd_w", 3 * XBC_CH + 2 * n + i))
                    ins.then_inc(s.xbc_t0, 1)
                    slab.wait_released(act)
                    nc.scalar.activation(xbc.rearrange("p (n i) t -> p n i t", i=2)[:, n, :, :], acc[:, b, :, :],
                                         ACT.Silu).then_inc(s.xbc_silu, 1)
                slabs(act, "xbc", xbc_conv, l)
                act.wait_ge(s.dt_tr, l + 1)
                nc.scalar.activation(pt[:, 1, 5 * P:6 * P], tr[:, 0:4 * SH], ACT.Copy).then_inc(s.dt_tok, 1)

                for b in range(4):
                    n = (b // 2 + 1) * P
                    act.wait_ge(s.ix_mm, 4 * l + b + 1)
                    if b >= 2:
                        act.wait_ge(s.ix_chain, IX_LINKS * l + (0, 0, 4, 8)[b])
                    nc.scalar.activation(ix_rel[:, b % 2, :, 0:n], logit[:, :, 0:n], ACT.Relu).then_inc(s.ix_rel, 1)

                def z_silu(slab, n, j):
                    slab.wait_done(act)
                    nc.scalar.activation(zs.rearrange("p (n i) t -> p n i t", i=2)[:, n, :, :], lin[slab.bank][:, :, :],
                                         ACT.Silu).then_inc(s.bank_free[slab.bank], 1)
                slabs(act, "z", z_silu, l)

                for u in range(4):
                    t, kv = u // 2, u % 2
                    n = (t + 1) * P
                    act.wait_ge(s.da_max, 4 * l + u + 1)
                    for i in range(QPK):
                        ins = nc.scalar.activation(score[:, u % 2, i * T:i * T + n], score[:, u % 2, i * T:i * T + n],
                                                   ACT.Exp, bias=small[:, 16 + i:17 + i], accum_out=small[:, 24 + i:25 + i])
                    ins.then_inc(s.da_exp, 1)
                    act.wait_ge(s.da_tr, 4 * l + u + 1)
                    for st in range(t + 1):
                        nc.scalar.activation(pt[:, st, 0:4 * P], (tr, stat)[st][:, :], ACT.Copy).then_inc(s.da_pt, 1)
                    act.wait_ge(s.da_pv, 4 * l + u + 1)
                    nc.scalar.activation(hid[:, kv * QPK:(kv + 1) * QPK, t * P:t * P + P],
                                         logit[:, 0:2, :].rearrange("p c (a b) -> p (c a) b", b=P), ACT.Copy).then_inc(s.da_out, 1)

                for b in range(8):
                    t, quad = b // 4, b % 4
                    act.wait_ge(s.xt_tr, 8 * l + b + 1)
                    nc.scalar.activation(xtok[:, t, quad * 512:(quad + 1) * 512], (tr, stat)[b % 2][:, :], ACT.Copy)\
                        .then_inc(s.xt_copied, 1)
                with act.Fori(0, XCH) as c:
                    for i in range(2):
                        act.wait_ge(s.ssd_seg, SH * l + 2 * c + i + 1)
                        nc.scalar.activation(seg_e[:, i, :], seg[:, i, :], ACT.Exp).then_inc(s.ssd_exp, 1)
                act.wait_ge(s.ssd_ydone, XCH * (l + 1))

                def gate_sig(slab, n, j):
                    slab.wait_done(act)
                    nc.scalar.activation(gates[:, n, :, :], lin[slab.bank][:, :, :], ACT.Sigmoid)\
                        .then_inc(s.bank_free[slab.bank], 1)
                slabs(act, "gates", gate_sig, l)
                for g in range(SG):
                    nc.scalar.activation(sq[:, 4 * (g % 2):4 * (g % 2) + 4, :], zs[:, 4 * g:4 * g + 4, :], ACT.Square)\
                        .then_inc(s.bn_sq, 1)
                    act.wait_ge(s.bn_sum, SG * l + g + 1)
                    if g >= 2:
                        act.wait_ge(s.bn_chain, 2 * (SG * l + g - 1))
                    nc.scalar.activation(std[:, g % 2, 0:T], (tr, stat)[g % 2][:, 0:T], ACT.Sqrt, bias=eps[:, :])\
                        .then_inc(s.bn_std, 1)
                stage_released(act, "out", l)
                norm(5 + 2 * l)
                ffn("up", None, l)
                stage_released(act, "down", l)

            for l in range(2):
                layer(l)
            norm(8)

        @block.vector
        def _(dve):
            tt, stt, ts = nc.vector.tensor_tensor, nc.vector.scalar_tensor_tensor, nc.vector.tensor_scalar

            def norm(n, gain):
                dve.wait_ge(s.norm_std, n + 1)
                nc.vector.reciprocal(rstd[:, 0, 0:T], std[:, 0, 0:T]).then_inc(s.norm_rstd, 1)
                dve.wait_ge(s.norm_rstd, n + 1)
                for c in range(DC):
                    ins = stt(h[:, c, :], x[:, c, :], gain(c), rstd[:, 0, 0:T], ALU.mult, ALU.mult)
                ins.then_inc(s.h_ready, 1)

            def softplus(chain, out, arg, mag, e, scratch):
                a, b = scratch
                chain.link(ts(a, e, 2.0, None, ALU.add))
                chain.link(nc.vector.reciprocal(b, a))
                chain.link(tt(e, e, b, ALU.mult))
                chain.link(tt(a, e, e, ALU.mult))
                chain.link(ts(b, a, 1.0 / 15.0, None, ALU.mult))
                for odd in (13, 11, 9, 7, 5, 3):
                    chain.link(stt(b, b, 1.0 / odd, a, ALU.add, ALU.mult))
                chain.link(stt(b, b, 1.0, e, ALU.add, ALU.mult))
                chain.link(ts(a, arg, 0.0, None, ALU.max))
                chain.link(stt(out, b, 2.0, a, ALU.mult, ALU.add))

            def add_residual(stage, l=None):
                pairs = x[:, :, :].rearrange("p (j i) t -> p j i t", i=2)

                def body(slab, n, j):
                    slab.wait_done(dve)
                    if n >= 4:
                        Slab(s, (AT[stage] if l is None else AT2[stage]) + n - 4,
                             0 if l is None else l * (PER_LAYER // RING)).wait_released(dve)
                    tt(pairs[:, j, :, :], pairs[:, j, :, :], lin[slab.bank][:, :, :], ALU.add)\
                        .then_inc(s.bank_free[slab.bank], 1)
                at, turns = (AT[stage], 0) if l is None else (AT2[stage], l * (PER_LAYER // RING))
                for n in range(COUNT[stage]):
                    body(Slab(s, at + n, turns), n, n % RING)

            def older_taps(outs, ins_, taps, weight, sem, base, release=None):
                k = len(outs)
                for d in range(1, taps):
                    for i in range(k):
                        if d >= 2:
                            dve.wait_ge(sem, base + (d - 2) * k + i + 1)
                        ins = stt(outs[i][:, d:T], ins_[i][:, 0:T - d], weight(taps - 1 - d, i), outs[i][:, d:T],
                                  ALU.mult, ALU.add)
                        last = d == taps - 1 and i == k - 1
                        ins.then_inc(release if last and release is not None else sem, 1)
                return base + (taps - 1) * k

            def ffn(stage, f, l=None):
                def body(slab, n, j):
                    b = j % 2
                    bank = lin[slab.bank]
                    if l is None:
                        dve.wait_ge(s.ffn_t0, f * FC + n + 1)
                        older_taps([acc[:, b, 0, :]], [bank[:, 0, :]], FFN_TAPS,
                                   lambda k, i: pcol(f"fw{f}", k * FC + n), s.ffn_tap, 2 * (f * FC + n))
                        dve.wait_ge(s.ffn_silu, f * FC + n + 1)
                        tt(hid[:, n, :], sil[:, b, :], bank[:, 1, :], ALU.mult).then_inc(s.bank_free[slab.bank], 1)
                    else:
                        dve.wait_ge(s.ffn2_t0, l * FC + n + 1)
                        done = older_taps([acc[:, b, 0, :], acc[:, b, 1, :]], [bank[:, 0, :], bank[:, 1, :]], FFN_TAPS,
                                          lambda k, i: pcol2(l, "fw", k * 2 * FC + i * FC + n), s.ffn2_tap,
                                          4 * (l * FC + n))
                        dve.wait_ge(s.ffn2_silu, l * FC + n + 1)
                        dve.wait_ge(s.ffn2_tap, done)
                        tt(hid[:, n, :], sil[:, b, :], acc[:, b, 1, :], ALU.mult).then_inc(s.bank_free[slab.bank], 1)
                slabs(dve, stage, body, l)

            dve.wait_ge(s.loaded, 64)
            dve.wait_ge(s.pads, 1)
            lam = par[:, PCOL["lam"]:PCOL["lam"] + NC4, :].rearrange("p c a -> p (c a)")
            chain = Chain(dve, s.lam_chain)
            norm(0, lambda c: pcol("mix_g0", c))

            def cf_u(slab, n, j):
                dve.wait_ge(s.cf_sig, n + 1)
                tt(u_pad[:, n, CF_TAPS - 1:], lin[slab.bank][:, 0, :], sq[:, n, :], ALU.mult)\
                    .then_inc(s.bank_free[slab.bank], 1)
            slabs(dve, "ev_cf", cf_u)
            stage_released(dve, "ev_cf")
            for c in range(NC4):
                ts(cf_acc[:, c, :], u_pad[:, c, CF_TAPS - 1:], pcol("cf_w", (CF_TAPS - 1) * NC4 + c), pcol("cf_b", c),
                   ALU.mult, ALU.add).then_inc(s.cf_tap, 1)
            with dve.Fori(0, (CF_TAPS - 1) // 3) as i:
                for d in range(3):
                    for c in range(NC4):
                        dve.wait_ge(s.cf_tap, (i * 3 + d) * NC4 + c + 1)
                        stt(cf_acc[:, c, :], u_pad[:, c, bass.ds(i * 3 + d, T)], pcol("cf_w", (i * 3 + d) * NC4 + c),
                            cf_acc[:, c, :], ALU.mult, ALU.add).then_inc(s.cf_tap, 1)
            stage_released(dve, "ev_sc")
            stage_released(dve, "ev_b")
            sc = Chain(dve, s.sc_chain)
            sc.link(tt(t_pad[:, :, SC_TAPS - 1:], sc_c[:, :, :], sc_x[:, :, :], ALU.mult))
            dve.wait_ge(s.ln_mean, 1)
            tt(diff[:, :, :], cf_acc[:, :, :], stat[:, 0:T].unsqueeze(1).to_broadcast([P, NC4, T]), ALU.subtract)\
                .then_inc(s.ln_diff, 1)
            for c in range(NC4):
                ins = ts(sc_acc[:, c, :], t_pad[:, c, 2:], pcol("sc_w", 2 * NC4 + c), None, ALU.mult)
            sc.link(ins)
            for k in (1, 0):
                for c in range(NC4):
                    ins = stt(sc_acc[:, c, :], t_pad[:, c, k:k + T], pcol("sc_w", k * NC4 + c), sc_acc[:, c, :],
                              ALU.mult, ALU.add)
                sc.link(ins)
            tt(hid[:, 0:NC4, :], sc_acc[:, :, :], sc_b[:, :, :], ALU.mult).then_inc(s.y_sc, 1)
            dve.wait_ge(s.ln_std, 1)
            nc.vector.reciprocal(rstd[:, 0, 0:T], std[:, 0, 0:T]).then_inc(s.ln_rstd, 1)
            dve.wait_ge(s.ln_rstd, 1)
            dve.wait_ge(s.ln_diff, 1)
            tt(diff[:, :, :], diff[:, :, :], rstd[:, 0, 0:T].unsqueeze(1).to_broadcast([P, NC4, T]), ALU.mult)\
                .then_inc(s.ln_scaled, 1)
            add_residual("ev_out")
            stage_released(dve, "ev_out")
            norm(1, lambda c: pcol("ffn_g0", c))
            ffn("up0", 0)
            add_residual("down0")
            stage_released(dve, "down0")

            norm(2, lambda c: pcol("mix_g1", c))
            chain.link(stt(small[:, 4:8], lam, -1.0, lam, ALU.mult, ALU.max))
            ts(small[:, 12:16], lam, -1.0, None, ALU.mult)
            dve.wait_ge(s.lam_e, 1)
            softplus(chain, small[:, 4:8], small[:, 12:16], None, small[:, 8:12], (small[:, 58:62], small[:, 32:36]))
            chain.link(ts(small[:, 0:4], small[:, 4:8], -8.0, None, ALU.mult))
            assert chain.n == LAM_LINKS

            def lru_conv(slab, n, j):
                dve.wait_ge(s.lru_t0, n + 1)
                older_taps([lru_xc[:, n, :]], [lin[slab.bank][:, 0, :]], LRU_TAPS,
                           lambda k, i: pcol("lru_w", k * NC4 + n), s.lru_tap, 2 * n, s.bank_free[slab.bank])
            slabs(dve, "od_lru", lru_conv)

            def qk_norm(slab, n, j):
                dve.wait_ge(s.qk_std, n + 1)
                nc.vector.reciprocal(rstd[:, n % 2, :], std[:, n % 2, :]).then_inc(s.qk_chain, 1)
                dve.wait_ge(s.qk_chain, n + 1)
                stt(qn[:, n, :], lin[slab.bank][:, 0, :], pcol("q_g"), rstd[:, n % 2, 0:T], ALU.mult, ALU.mult)
                stt(kn[:, n, :], lin[slab.bank][:, 1, :], pcol("k_g"), rstd[:, n % 2, T:2 * T], ALU.mult, ALU.mult)\
                    .then_inc(s.bank_free[slab.bank], 1)
            slabs(dve, "od_qk", qk_norm)

            lc = Chain(dve, s.lru_chain)
            dve.wait_ge(s.lru_i, 1)
            stage_released(dve, "od_lru")
            lc.link(tt(lru_i[:, :, :], lru_i[:, :, :], lru_xc[:, :, :], ALU.mult))
            dve.wait_ge(s.lru_a, 1)
            lc.link(ts(lru_m[:, :, :], lru_th[:, :, :], -1.0, 1.0, ALU.mult, ALU.add))
            lc.link(nc.vector.reciprocal(lru_r[:, :, :], lru_m[:, :, :]))
            stt(lru_m[:, :, :], lru_th[:, :, :], -2.0, lru_r[:, :, :], ALU.mult, ALU.mult).then_inc(s.lru_m2, 1)
            dve.wait_ge(s.lru_mult, 1)
            lc.link(tt(lru_i[:, :, :], lru_i[:, :, :], lru_th[:, :, :], ALU.mult))
            for c in range(NC4):
                ins = nc.vector.tensor_tensor_scan(lru_hs[:, c, :], lru_a[:, c, :], lru_i[:, c, :], 0.0, ALU.mult, ALU.add)
            lc.link(ins)
            tt(hid[:, 0:NC4, :], lru_hs[:, :, :], lru_gate[:, :, :], ALU.mult).then_inc(s.lru_y, 1)

            ac = Chain(dve, s.at_chain)
            for u in range(2 * DIL_H):
                head, t = u // 2, u % 2
                n = (t + 1) * P
                dve.wait_ge(s.at_logits, u + 1)
                if u >= 2:
                    dve.wait_ge(s.at_tr, u - 1)
                sc3 = score[:, u % 2, 0:DIL_G * n].rearrange("p (g k) -> p g k", g=DIL_G)
                stt(sc3, logit[:, 0:DIL_G, 0:n], DIL_D ** -0.5,
                    const(f"dil{t}", DIL_G * n).rearrange("p (g k) -> p g k", g=DIL_G), ALU.mult, ALU.add)\
                    .then_inc(s.at_masked, 1)
                dve.wait_ge(s.at_masked, u + 1)
                nc.vector.tensor_reduce(small[:, 16 + u:17 + u], score[:, u % 2, 0:DIL_G * n], AX_X, ALU.max, negate=True)\
                    .then_inc(s.at_max, 1)
                dve.wait_ge(s.at_exp, u + 1)
                ac.link(nc.vector.reciprocal(small[:, 32 + u:33 + u], small[:, 24 + u:25 + u]))
                ts(score[:, u % 2, 0:DIL_G * n], score[:, u % 2, 0:DIL_G * n], small[:, 32 + u:33 + u], None, ALU.mult)\
                    .then_inc(s.at_p, 1)
            add_residual("od_out")
            stage_released(dve, "od_out")
            norm(3, lambda c: pcol("ffn_g1", c))
            ffn("up1", 1)
            add_residual("down1")
            stage_released(dve, "down1")

            def layer(l):
                norm(4 + 2 * l, lambda c: pcol2(l, "mix_g", c))
                rope_unit = [0]

                def rope(out, chunks, which):
                    r = rope_unit[0]
                    rope_unit[0] += 1
                    base = 8 * 2 * l + 2 * r
                    raw, part = rope_raw[:, r % 2, 0:chunks, :], rope_t[:, 0, 0:chunks, :]
                    cos, sin = (const(f"{f}_{which}", T).unsqueeze(1).to_broadcast([P, chunks, T])
                                for f in ("cos", "sin"))
                    dve.wait_ge(s.rope_rot, 8 * l + r + 1)
                    tt(out, raw, cos, ALU.mult).then_inc(s.rope_chain, 1)
                    tt(part, stat[:, 0:chunks * T].rearrange("p (c t) -> p c t", t=T), sin, ALU.mult)\
                        .then_inc(s.rope_chain, 1)
                    dve.wait_ge(s.rope_chain, base + 2)
                    tt(out, out, part, ALU.add).then_inc(s.rope_done, 1)

                rope(ki2[:, :, :], 1, "idx")
                dt, adt, cum = (dtb[0:SH, i, :] for i in range(3))
                arg, mag = dscr[0:SH, 2, :], dscr[0:SH, 3, :]
                Slab(s, AT2["kidt"], l * (PER_LAYER // RING)).wait_released(dve)
                stt(mag, arg, -1.0, arg, ALU.mult, ALU.max).then_inc(s.dt_abs, 1)
                dve.wait_ge(s.dt_e, l + 1)
                ch = Chain(dve, s.dt_chain, DT_LINKS * l)
                softplus(ch, dt, arg, None, mag, (adt, cum))
                dve.wait_ge(s.a_exp, l + 1)
                ch.link(ts(adt, dt, small[0:SH, 40:41], -1.0, ALU.mult, ALU.mult))
                ch.link(nc.vector.tensor_tensor_scan(cum, adt, adt, 0.0, ALU.add, ALU.min))
                assert ch.n == DT_LINKS

                for stage, dest, which in (("qi", qi2, "idx"), ("q", q2, "attn"), ("k", k2, "attn")):
                    for n in range(COUNT[stage]):
                        rope(dest[:, 2 * n:2 * n + 2, :], 2, which)

                def xbc_taps(slab, n, j):
                    b = j % 2
                    dve.wait_ge(s.xbc_t0, 12 * l + n + 1)
                    older_taps([acc[:, b, i, :] for i in range(2)], [lin[slab.bank][:, i, :] for i in range(2)],
                               SSD_TAPS, lambda k, i: pcol2(l, "ssd_w", k * XBC_CH + 2 * n + i), s.xbc_tap,
                               5 * (12 * l + n), s.bank_free[slab.bank])
                slabs(dve, "xbc", xbc_taps, l)

                ix = Chain(dve, s.ix_chain, IX_LINKS * l)
                for t in range(2):
                    n = (t + 1) * P
                    row = ix_sc[:, 0, 0:n]
                    for head in range(IH):
                        b, i = 2 * t + head // 4, 2 * (head % 2) + head % 4 // 2
                        if head % 4 == 0:
                            dve.wait_ge(s.ix_rel, 4 * l + b + 1)
                        w = small[:, 42 + t * IH + head:43 + t * IH + head]
                        if head == 0:
                            ix.link(ts(row, ix_rel[:, b % 2, i, 0:n], w, None, ALU.mult))
                        else:
                            ix.link(stt(row, ix_rel[:, b % 2, i, 0:n], w, row, ALU.mult, ALU.add))
                    ix.link(tt(row, row, const(f"causal{t}", n), ALU.add))
                    now = row
                    for r in range(TOPK // 8):
                        nxt = ix_w[:, r % 2, 0:n]
                        ix.link(nc.vector.max(small[:, 0:8], now))
                        ix.link(nc.vector.match_replace(nxt, small[:, 0:8], now, TAKEN))
                        now = nxt
                    ix.link(ts(sel[:, t, 0:n], now, TAKEN / 2, NEG, ALU.is_gt, ALU.mult))
                    ins = tt(sel[:, t, 0:n], sel[:, t, 0:n], const(f"causal{t}", n), ALU.add)
                    ix.link(ins)
                assert ix.n == IX_LINKS

                dc = Chain(dve, s.da_chain, 8 * l)
                for u in range(4):
                    t, kv = u // 2, u % 2
                    n = (t + 1) * P
                    dve.wait_ge(s.da_logits, 4 * l + u + 1)
                    sc4 = score[:, u % 2, :].rearrange("p (i k) -> p i k", i=4)[:, :, 0:n]
                    for i in range(QPK):
                        ins = stt(sc4[:, i, :], logit[:, i, 0:n], HD ** -0.5, sel[:, t, 0:n], ALU.mult, ALU.add)
                    dc.link(ins)
                    nc.vector.tensor_reduce(small[:, 16:20], sc4, AX_X, ALU.max, negate=True).then_inc(s.da_max, 1)
                    dve.wait_ge(s.da_exp, 4 * l + u + 1)
                    dc.link(nc.vector.reciprocal(small[:, 32:36], small[:, 24:28]))
                    for i in range(QPK):
                        ins = ts(sc4[:, i, :], sc4[:, i, :], small[:, 32 + i:33 + i], None, ALU.mult)
                    ins.then_inc(s.da_p, 1)

                dt_tok = pt[:, 1, 5 * P:6 * P].rearrange("p (i t h) -> p i t h", i=2, t=2)
                dve.wait_ge(s.dt_tok, l + 1)

                def ssd_seg(c, j, i):
                    head = 2 * c + i
                    dve.wait_ge(s.ssd_abc, XCH * l + c + 1)
                    for t, (lo, n) in enumerate(((0, T), (T, P))):
                        ins = ts(seg[:, i, lo:lo + n], logit[:, 2 * (j % 2) + i, T - n:T], dt_tok[:, 1, t, bass.ds(head, 1)],
                                 0.0, ALU.subtract, ALU.min)
                    ins.then_inc(s.ssd_seg, 1)

                def ssd_m(c, j, i):
                    head = 2 * c + i
                    dve.wait_ge(s.ssd_exp, SH * l + head + 1)
                    for t, (lo, n) in enumerate(((0, T), (T, P))):
                        ins = stt(m_buf[:, 2 * (j % 2) + i, lo:lo + n], seg_e[:, i, lo:lo + n],
                                  dt_tok[:, 0, t, bass.ds(head, 1)], cbm[:, lo:lo + n], ALU.mult, ALU.mult)
                    ins.then_inc(s.ssd_m, 1)

                def ssd_out(c, j):
                    dve.wait_ge(s.ssd_y, XCH * l + c + 1)
                    stt(y_raw[:, j % 2, :], xbc[:, c, :], pcol2(l, "ssd_d", c), (tr, stat)[j % 2][:, 0:T],
                        ALU.mult, ALU.add).then_inc(s.ssd_chain, 1)
                    dve.wait_ge(s.ssd_chain, XCH * l + c + 1)
                    tt(zs[:, c, :], y_raw[:, j % 2, :], zs[:, c, :], ALU.mult).then_inc(s.ssd_ydone, 1)

                def ssd_group(g, first):
                    dve.wait_ge(s.ssd_cb, SG * l + g + 1)
                    tt(cbm[:, 0:T], tr[:, 0:T], const("tril", T + P)[:, 0:T], ALU.mult)
                    tt(cbm[:, T:T + P], tr[:, T:T + P], const("tril", T + P)[:, T:], ALU.mult).then_inc(s.ssd_cbm, 1)
                    dve.wait_ge(s.ssd_cbm, SG * l + g + 1)
                    for j in range(4):
                        c = 4 * g + j
                        ssd_seg(c, j, 0)
                        ssd_seg(c, j, 1)
                        ssd_m(c, j, 0)
                        ssd_m(c, j, 1)
                        if j >= 1 or not first:
                            ssd_out(c - 1, j + 3)
                ssd_group(0, True)
                with dve.Fori(1, SG) as g:
                    ssd_group(g, False)
                ssd_out(XCH - 1, 3)

                for g in range(SG):
                    dve.wait_ge(s.bn_std, SG * l + g + 1)
                    nc.vector.reciprocal(rstd[:, g % 2, 0:T], std[:, g % 2, 0:T]).then_inc(s.bn_chain, 1)
                    dve.wait_ge(s.bn_chain, 2 * (SG * l + g) + 1)
                    for c in range(4 * g, 4 * g + 4):
                        ins = stt(hid[:, 8 + c, :], zs[:, c, :], pcol2(l, "ssd_norm", c), rstd[:, g % 2, 0:T],
                                  ALU.mult, ALU.mult)
                    ins.then_inc(s.bn_chain, 1)

                def pa(slab, n, j):
                    slab.wait_done(dve)
                    tt(merged[:, 2 * n:2 * n + 2, :], lin[slab.bank][:, :, :], gates[:, 2 * n:2 * n + 2, 0, :], ALU.mult)\
                        .then_inc(s.bank_free[slab.bank], 1)
                slabs(dve, "pa", pa, l)
                stage_released(dve, "pa", l)
                pc = Chain(dve, s.ps_chain, 8 * l)
                for n in range(8):
                    slab = Slab(s, AT2["ps"] + n, l * (PER_LAYER // RING))
                    j = n % 4
                    slab.wait_done(dve)
                    if n >= 4:
                        Slab(s, AT2["ps"] + n - 4, l * (PER_LAYER // RING)).wait_released(dve)
                    part = acc[:, n % 2, :, :]
                    pc.link(tt(part, lin[slab.bank][:, :, :], gates[:, 2 * j:2 * j + 2, 1, :], ALU.mult))
                    tt(merged[:, 2 * j:2 * j + 2, :], merged[:, 2 * j:2 * j + 2, :], part, ALU.add)\
                        .then_inc(s.bank_free[slab.bank], 1)
                add_residual("out", l)
                stage_released(dve, "out", l)
                norm(5 + 2 * l, lambda c: pcol2(l, "ffn_g", c))
                ffn("up", None, l)
                add_residual("down", l)
                stage_released(dve, "down", l)

            for l in range(2):
                layer(l)
            dve.wait_ge(s.norm_std, 9)
            nc.vector.reciprocal(rstd[:, 0, 0:T], std[:, 0, 0:T]).then_inc(s.norm_rstd, 1)
            dve.wait_ge(s.norm_rstd, 9)
            for c in range(DC):
                ins = stt(h[:, c, :], x[:, c, :], pcol("final_g", c), rstd[:, 0, 0:T], ALU.mult, ALU.mult)
            ins.then_inc(s.final, 1)


def constants():
    c = np.zeros((P, NCONST), np.float32)

    def put(name, a):
        c[:a.shape[0], CCOL[name]:CCOL[name] + a.shape[1]] = a

    put("ident", np.eye(P))
    put("mean1024", np.full((P, P), 1 / 1024))
    put("mean512", np.full((P, P), 1 / 512))
    put("mean64", np.kron(np.eye(2), np.full((64, 64), 1 / 64)))
    for name, dim, heads in (("attn", HD, 1), ("idx", ID, 2)):
        rot = dim // ROPE_FRACTION
        half = rot // 2
        inv = np.float32(ROPE_THETA) ** (-np.arange(0, rot, 2, dtype=np.float32) / np.float32(rot))
        ang = np.arange(T, dtype=np.float32)[None, :] * inv.astype(np.float32)[:, None]
        swap, cos, sin = np.zeros((dim, dim)), np.ones((dim, T), np.float32), np.zeros((dim, T), np.float32)
        for i in range(half):
            swap[i, i + half] = swap[i + half, i] = 1
        cos[0:half] = cos[half:rot] = np.cos(ang)
        sin[0:half], sin[half:rot] = -np.sin(ang), np.sin(ang)
        put(f"swap_{name}", np.kron(np.eye(heads), swap))
        put(f"cos_{name}", np.tile(cos, (heads, 1)))
        put(f"sin_{name}", np.tile(sin, (heads, 1)))
    q, k = np.arange(T)[:, None], np.arange(T)[None, :]
    for t in range(2):
        rows, n = slice(t * P, (t + 1) * P), (t + 1) * P
        seen = [(k <= q) & (q - k <= w) & ((q - k) % d == 0) for w, d in DIL]
        put(f"dil{t}", np.concatenate([np.where(m, 0.0, NEG)[rows, :n] for m in seen], axis=1))
        put(f"causal{t}", np.where(k <= q, 0.0, NEG)[rows, :n])
    after = (k >= q).astype(np.float32)
    put("tril", np.concatenate([after[0:P, :], after[P:, P:]], axis=1))
    return c


def slab_of(w, cols, chunks=None):
    kc = w.shape[0] // P
    w = w.reshape(kc, P, w.shape[1])
    return np.stack([np.ascontiguousarray(w[:, :, c].transpose(1, 0, 2)).reshape(P, -1) for c in cols])


def tile(n, at=0):
    return np.arange(at + n * P, at + n * P + P)


def pair(a, b, at=0, at_b=None):
    return np.concatenate([tile(a, at), tile(b, at if at_b is None else at_b)])


def pairs(n, at=0):
    return [pair(2 * j, 2 * j + 1, at) for j in range(n // 2)]


def down_slabs(w, groups):
    out = []
    for c0, n in groups:
        part = slab_of(w[c0 * P:(c0 + n) * P], pairs(DC))
        out.append(np.pad(part, ((0, 0), (0, 0), (0, KC * 256 - part.shape[2]))))
    return np.concatenate(out)


def by_channel(a):
    a = a.reshape(-1, a.shape[-1] // P, P)
    return a.transpose(2, 0, 1).reshape(P, -1)


def column(a):
    return np.pad(a.reshape(-1, 1), ((0, P - a.size), (0, 0)))


_OUT = (1, T, D)


def kernel(**inputs):
    import concourse.bacc as bacc
    from concourse.bass_utils import run_bass_kernel_spmd

    i = {k: np.asarray(v) for k, v in inputs.items()}
    arrays = {"x": np.ascontiguousarray(i["x"][0].T.reshape(DC, P, T).transpose(1, 0, 2)), "consts": constants()}
    ev, od = i["ev_w_in"][0], i["od_w_in"][0]
    arrays["ev_cf"] = slab_of(ev, [pair(c, c, 3 * SC, 3 * SC + CF) for c in range(NC4)])
    arrays["ev_sc"] = slab_of(ev, [pair(c, c, SC, 2 * SC) for c in range(NC4)])
    arrays["ev_b"] = slab_of(ev, pairs(NC4))
    arrays["ev_out"] = slab_of(i["ev_w_out"][0], pairs(DC))
    arrays["od_lru"] = slab_of(od, [pair(c, c, 0, LRU) for c in range(NC4)])
    arrays["od_qk"] = slab_of(od, [pair(c, c, 2 * LRU, 2 * LRU + DIL_W) for c in range(DIL_W // P)])
    arrays["od_v"] = slab_of(od, pairs(DIL_W // P, 2 * LRU + 2 * DIL_W))
    arrays["od_out"] = slab_of(i["od_w_out"][0], pairs(DC))
    for f in range(2):
        both = np.concatenate([i["ffn_w_gate"][f], i["ffn_w_up"][f]], axis=1)
        arrays[f"up{f}"] = slab_of(both, [pair(c, c, 0, FF) for c in range(FC)])
        arrays[f"down{f}"] = down_slabs(i["ffn_w_down"][f], DOWN_GROUPS)
    at = np.cumsum((0,) + IN_SPLITS)
    stages = {name: [] for name, _ in SECOND}
    for l in range(2):
        w = i["w_in_2"][l]
        ki = np.arange(at[4], at[5])
        kidt = slab_of(np.concatenate([w, np.zeros((D, 256 - P - SH), np.float32)], axis=1),
                       [np.concatenate([ki, ki, np.arange(at[8], at[9]), np.arange(w.shape[1], w.shape[1] + 256 - P - SH)])])
        stages["kidt"].append(kidt)
        stages["wi"].append(slab_of(w, [np.arange(at[5], at[6])]))
        stages["qi"].append(slab_of(w, pairs(4, at[3])))
        stages["q"].append(slab_of(w, pairs(8, at[0])))
        stages["k"].append(slab_of(w, pairs(2, at[1])))
        stages["v"].append(slab_of(w, pairs(2, at[2])))
        stages["xbc"].append(slab_of(w, pairs(XBC_CH, at[7])))
        stages["z"].append(slab_of(w, pairs(XCH, at[6])))
        stages["gates"].append(slab_of(w, [pair(m, m, at[9], at[10]) for m in range(DC)]))
        stages["pa"].append(slab_of(i["w_proj_attn_2"][l], pairs(DC)))
        stages["ps"].append(down_slabs(i["w_proj_ssd_2"][l], ((0, 8), (8, 8))))
        stages["out"].append(slab_of(i["w_out_2"][l], pairs(DC)))
        stages["up"].append(slab_of(i["ffn_w_up_2"][l], [pair(c, c, 0, FF) for c in range(FC)]))
        stages["down"].append(down_slabs(i["ffn_w_down_2"][l], DOWN_GROUPS))
    for name, parts in stages.items():
        arrays[name] = np.concatenate(parts)

    first = [i["mix_norm_g"][0], i["ffn_norm_g"][0], i["mix_norm_g"][1], i["ffn_norm_g"][1], i["ev_sc_conv_w"][0],
             i["ev_cf_conv_w"][0], i["ev_cf_conv_b"][0], i["ev_cf_ln_g"][0], i["ev_cf_ln_b"][0], i["od_lru_conv_w"][0],
             i["od_lru_conv_b"][0], i["od_lru_ba"][0], i["od_lru_bx"][0], i["od_lru_lam"][0],
             np.tile(i["od_q_norm_g"][0], 2), np.tile(i["od_k_norm_g"][0], 2), i["ffn_conv_w"][0], i["ffn_conv_b"][0],
             i["ffn_conv_w"][1], i["ffn_conv_b"][1], i["norm_final_w_2"]]
    cols = [by_channel(a) for a in first]
    for l in range(2):
        cols += [by_channel(i[n][l]) for n in ("norm_mix_w_2", "norm_ffn_w_2", "ssd_conv_w_2", "ssd_conv_b_2", "ssd_norm_w_2")]
        cols.append(by_channel(np.repeat(i["ssd_d_2"][l], XI // SH)))
        cols += [column(i["ssd_dt_bias_2"][l]), column(i["ssd_a_log_2"][l])]
        cols += [by_channel(i["ffn_conv_w_2"][l]), by_channel(i["ffn_conv_b_2"][l])]
    arrays["params"] = np.ascontiguousarray(np.concatenate(cols, axis=1))
    assert arrays["params"].shape == (P, NPARAM)
    gate_w = np.zeros((P, 2 * NC4, P), np.float32)
    for n, w in enumerate((i["od_lru_wa"][0], i["od_lru_wx"][0])):
        for head in range(8):
            lo = 64 * (head % 2)
            gate_w[lo:lo + 64, NC4 * n + head // 2, lo:lo + 64] = w[head]
    arrays["gate_w"] = gate_w

    nc = bacc.Bacc("TRN2", target_bir_lowering=False, num_devices=1)
    arrays = {f"in_{k}": np.ascontiguousarray(a, dtype=np.float32) for k, a in arrays.items()}
    dram = {k[3:]: nc.dram_tensor(k, a.shape, F32, kind="ExternalInput").ap() for k, a in arrays.items()}
    dram["result"] = nc.dram_tensor("out_0", (P, DC, T), F32, kind="ExternalOutput").ap()
    build(nc, dram)
    got = run_bass_kernel_spmd(nc, [arrays], core_ids=[0]).results[0]["out_0"]
    return np.ascontiguousarray(got.transpose(1, 0, 2).reshape(D, T).T).reshape(_OUT)
```

```python
from contextlib import ExitStack

import numpy as np

import concourse.bass as bass
from concourse import mybir

F32 = mybir.dt.float32
F32R = mybir.dt.float32r
ALU = mybir.AluOpType
ACT = mybir.ActivationFunctionType
AX_X = mybir.AxisListType.X

P = 128
T = 256
D = 1024
DC = D // P
RING = 4
WSLOTS = 2
KC = 8
EPS = 1e-6
NEG = -1.0e30
TAKEN = -3.0e38

SC = CF = LRU = 512
NC4 = SC // P
SC_TAPS, CF_TAPS, LRU_TAPS, FFN_TAPS = 3, 31, 4, 3
DIL = ((128, 1), (512, 4), (2048, 16))
DIL_G, DIL_H, DIL_D = 3, 4, 64
DIL_W = DIL_G * DIL_H * DIL_D
FF = 2816
FC = FF // P
DOWN_GROUPS = ((0, 8), (8, 8), (16, 6))
HID = 14
UP_CHUNKS = range(HID), range(HID, FC)
UP_A, UP_B = HID, FC - HID

NH, HD, NKV = 8, 128, 2
QPK = NH // NKV
IH, ID = 8, 64
TOPK = min(256, T // 4)
XI = 2048
XCH = XI // P
SH, SG, SN = 32, 4, 128
XBC = XI + 2 * SG * SN
XBC_CH = XBC // P
SSD_TAPS = 4
ROPE_THETA, ROPE_FRACTION = 500000.0, 4
IN_SPLITS = (NH * HD, NKV * HD, NKV * HD, IH * ID, ID, IH, XI, XBC, SH, D, D)

FIRST = [("ev_cf", 4), ("ev_sc", 4), ("ev_b", 2), ("ev_out", 4),
         ("upA0", UP_A), ("dnA0", 4), ("upB0", UP_B), ("dnB0", 8),
         ("od_lru", 4), ("od_qk", 6), ("od_v", 3), ("od_out", 4),
         ("upA1", UP_A), ("dnA1", 4), ("upB1", UP_B), ("dnB1", 8)]
SECOND = [("kidt", 1), ("wi", 1), ("qi", 2), ("k", 1), ("q", 4), ("v", 1), ("xbc", 12), ("z", 8),
          ("gates", 8), ("pa", 4), ("ps", 8), ("out", 4),
          ("upA", UP_A), ("dnA", 4), ("upB", UP_B), ("dnB", 8)]


def starts(stages, at):
    where = {}
    for name, n in stages:
        where[name] = at
        at += n
    return where, at


AT, SECOND_AT = starts(FIRST, 0)
AT2, END2 = starts(SECOND, SECOND_AT)
PER_LAYER = END2 - SECOND_AT
SLABS = SECOND_AT + 2 * PER_LAYER
assert PER_LAYER % RING == 0
WIDTH = {"od_out": 6 * 256, "wi": KC * IH}
COUNT = dict(FIRST + SECOND)


def columns(parts):
    where, at = {}, 0
    for name, n in parts:
        where[name] = at
        at += n
    return where, at


PCOL, P_FIRST = columns([
    ("mix_g0", DC), ("ffn_g0", DC), ("mix_g1", DC), ("ffn_g1", DC), ("sc_w", SC_TAPS * NC4),
    ("cf_w", CF_TAPS * NC4), ("cf_b", NC4), ("ln_g", NC4), ("ln_b", NC4), ("lru_w", LRU_TAPS * NC4),
    ("lru_b", NC4), ("lru_ba", NC4), ("lru_bx", NC4), ("lam", NC4), ("q_g", 1), ("k_g", 1),
    ("fw0", FFN_TAPS * FC), ("fb0", FC), ("fw1", FFN_TAPS * FC), ("fb1", FC), ("final_g", DC)])
PCOL2, P_LAYER = columns([
    ("mix_g", DC), ("ffn_g", DC), ("ssd_w", SSD_TAPS * XBC_CH), ("ssd_b", XBC_CH), ("ssd_norm", XCH),
    ("ssd_d", XCH), ("dt_bias", 1), ("a_log", 1), ("fw", FFN_TAPS * 2 * FC), ("fb", 2 * FC)])
NPARAM = P_FIRST + 2 * P_LAYER

CCOL, NCONST = columns([
    ("ident", P), ("mean1024", P), ("mean512", P), ("mean64", P), ("swap_attn", P), ("swap_idx", P),
    ("cos_attn", T), ("sin_attn", T), ("cos_idx", T), ("sin_idx", T),
    ("causal0", P), ("causal1", T), ("tril", T + P)])
DIL_AT = (0, DIL_G * P)
NDIL = DIL_G * (P + T)


class Semaphores:
    pass


class Slab:

    def __init__(self, sems, first, turns):
        self.sems, self.first, self.turns = sems, first, turns
        self.bank, self.slot = first % RING, first % WSLOTS
        self.use = turns + first // RING
        self.number = turns * RING + first
        self.fixed = isinstance(turns, int)

    def ahead(self):
        if self.fixed and self.number + WSLOTS >= SLABS:
            return None
        return Slab(self.sems, self.first + WSLOTS, self.turns)

    def wait_raw_free(self, eng):
        if not self.fixed or self.number >= WSLOTS:
            eng.wait_ge(self.sems.w_lo_a, self.number - WSLOTS + 1)
            eng.wait_ge(self.sems.w_lo_b, self.number - WSLOTS + 1)

    def wait_landed(self, eng):
        eng.wait_ge(self.sems.w_landed[self.slot], (self.turns * (RING // WSLOTS) + self.first // WSLOTS + 1) * 16)

    def wait_hi(self, eng, half):
        eng.wait_ge(self.sems.w_hi, 2 * self.number + half + 1)

    def wait_split(self, eng):
        eng.wait_ge(self.sems.w_lo_a, self.number + 1)
        eng.wait_ge(self.sems.w_lo_b, self.number + 1)

    def wait_bank_free(self, eng):
        if not self.fixed or self.number >= RING:
            eng.wait_ge(self.sems.bank_free[self.bank], self.use)

    def wait_done(self, eng):
        eng.wait_ge(self.sems.lin_done, self.number + 1)

    def wait_released(self, eng):
        eng.wait_ge(self.sems.bank_free[self.bank], self.use + 1)


def each_slab(sems, eng, first, count, turns, body, peel=0):
    whole = count // RING if count >= 2 * RING else 0
    for n in range(peel * RING if whole else 0):
        body(Slab(sems, first + n, turns), n, n % RING)
    if whole:
        with eng.Fori(peel, whole) as i:
            for j in range(RING):
                body(Slab(sems, first + j, turns + i), i * RING + j, j)
    for n in range(whole * RING, count):
        body(Slab(sems, first + n, turns), n, n % RING)


class Chain:

    def __init__(self, eng, sem, base=0):
        self.eng, self.sem, self.base, self.n = eng, sem, base, 0

    def link(self, ins):
        self.n += 1
        ins.then_inc(self.sem, 1)
        self.eng.wait_ge(self.sem, self.base + self.n)





SOFTPLUS_LINKS = 14
LAM_LINKS = SOFTPLUS_LINKS + 2
DT_LINKS = SOFTPLUS_LINKS + 2
IX_LINKS = 2 * (IH + 1 + 2 * (TOPK // 8) + 2)


def build(nc, dram):
    ctx = ExitStack()
    with ctx:
        def sb(name, shape, dtype=F32):
            return ctx.enter_context(nc.sbuf_tensor(name, shape, dtype))

        def psum(name, shape):
            return ctx.enter_context(nc.psum_tensor(name, shape, F32))

        def sem(name):
            return ctx.enter_context(nc.semaphore(name))

        s = Semaphores()
        s.loaded = sem("loaded")
        s.pads = sem("pads")
        s.lin_done = sem("lin_done")
        s.norm_sq = sem("norm_sq")
        s.norm_sum = sem("norm_sum")
        s.norm_std = sem("norm_std")
        s.norm_rstd = sem("norm_rstd")
        s.h_f32 = sem("h_f32")
        s.h_hi = sem("h_hi")
        s.h_lo_p = sem("h_lo_p")
        s.h_lo_v = sem("h_lo_v")
        s.w_hi = sem("w_hi")
        s.w_lo_a = sem("w_lo_a")
        s.w_lo_b = sem("w_lo_b")
        s.ffn2_prod = sem("ffn2_prod")
        s.hid_hi = sem("hid_hi")
        s.hid_split = sem("hid_split")
        s.y_sc_hi = sem("y_sc_hi")
        s.y_sc_lo = sem("y_sc_lo")
        s.u_lo = sem("u_lo")
        s.lru_y_hi = sem("lru_y_hi")
        s.lru_y_lo = sem("lru_y_lo")
        s.att_hi = sem("att_hi")
        s.att_lo = sem("att_lo")
        s.a_hi = sem("a_hi")
        s.a_lo = sem("a_lo")
        s.bn_hi = sem("bn_hi")
        s.bn_lo = sem("bn_lo")
        s.merged_hi = sem("merged_hi")
        s.merged_lo = sem("merged_lo")
        s.cf_sig = sem("cf_sig")
        s.cf_tap = sem("cf_tap")
        s.ln_mean = sem("ln_mean")
        s.ln_diff = sem("ln_diff")
        s.ln_sq = sem("ln_sq")
        s.ln_var = sem("ln_var")
        s.ln_std = sem("ln_std")
        s.ln_rstd = sem("ln_rstd")
        s.ln_scaled = sem("ln_scaled")
        s.u_ready = sem("u_ready")
        s.sc_chain = sem("sc_chain")
        s.y_sc = sem("y_sc")
        s.ffn_t0 = sem("ffn_t0")
        s.ffn_tap = sem("ffn_tap")
        s.ffn_silu = sem("ffn_silu")
        s.ffn2_t0 = sem("ffn2_t0")
        s.ffn2_tap = sem("ffn2_tap")
        s.ffn2_silu = sem("ffn2_silu")
        s.lru_t0 = sem("lru_t0")
        s.lru_tap = sem("lru_tap")
        s.lru_r = sem("lru_r")
        s.lru_i = sem("lru_i")
        s.lru_gates = sem("lru_gates")
        s.lru_a = sem("lru_a")
        s.lru_m2 = sem("lru_m2")
        s.lru_mult = sem("lru_mult")
        s.lru_chain = sem("lru_chain")
        s.lru_y = sem("lru_y")
        s.lam_chain = sem("lam_chain")
        s.lam_e = sem("lam_e")
        s.qk_sq = sem("qk_sq")
        s.qk_sum = sem("qk_sum")
        s.qk_std = sem("qk_std")
        s.qk_chain = sem("qk_chain")
        s.at_logits = sem("at_logits")
        s.at_masked = sem("at_masked")
        s.at_max = sem("at_max")
        s.at_exp = sem("at_exp")
        s.at_chain = sem("at_chain")
        s.at_p = sem("at_p")
        s.at_tr = sem("at_tr")
        s.at_pt = sem("at_pt")
        s.at_pv = sem("at_pv")
        s.at_out = sem("at_out")
        s.rope_rot = sem("rope_rot")
        s.rope_chain = sem("rope_chain")
        s.rope_done = sem("rope_done")
        s.dt_abs = sem("dt_abs")
        s.dt_e = sem("dt_e")
        s.dt_chain = sem("dt_chain")
        s.dt_tr = sem("dt_tr")
        s.dt_tok = sem("dt_tok")
        s.xbc_t0 = sem("xbc_t0")
        s.xbc_tap = sem("xbc_tap")
        s.xbc_silu = sem("xbc_silu")
        s.ix_mm = sem("ix_mm")
        s.ix_rel = sem("ix_rel")
        s.ix_chain = sem("ix_chain")
        s.da_logits = sem("da_logits")
        s.da_max = sem("da_max")
        s.da_exp = sem("da_exp")
        s.da_chain = sem("da_chain")
        s.da_p = sem("da_p")
        s.da_tr = sem("da_tr")
        s.da_pt = sem("da_pt")
        s.da_pv = sem("da_pv")
        s.da_out = sem("da_out")
        s.xt_tr = sem("xt_tr")
        s.xt_copied = sem("xt_copied")
        s.a_exp = sem("a_exp")
        s.ssd_cb = sem("ssd_cb")
        s.ssd_cbm = sem("ssd_cbm")
        s.ssd_abc = sem("ssd_abc")
        s.ssd_seg = sem("ssd_seg")
        s.ssd_exp = sem("ssd_exp")
        s.ssd_m = sem("ssd_m")
        s.ssd_y = sem("ssd_y")
        s.ssd_chain = sem("ssd_chain")
        s.ssd_ydone = sem("ssd_ydone")
        s.bn_sq = sem("bn_sq")
        s.bn_sum = sem("bn_sum")
        s.bn_std = sem("bn_std")
        s.bn_chain = sem("bn_chain")
        s.ps_chain = sem("ps_chain")
        s.final = sem("final")
        s.out_written = sem("out_written")
        s.w_landed = [sem(f"w_landed{i}") for i in range(WSLOTS)]
        s.bank_free = [sem(f"bank_free{i}") for i in range(RING)]

        x = sb("x", [P, DC, T])
        h_hi = sb("h_hi", [P, DC, T], F32R)
        h_lo = sb("h_lo", [P, DC, T], F32R)
        sq = sb("sq", [P, DC, T])
        hid_hi = sb("hid_hi", [P, HID, T], F32R)
        hid_lo = sb("hid_lo", [P, HID, T], F32R)
        w_raw = [sb(f"w_raw{i}", [P, KC * 256]) for i in range(WSLOTS)]
        w_hi = [sb(f"w_hi{i}", [P, KC * 256], F32R) for i in range(WSLOTS)]
        w_lo = [sb(f"w_lo{i}", [P, KC * 256], F32R) for i in range(WSLOTS)]
        arena = sb("arena", [P, 74 * T])
        par = sb("par", [P, NPARAM, 1])
        cst = sb("cst", [P, NCONST])
        std = sb("std", [P, 2, 2 * T])
        eps = sb("eps", [P, 1])
        acc = sb("acc", [P, 2, 2, T])
        sil = std[:, :, 0:T]
        score = arena[:, 57 * T:65 * T].rearrange("p (b n) -> p b n", b=2)
        dt_tok_sb = sb("dt_tok_sb", [P, 4 * SH])
        small = sb("small", [P, 64])
        sqf = sq[:, :, :].rearrange("p c t -> p (c t)")

        lin = [psum(f"lin{i}", [P, 2, T]) for i in range(RING)]
        stat = psum("stat", [P, 2 * T])
        logit = psum("logit", [P, 4, T])
        tr = psum("tr", [P, 2 * T])

        def cut(at, chunks):
            return arena[:, at * T:(at + chunks) * T].rearrange("p (c t) -> p c t", t=T)

        prod = cut(34, 2)
        pt = sq[:, 0:4, :].rearrange("p (b c) t -> p b (c t)", b=2)

        u_pad = arena[:, 0:NC4 * (T + 30)].rearrange("p (c t) -> p c t", c=NC4)
        t_pad = arena[:, 5 * T:5 * T + NC4 * (T + 2)].rearrange("p (c t) -> p c t", c=NC4)
        cf_acc, sc_c, sc_x, sc_b, diff, sc_acc = (cut(10 + 4 * i, 4) for i in range(6))
        lru_xc, lru_gate, lru_r, lru_i, lru_a, lru_th, lru_m, lru_hs = (cut(4 * i, 4) for i in range(8))
        qn, kn = cut(32, 6), cut(38, 6)
        vt = arena[:, 44 * T:50 * T].rearrange("p (t n) -> p t n", t=2)
        qk_sq = cut(50, 4).rearrange("p (b c) t -> p b (c t)", b=2)
        pt1 = (sqf[:, 0:6 * P], arena[:, 54 * T:57 * T])
        gate_w = arena[:, 65 * T:69 * T].rearrange("p (c n) -> p c n", n=P)
        dil = arena[:, 69 * T:69 * T + NDIL]
        q2, k2, v2, qi2, ki2 = cut(0, 8), cut(8, 2), cut(10, 2), cut(12, 4), cut(16, 1)
        xbc = cut(17, XBC_CH)
        zs = cut(41, XCH)
        ix_rel = zs.rearrange("p (b c) t -> p b c t", b=4)
        xtok = [[arena[:, at * T:(at + 2) * T] for at in tile_at] for tile_at in ((12, 14, 8, 10), (57, 59, 61, 63))]
        gates = arena[:, 17 * T:33 * T].rearrange("p (m g t) -> p m g t", g=2, t=T)
        merged = cut(57, 8)
        ix_sc, ix_w = cut(65, 1), cut(66, 2)
        sel = cut(68, 2)
        dtb = cut(70, 3)
        m_buf = arena[:, 0:6 * T].rearrange("p (b c) -> p b c", b=4)
        cbm = arena[:, 6 * T:6 * T + T + P]
        rope_raw = sq[:, 0:4, :].rearrange("p (b c) t -> p b c t", b=2)
        rope_t = sq[:, 4:8, :].rearrange("p (b c) t -> p b c t", b=2)
        dscr = sq[:, 4:8, :]
        da_score = sq[:, 4:8, :]
        seg = sqf[:, 0:3 * T].rearrange("p (b c) -> p b c", b=2)
        seg_e = sqf[:, 3 * T:6 * T].rearrange("p (b c) -> p b c", b=2)
        y_raw = sq[:, 6:8, :]

        ident = cst[:, CCOL["ident"]:CCOL["ident"] + P]

        def const(name, n=P):
            return cst[:, CCOL[name]:CCOL[name] + n]

        def pcol(name, n=0):
            return par[:, PCOL[name] + n, :]

        def pcol2(l, name, n=0):
            return par[:, P_FIRST + PCOL2[name] + l * P_LAYER + n, :]

        def slab_at(stage, n, l=None):
            return Slab(s, AT[stage] + n, 0) if l is None else Slab(s, AT2[stage] + n, l * (PER_LAYER // RING))

        def slabs(eng, stage, body, l=None, peel=0):
            if l is None:
                each_slab(s, eng, AT[stage], COUNT[stage], 0, body, peel)
            else:
                each_slab(s, eng, AT2[stage], COUNT[stage], l * (PER_LAYER // RING), body, peel)

        def straight(stage, body, l=None):
            for n in range(COUNT[stage]):
                body(slab_at(stage, n, l), n, n % RING)

        XT_ORDER = ((1, 0), (0, 0), (1, 1), (0, 1), (1, 2), (1, 3), (0, 2), (0, 3))
        half_slab = KC * 256 // 2

        def split_lo(eng, slab, half):
            if slab is None:
                return
            slab.wait_hi(eng, half)
            part = slice(half * half_slab, (half + 1) * half_slab)
            eng.tensor_tensor(w_lo[slab.slot][:, part], w_raw[slab.slot][:, part], w_hi[slab.slot][:, part].bitcast(F32),
                              ALU.subtract).then_inc((s.w_lo_a, s.w_lo_b)[half], 1)

        def take_over(eng, stage, l=None):
            eng.wait_ge(s.w_lo_b, slab_at(stage, 0, l).ahead().number)

        def lo_part(eng, lo, whole, hi):
            return eng.tensor_tensor(lo, whole, hi.bitcast(F32), ALU.subtract)

        ffn_number = {"0": 0, "1": 1}

        def stage_ffn(f, l):
            return ("", FC * (2 + l)) if l is not None else (str(f), FC * ffn_number[str(f)])

        def stage_released(eng, stage, l=None):
            for n in range(max(0, COUNT[stage] - RING), COUNT[stage]):
                slab_at(stage, n, l).wait_released(eng)

        block = ctx.enter_context(nc.Block())

        @block.sync
        def _(sp):
            def stream(stage, l=None):
                width = WIDTH.get(stage, KC * 256)

                def body(slab, n, j):
                    slab.wait_raw_free(sp)
                    at = n if l is None else l * COUNT[stage] + n
                    sp.dma_start(w_raw[slab.slot][:, 0:width], dram[stage][at, :, :])\
                        .then_inc(s.w_landed[slab.slot], 16)
                slabs(sp, stage, body, l)

            for stage, _n in FIRST:
                stream(stage)
            for l in range(2):
                for stage, _n in SECOND:
                    stream(stage, l)
            for half in range(2):
                sp.wait_ge(s.final, half + 1)
                part = slice(half * DC // 2, (half + 1) * DC // 2)
                sp.dma_start(dram["result"][:, part, :], sq[:, part, :]).then_inc(s.out_written, 16)
            sp.wait_ge(s.out_written, 32)

        @block.gpsimd
        def _(pool):
            def norm(n):
                for c in range(DC // 2):
                    pool.wait_ge(s.h_hi, DC * n + c + 1)
                    lo_part(pool, h_lo[:, c, :], sq[:, c, :], h_hi[:, c, :]).then_inc(s.h_lo_p, 1)

            def weights(stage, l=None, both=False):
                def body(slab, n, j):
                    split_lo(pool, slab.ahead(), 0)
                    if both:
                        split_lo(pool, slab.ahead(), 1)
                if both:
                    take_over(pool, stage, l)
                if stage[:3] == "dnB":
                    straight(stage, body, l)
                else:
                    slabs(pool, stage, body, l)

            def ffn(f, l=None):
                sfx, base = stage_ffn(f, l)

                def up(off):
                    def body(slab, n, j):
                        split_lo(pool, slab.ahead(), 0)
                        if l is None:
                            slab.wait_released(pool)
                        else:
                            pool.wait_ge(s.ffn2_prod, l * FC + off + n + 1)
                        slot = n
                        pool.tensor_copy(hid_hi[:, slot, :], prod[:, j % 2, :]).then_inc(s.hid_hi, 1)
                        pool.wait_ge(s.hid_hi, base + off + n + 1)
                        lo_part(pool, hid_lo[:, slot, :], prod[:, j % 2, :], hid_hi[:, slot, :]).then_inc(s.hid_split, 1)
                    return body
                slabs(pool, "upA" + sfx, up(0), l)
                weights("dnA" + sfx, l)
                slabs(pool, "upB" + sfx, up(UP_A), l)
                weights("dnB" + sfx, l)

            nc.gpsimd.memset(eps[:, :], EPS)
            nc.gpsimd.memset(u_pad[:, :, 0:CF_TAPS - 1], 0.0)
            nc.gpsimd.memset(t_pad[:, :, 0:SC_TAPS - 1], 0.0).then_inc(s.pads, 1)
            for b in range(2):
                nc.gpsimd.memset(prod[:, b, :], 0.0).then_inc(s.hid_split, 1)
            for n in range(WSLOTS):
                split_lo(pool, Slab(s, n, 0), 0)
            norm(0)
            weights("ev_cf")
            weights("ev_sc", both=True)
            weights("ev_b", both=True)
            weights("ev_out")
            norm(1)
            ffn(0)
            norm(2)
            weights("od_lru")
            weights("od_qk")
            weights("od_v", both=True)
            weights("od_out")
            norm(3)
            ffn(1)
            for l in range(2):
                norm(4 + 2 * l)
                weights("kidt", l, both=True)
                weights("wi", l, both=True)
                for stage in ("qi", "k", "q", "v", "xbc"):
                    weights(stage, l)
                for u in range(4):
                    split_lo(pool, slab_at("z", 2 * u, l).ahead(), 0)
                    split_lo(pool, slab_at("z", 2 * u + 1, l).ahead(), 0)
                    t, kv = u // 2, u % 2
                    out = (slice(None), slice(kv * QPK, (kv + 1) * QPK), slice(t * P, t * P + P))
                    raw = acc[:, u % 2, :, :].rearrange("p c (a b) -> p (c a) b", b=P)
                    pool.wait_ge(s.da_out, 4 * l + u + 1)
                    pool.tensor_copy(hid_hi[out], raw).then_inc(s.a_hi, 1)
                    pool.wait_ge(s.a_hi, 4 * l + u + 1)
                    lo_part(pool, hid_lo[out], raw, hid_hi[out]).then_inc(s.a_lo, 1)
                weights("gates", l)
                for stage in ("pa", "ps", "out"):
                    weights(stage, l)
                norm(5 + 2 * l)
                ffn(None, l)

        @block.tensor
        def _(pe):
            def passes(out, lhs, rhs, first, last):
                nc.tensor.matmul(out, lhs[0], rhs[0], start=first, stop=False)
                nc.tensor.matmul(out, lhs[0], rhs[1], start=False, stop=False)
                return nc.tensor.matmul(out, lhs[1], rhs[0], start=False, stop=last)

            def operand(pair, chunks=range(KC)):
                return [(pair[0][:, c, :], pair[1][:, c, :]) for c in chunks]

            h_op = operand((h_hi, h_lo))
            hid = (hid_hi, hid_lo)

            def slab_products(slab, rhs, wait_chunk=None):
                slab.wait_split(pe)
                slab.wait_bank_free(pe)
                for half in range(2):
                    for k, chunk in enumerate(rhs):
                        if wait_chunk is not None and half == 0:
                            wait_chunk(k)
                        cols = slice(k * 256 + half * P, k * 256 + half * P + P)
                        mm = passes(lin[slab.bank][:, half, :], (w_hi[slab.slot][:, cols], w_lo[slab.slot][:, cols]),
                                    chunk, k == 0, k == len(rhs) - 1)
                mm.then_inc(s.lin_done, 1)

            def slab_tokens(slab, width=256):
                slab.wait_split(pe)
                slab.wait_bank_free(pe)
                for t in range(2):
                    for k in range(KC):
                        tokens = tuple(part[:, k, t * P:t * P + P] for part in (h_hi, h_lo))
                        cols = slice(k * width, (k + 1) * width)
                        mm = passes(lin[slab.bank][:, t, 0:width], tokens, (w_hi[slab.slot][:, cols], w_lo[slab.slot][:, cols]),
                                    k == 0, k == KC - 1)
                mm.then_inc(s.lin_done, 1)

            def products(stage, rhs, l=None, wait_chunk=None):
                slabs(pe, stage, lambda slab, n, j: slab_products(slab, rhs, wait_chunk if isinstance(n, int) and n == 0 else None), l,
                      1 if wait_chunk is not None else 0)

            def mean_pair(n, j):
                pe.wait_ge(s.norm_sq, 4 * n + j + 1)
                for k in (2 * j, 2 * j + 1):
                    mm = nc.tensor.matmul(stat[:, 0:T], const("mean1024"), sq[:, k, :],
                                          start=(k == 0), stop=(k == DC - 1))
                if j == 3:
                    mm.then_inc(s.norm_sum, 1)

            def closing(slab_list, rhs, n, wait_chunk=None):
                for j, slab in enumerate(slab_list):
                    slab_products(slab, rhs, wait_chunk if j == 0 else None)
                    if j >= 1:
                        mean_pair(n, j - 1)
                mean_pair(n, 3)

            def normed(n):
                def wait_chunk(k):
                    pe.wait_ge(s.h_hi, DC * n + k + 1)
                    half = DC // 2
                    if k < half:
                        pe.wait_ge(s.h_lo_p, half * n + k + 1)
                    else:
                        pe.wait_ge(s.h_lo_v, half * n + k - half + 1)
                return wait_chunk

            def ffn(f, n, l=None):
                sfx, base = stage_ffn(f, l)
                ups = 2 + base
                products("upA" + sfx, h_op, l, normed(n))

                def group(g, stage, at):
                    c0, chunks = DOWN_GROUPS[g]
                    rhs = operand(hid, [c % HID for c in range(c0, c0 + chunks)])
                    return [slab_at(stage + sfx, at + j, l) for j in range(4)], rhs, \
                        lambda k: pe.wait_ge(s.hid_split, ups + c0 + k + 1)

                slab_list, rhs, wait_chunk = group(0, "dnA", 0)
                for j, slab in enumerate(slab_list):
                    slab_products(slab, rhs, wait_chunk if j == 0 else None)
                products("upB" + sfx, h_op, l)
                slab_list, rhs, wait_chunk = group(1, "dnB", 0)
                for j, slab in enumerate(slab_list):
                    slab_products(slab, rhs, wait_chunk if j == 0 else None)
                slab_list, rhs, wait_chunk = group(2, "dnB", 4)
                closing(slab_list, rhs, n + 1, wait_chunk)

            pe.wait_ge(s.loaded, 80)
            for j in range(4):
                mean_pair(0, j)
            products("ev_cf", h_op, wait_chunk=normed(0))
            products("ev_sc", h_op)
            products("ev_b", h_op)
            pe.wait_ge(s.cf_tap, CF_TAPS * NC4)
            for k in range(NC4):
                mm = nc.tensor.matmul(stat[:, 0:T], const("mean512"), cf_acc[:, k, :],
                                      start=(k == 0), stop=(k == NC4 - 1))
            mm.then_inc(s.ln_mean, 1)
            pe.wait_ge(s.ln_sq, 1)
            for k in range(NC4):
                mm = nc.tensor.matmul(stat[:, T:2 * T], const("mean512"), sq[:, k, :],
                                      start=(k == 0), stop=(k == NC4 - 1))
            mm.then_inc(s.ln_var, 1)
            pe.wait_ge(s.y_sc_lo, 1)
            pe.wait_ge(s.u_lo, 1)
            closing([slab_at("ev_out", j) for j in range(4)], operand(hid), 1)
            ffn(0, 1)

            products("od_lru", h_op, wait_chunk=normed(2))

            def qk_mean(n):
                pe.wait_ge(s.qk_sq, n + 1)
                if n >= 1:
                    pe.wait_ge(s.qk_std, n)
                nc.tensor.matmul(stat[:, :], const("mean64"), qk_sq[:, n % 2, :],
                                 start=True, stop=True).then_inc(s.qk_sum, 1)

            def qk_slab(slab, n, j):
                slab_products(slab, h_op)
                if n >= 1:
                    qk_mean(n - 1)
            slabs(pe, "od_qk", qk_slab)
            qk_mean(COUNT["od_qk"] - 1)
            slabs(pe, "od_v", lambda slab, n, j: slab_tokens(slab))
            stage_released(pe, "od_lru")
            pe.wait_ge(s.qk_std, COUNT["od_qk"])
            for c in range(NC4):
                mm = nc.tensor.matmul(logit[:, c, :], gate_w[:, c, :], lru_xc[:, c, :], start=True, stop=True)
            mm.then_inc(s.lru_gates, 1)
            for c in range(NC4):
                out = (stat, tr)[c // 2][:, (c % 2) * T:(c % 2 + 1) * T]
                mm = nc.tensor.matmul(out, gate_w[:, NC4 + c, :], lru_xc[:, c, :], start=True, stop=True)
            mm.then_inc(s.lru_gates, 1)
            stage_released(pe, "od_qk")
            pe.wait_ge(s.lru_r, 1)
            pe.wait_ge(s.lru_i, 1)
            stage_released(pe, "od_v")

            def at_logits(u):
                head, t = u // 2, u % 2
                lo = 64 * (head % 2)
                if u >= 1:
                    pe.wait_ge(s.at_masked, u)
                for g in range(DIL_G):
                    c = (g * DIL_H + head) // 2
                    mm = nc.tensor.matmul(logit[:, g, 0:(t + 1) * P], qn[lo:lo + 64, c, t * P:t * P + P],
                                          kn[lo:lo + 64, c, 0:(t + 1) * P], start=True, stop=True)
                mm.then_inc(s.at_logits, 1)

            at_logits(0)
            for u in range(2 * DIL_H):
                head, t = u // 2, u % 2
                lo = 64 * (head % 2)
                if u + 1 < 2 * DIL_H:
                    at_logits(u + 1)
                nb = DIL_G * (t + 1)
                pe.wait_ge(s.at_p, u + 1)
                if u >= 1:
                    pe.wait_ge(s.at_out, u)
                for b in range(nb):
                    where = tr[:, b * P:b * P + P] if b < 4 else stat[:, T + (b - 4) * P:T + (b - 3) * P]
                    g, st = b // (t + 1), b % (t + 1)
                    at = g * (t + 1) * P + st * P
                    mm = nc.tensor.transpose(where, score[:, u % 2, at:at + P], ident)
                mm.then_inc(s.at_tr, 1)
                pe.wait_ge(s.at_pt, u + 1)
                for b in range(nb):
                    g, st = b // (t + 1), b % (t + 1)
                    v_at = (g * DIL_H + head) * DIL_D
                    mm = nc.tensor.matmul(stat[lo:lo + 64, 0:P], vt[:, st, v_at:v_at + DIL_D],
                                          pt1[u % 2][:, b * P:b * P + P], start=(b == 0), stop=(b == nb - 1))
                mm.then_inc(s.at_pv, 1)
            pe.wait_ge(s.lru_y_lo, 1)
            pe.wait_ge(s.att_lo, 1)
            closing([slab_at("od_out", j) for j in range(4)], operand(hid, range(6)), 3)
            ffn(1, 3)

            def layer(l):
                rope_unit = [0]

                def swap(which, n, stage, at=0):
                    r = rope_unit[0]
                    rope_unit[0] += 1
                    Slab(s, AT2[stage] + at, l * (PER_LAYER // RING)).wait_released(pe)
                    if r >= 1:
                        pe.wait_ge(s.rope_done, 8 * l + r)
                    nc.tensor.matmul(stat[:, 0:n], const(which),
                                     rope_raw[:, r % 2, :, :].rearrange("p c t -> p (c t)")[:, 0:n],
                                     start=True, stop=True).then_inc(s.rope_rot, 1)

                products("kidt", h_op, l, normed(4 + 2 * l))
                slabs(pe, "wi", lambda slab, n, j: slab_tokens(slab, IH), l)
                swap("swap_idx", T, "kidt")

                def index_products(b):
                    t, half = b // 2, b % 2
                    if b >= 1:
                        pe.wait_ge(s.ix_rel, 4 * l + b)
                    for i in range(4):
                        head = 4 * half + i
                        lo = 64 * (head % 2)
                        mm = nc.tensor.matmul(logit[:, 2 * (i % 2) + i // 2, 0:(t + 1) * P],
                                              qi2[lo:lo + 64, head // 2, t * P:t * P + P],
                                              ki2[lo:lo + 64, 0, 0:(t + 1) * P], start=True, stop=True)
                    mm.then_inc(s.ix_mm, 1)

                slab_products(slab_at("qi", 0, l), h_op)
                slab_products(slab_at("qi", 1, l), h_op)
                swap("swap_idx", 2 * T, "qi", 0)
                slab_products(slab_at("k", 0, l), h_op)
                swap("swap_idx", 2 * T, "qi", 1)
                for n in range(4):
                    slab_products(slab_at("q", n, l), h_op)
                    if n == 0:
                        swap("swap_attn", 2 * T, "k")
                    else:
                        swap("swap_attn", 2 * T, "q", n - 1)
                    index_products(n)
                slab_tokens(slab_at("v", 0, l))
                swap("swap_attn", 2 * T, "q", 3)
                pe.wait_ge(s.dt_chain, DT_LINKS * (l + 1))
                for i, row in enumerate((0, 2)):
                    for t in range(2):
                        mm = nc.tensor.transpose(tr[:, (2 * i + t) * SH:(2 * i + t + 1) * SH],
                                                 dtb[0:SH, row, t * P:t * P + P], ident[0:SH, 0:SH])
                mm.then_inc(s.dt_tr, 1)
                products("xbc", h_op, l)

                def da_logits(u):
                    t, kv = u // 2, u % 2
                    n = (t + 1) * P
                    for i in range(QPK):
                        mm = nc.tensor.matmul(logit[:, i, 0:n], q2[:, kv * QPK + i, t * P:t * P + P],
                                              k2[:, kv, 0:n], start=True, stop=True)
                    mm.then_inc(s.da_logits, 1)

                def by_token(b):
                    t, quarter = XT_ORDER[b]
                    if b == 0:
                        pe.wait_ge(s.xbc_silu, 12 * (l + 1))
                    else:
                        pe.wait_ge(s.xt_copied, 8 * l + b)
                    for i in range(4):
                        mm = nc.tensor.transpose(stat[:, i * P:i * P + P], xbc[:, 4 * quarter + i, t * P:t * P + P], ident)
                    mm.then_inc(s.xt_tr, 1)

                pe.wait_ge(s.rope_done, 8 * l + 8)
                pe.wait_ge(s.ix_rel, 4 * l + 4)
                da_logits(0)
                for u in range(4):
                    t, kv = u // 2, u % 2
                    slab_products(slab_at("z", 2 * u, l), h_op)
                    if u >= 1:
                        by_token(2 * u - 1)
                    pe.wait_ge(s.da_p, 4 * l + u + 1)
                    if u == 0:
                        pe.wait_ge(s.dt_tok, l + 1)
                    else:
                        pe.wait_ge(s.da_out, 4 * l + u)
                    if t == 1:
                        pe.wait_ge(s.xt_copied, 8 * l + 2 * u)
                    for st in range(t + 1):
                        for i in range(QPK):
                            mm = nc.tensor.transpose((tr, stat)[st][:, i * P:i * P + P],
                                                     da_score[:, i, st * P:st * P + P], ident)
                    mm.then_inc(s.da_tr, 1)
                    slab_products(slab_at("z", 2 * u + 1, l), h_op)
                    pe.wait_ge(s.da_pt, 6 * l + (1, 2, 4, 6)[u])
                    for st in range(t + 1):
                        mm = nc.tensor.matmul(tr[:, :], v2[:, st, kv * P:kv * P + P], pt[:, st, 0:4 * P],
                                              start=(st == 0), stop=(st == t))
                    mm.then_inc(s.da_pv, 1)
                    if u < 3:
                        da_logits(u + 1)
                    by_token(2 * u)

                def running_sums(c):
                    if c >= 2:
                        pe.wait_ge(s.ssd_seg, SH * l + 2 * c - 2)
                    for i in range(2):
                        mm = nc.tensor.matmul(logit[:, 2 * (c % 2) + i, :],
                                              ident[0:SH, 2 * c + i:2 * c + i + 1].to_broadcast([SH, P]),
                                              dtb[0:SH, 2, :], start=True, stop=True)
                    mm.then_inc(s.ssd_abc, 1)

                running_sums(0)
                by_token(7)
                pe.wait_ge(s.da_out, 4 * l + 4)
                for c in range(XCH):
                    where = (tr, stat)[c % 2]

                    def bank_read():
                        if c >= 2:
                            pe.wait_ge(s.ssd_ydone, XCH * l + c - 1)
                    if c % 4 == 0:
                        g = c // 4
                        bank_read()
                        nc.tensor.matmul(where[:, 0:T], xbc[:, XCH + g, 0:P], xbc[:, XCH + SG + g, :],
                                         start=True, stop=True)
                        nc.tensor.matmul(where[:, T:T + P], xbc[:, XCH + g, P:T], xbc[:, XCH + SG + g, P:T],
                                         start=True, stop=True).then_inc(s.ssd_cb, 1)
                    if c + 1 < XCH:
                        running_sums(c + 1)
                    if c % 2 == 0:
                        slab_products(slab_at("gates", c // 2, l), h_op)
                    if c == 0:
                        pe.wait_ge(s.xt_copied, 8 * l + 8)
                    bank_read()
                    for head in (2 * c, 2 * c + 1):
                        lo = 64 * (head % 2)
                        pe.wait_ge(s.ssd_m, SH * l + head + 1)
                        by_tok = [xtok[t][head // 8][:, head % 8 * 64:head % 8 * 64 + 64] for t in range(2)]
                        nc.tensor.matmul(where[lo:lo + 64, 0:T], by_tok[0], m_buf[:, head % 4, 0:T], start=True, stop=False)
                        mm = nc.tensor.matmul(where[lo:lo + 64, P:T], by_tok[1], m_buf[:, head % 4, T:T + P],
                                              start=False, stop=True)
                    mm.then_inc(s.ssd_y, 1)
                pe.wait_ge(s.a_lo, 4 * (l + 1))
                pe.wait_ge(s.ssd_ydone, XCH * (l + 1))
                for g in range(SG):
                    slab_products(slab_at("pa", g, l), operand(hid))
                    pe.wait_ge(s.bn_sq, SG * l + g + 1)
                    for k in range(4):
                        mm = nc.tensor.matmul((tr, stat)[g % 2][:, 0:T], const("mean512"),
                                              sq[:, 4 * (g % 2) + k, :], start=(k == 0), stop=(k == 3))
                    mm.then_inc(s.bn_sum, 1)
                for n in range(8):
                    slab_products(slab_at("ps", n, l), (h_op, operand(hid))[n // 4],
                                  (lambda k: pe.wait_ge(s.bn_lo, SG * l + 2 * (n // 4) + k // 4 + 1)) if n % 4 == 0 else None)
                closing([slab_at("out", j, l) for j in range(4)], h_op, 5 + 2 * l,
                        lambda k: pe.wait_ge(s.merged_lo, 4 * l + k // 2 + 1))
                ffn(None, 5 + 2 * l, l)

            for l in range(2):
                layer(l)

        @block.scalar
        def _(act):
            def weights_hi(slab):
                if slab is None:
                    return
                slab.wait_landed(act)
                for half in range(2):
                    part = slice(half * half_slab, (half + 1) * half_slab)
                    nc.scalar.activation(w_hi[slab.slot][:, part], w_raw[slab.slot][:, part], ACT.Copy).then_inc(s.w_hi, 1)

            def done(slab):
                slab.wait_done(act)
                weights_hi(slab.ahead())

            def square(j):
                nc.scalar.activation(sq[:, 2 * j:2 * j + 2, :], x[:, 2 * j:2 * j + 2, :], ACT.Square).then_inc(s.norm_sq, 1)

            def norm(n):
                nc.scalar.activation(small[:, 63:64], eps[:, :], ACT.Sqrt)
                act.wait_ge(s.norm_sum, n + 1)
                nc.scalar.activation(std[:, 0, 0:T], stat[:, 0:T], ACT.Sqrt, bias=eps[:, :]).then_inc(s.norm_std, 1)
                if n == 8:
                    return
                for c in range(DC):
                    act.wait_ge(s.h_f32, DC * n + c + 1)
                    nc.scalar.activation(h_hi[:, c, :], sq[:, c, :], ACT.Copy).then_inc(s.h_hi, 1)

            def residual(stage, l=None):
                def body(slab, n, j):
                    last = n >= COUNT[stage] - 4 and stage[:3] != "dnA"
                    if n < COUNT[stage] - 2:
                        done(slab)
                    if last:
                        slab.wait_released(act)
                        square(j)
                    if n >= COUNT[stage] - 2:
                        done(slab)
                straight(stage, body, l)

            def ffn(f, l=None):
                sfx, base = stage_ffn(f, l)

                def up(off):
                    def body(slab, n, j):
                        b = j % 2
                        bank = lin[slab.bank]
                        done(slab)
                        c = off + n
                        if l is None:
                            nc.scalar.activation(acc[:, b, 0, :], bank[:, 0, :], ACT.Identity,
                                                 bias=pcol(f"fb{f}", c), scale=pcol(f"fw{f}", 2 * FC + c)).then_inc(s.ffn_t0, 1)
                            act.wait_ge(s.ffn_tap, 2 * (base + c) + 2)
                            nc.scalar.activation(sil[:, b, :], acc[:, b, 0, :], ACT.Silu).then_inc(s.ffn_silu, 1)
                        else:
                            for i in range(2):
                                ins = nc.scalar.activation(acc[:, b, i, :], bank[:, i, :], ACT.Identity,
                                                           bias=pcol2(l, "fb", i * FC + c),
                                                           scale=pcol2(l, "fw", 2 * 2 * FC + i * FC + c))
                            ins.then_inc(s.ffn2_t0, 1)
                            act.wait_ge(s.ffn2_tap, 3 * (l * FC + c) + 3)
                            nc.scalar.activation(sil[:, b, :], acc[:, b, 0, :], ACT.Silu).then_inc(s.ffn2_silu, 1)
                    return body
                slabs(act, "upA" + sfx, up(0), l)
                residual("dnA" + sfx, l)
                slabs(act, "upB" + sfx, up(UP_A), l)
                residual("dnB" + sfx, l)

            act.dma_start(x[:, :, :], dram["x"]).then_inc(s.loaded, 16)
            act.dma_start(cst[:, :], dram["consts"]).then_inc(s.loaded, 16)
            act.dma_start(par[:, :, :], dram["params"].rearrange("p (n a) -> p n a", a=1)).then_inc(s.loaded, 16)
            act.dma_start(gate_w[:, :, :], dram["gate_w"]).then_inc(s.loaded, 16)
            act.dma_start(dil, dram["dil"]).then_inc(s.loaded, 16)
            act.wait_ge(s.loaded, 80)
            act.wait_ge(s.pads, 1)

            for j in range(4):
                square(j)
            for n in range(WSLOTS):
                weights_hi(Slab(s, n, 0))
            norm(0)

            def cf_gate(slab, n, j):
                done(slab)
                nc.scalar.activation(sq[:, n, :], lin[slab.bank][:, 1, :], ACT.Sigmoid).then_inc(s.cf_sig, 1)
            slabs(act, "ev_cf", cf_gate)

            def sc_copy(slab, n, j):
                done(slab)
                nc.scalar.activation(sc_c[:, n, :], lin[slab.bank][:, 0, :], ACT.Copy)
                nc.scalar.activation(sc_x[:, n, :], lin[slab.bank][:, 1, :], ACT.Copy).then_inc(s.bank_free[slab.bank], 1)
            slabs(act, "ev_sc", sc_copy)

            def b_copy(slab, n, j):
                done(slab)
                nc.scalar.activation(sc_b[:, 2 * n:2 * n + 2, :], lin[slab.bank][:, :, :], ACT.Copy)\
                    .then_inc(s.bank_free[slab.bank], 1)
            slabs(act, "ev_b", b_copy)
            act.wait_ge(s.ln_diff, 1)
            nc.scalar.activation(sq[:, 0:NC4, :], diff[:, :, :], ACT.Square).then_inc(s.ln_sq, 1)
            act.wait_ge(s.ln_var, 1)
            nc.scalar.activation(std[:, 0, 0:T], stat[:, T:2 * T], ACT.Sqrt, bias=eps[:, :]).then_inc(s.ln_std, 1)
            act.wait_ge(s.y_sc, 1)
            nc.scalar.activation(hid_hi[:, 0:NC4, :], sc_acc[:, :, :], ACT.Copy).then_inc(s.y_sc_hi, 1)
            act.wait_ge(s.ln_scaled, 1)
            for c in range(NC4):
                for out in (sq[:, c, :], hid_hi[:, NC4 + c, :]):
                    ins = nc.scalar.activation(out, diff[:, c, :], ACT.Silu, bias=pcol("ln_b", c), scale=pcol("ln_g", c))
            ins.then_inc(s.u_ready, 1)
            residual("ev_out")
            norm(1)
            ffn(0)

            norm(2)
            act.wait_ge(s.lam_chain, 1)
            nc.scalar.activation(small[:, 8:12], small[:, 4:8], ACT.Exp, scale=-1.0).then_inc(s.lam_e, 1)

            def lru_in(slab, n, j):
                done(slab)
                nc.scalar.activation(lru_gate[:, n, :], lin[slab.bank][:, 1, :], ACT.Gelu_apprx_tanh)
                nc.scalar.activation(lru_xc[:, n, :], lin[slab.bank][:, 0, :], ACT.Identity,
                                     bias=pcol("lru_b", n), scale=pcol("lru_w", 3 * NC4 + n)).then_inc(s.lru_t0, 1)
            slabs(act, "od_lru", lru_in)

            def qk_square(slab, n, j):
                done(slab)
                if n >= 2:
                    act.wait_ge(s.qk_sum, n - 1)
                nc.scalar.activation(qk_sq[:, n % 2, :], lin[slab.bank][:, :, :].rearrange("p c t -> p (c t)"),
                                     ACT.Square).then_inc(s.qk_sq, 1)
                if n >= 1:
                    qk_root(n - 1)

            def qk_root(n):
                act.wait_ge(s.qk_sum, n + 1)
                if n >= 2:
                    slab_at("od_qk", n - 2).wait_released(act)
                nc.scalar.activation(std[:, n % 2, :], stat[:, :], ACT.Sqrt, bias=eps[:, :]).then_inc(s.qk_std, 1)
            slabs(act, "od_qk", qk_square)
            qk_root(COUNT["od_qk"] - 1)

            def v_copy(slab, n, j):
                done(slab)
                nc.scalar.activation(vt[:, :, n * 256:(n + 1) * 256], lin[slab.bank][:, :, :], ACT.Copy)\
                    .then_inc(s.bank_free[slab.bank], 1)
            slabs(act, "od_v", v_copy)
            act.wait_ge(s.lru_gates, 1)
            for c in range(NC4):
                ins = nc.scalar.activation(lru_r[:, c, :], logit[:, c, :], ACT.Sigmoid, bias=pcol("lru_ba", c))
            ins.then_inc(s.lru_r, 1)
            act.wait_ge(s.lru_gates, 2)
            for c in range(NC4):
                ins = nc.scalar.activation(lru_i[:, c, :], (stat, tr)[c // 2][:, (c % 2) * T:(c % 2 + 1) * T],
                                           ACT.Sigmoid, bias=pcol("lru_bx", c))
            ins.then_inc(s.lru_i, 1)
            act.wait_ge(s.lru_r, 1)
            act.wait_ge(s.lam_chain, LAM_LINKS)
            for c in range(NC4):
                nc.scalar.activation(lru_th[:, c, :], lru_r[:, c, :], ACT.Tanh, scale=small[:, c:c + 1])
                ins = nc.scalar.activation(lru_a[:, c, :], lru_r[:, c, :], ACT.Exp, scale=small[:, c:c + 1])
            ins.then_inc(s.lru_a, 1)
            act.wait_ge(s.lru_m2, 1)
            nc.scalar.activation(lru_th[:, :, :], lru_m[:, :, :], ACT.Sqrt).then_inc(s.lru_mult, 1)

            act.wait_ge(s.lru_y, 1)
            nc.scalar.activation(hid_hi[:, 0:NC4, :], lru_hs[:, :, :], ACT.Copy).then_inc(s.lru_y_hi, 1)

            for u in range(2 * DIL_H):
                head, t = u // 2, u % 2
                lo = 64 * (head % 2)
                n = DIL_G * (t + 1) * P
                act.wait_ge(s.at_max, u + 1)
                nc.scalar.activation(score[:, u % 2, 0:n], score[:, u % 2, 0:n], ACT.Exp,
                                     bias=small[:, 16 + u:17 + u], accum_out=small[:, 24 + u:25 + u]).then_inc(s.at_exp, 1)
                act.wait_ge(s.at_tr, u + 1)
                first = min(n, 4 * P)
                ins = nc.scalar.activation(pt1[u % 2][:, 0:first], tr[:, 0:first], ACT.Copy)
                if n > first:
                    ins = nc.scalar.activation(pt1[u % 2][:, first:n], stat[:, T:T + n - first], ACT.Copy)
                ins.then_inc(s.at_pt, 1)
                act.wait_ge(s.at_pv, u + 1)
                nc.scalar.activation(acc[lo:lo + 64, 0, head // 2, t * P:t * P + P], stat[lo:lo + 64, 0:P],
                                     ACT.Copy).then_inc(s.at_out, 1)
            act.wait_ge(s.at_out, 2 * DIL_H)
            nc.scalar.activation(hid_hi[:, NC4:NC4 + 2, :], acc[:, 0, :, :], ACT.Copy).then_inc(s.att_hi, 1)
            residual("od_out")
            norm(3)
            ffn(1)

            def layer(l):
                norm(4 + 2 * l)
                rope_unit = [0]

                def raw_copy(slab, chunks):
                    r = rope_unit[0]
                    rope_unit[0] += 1
                    if r >= 2:
                        act.wait_ge(s.rope_done, 8 * l + r - 1)
                    return nc.scalar.activation(rope_raw[:, r % 2, 0:chunks, :], lin[slab.bank][:, 0:chunks, :], ACT.Copy)

                def kidt(slab, n, j):
                    done(slab)
                    raw_copy(slab, 1)
                    nc.scalar.activation(dscr[0:SH, 2, :], lin[slab.bank][0:SH, 1, :], ACT.Identity,
                                         bias=pcol2(l, "dt_bias")[0:SH, :]).then_inc(s.bank_free[slab.bank], 1)
                    nc.scalar.activation(small[0:SH, 40:41], pcol2(l, "a_log")[0:SH, :], ACT.Exp).then_inc(s.a_exp, 1)
                slabs(act, "kidt", kidt, l)

                def wi_copy(slab, n, j):
                    done(slab)
                    nc.scalar.activation(small[:, 42:58].rearrange("p (t h) -> p t h", t=2),
                                         lin[slab.bank][:, :, 0:IH], ACT.Copy).then_inc(s.bank_free[slab.bank], 1)
                slabs(act, "wi", wi_copy, l)
                act.wait_ge(s.dt_abs, l + 1)
                nc.scalar.activation(dscr[0:SH, 3, :], dscr[0:SH, 3, :], ACT.Exp, scale=-1.0).then_inc(s.dt_e, 1)

                def rope_copy(slab):
                    done(slab)
                    raw_copy(slab, 2).then_inc(s.bank_free[slab.bank], 1)

                def rectified(b):
                    n = (b // 2 + 1) * P
                    act.wait_ge(s.ix_mm, 4 * l + b + 1)
                    nc.scalar.activation(ix_rel[:, b, :, 0:n], logit[:, :, 0:n], ACT.Relu).then_inc(s.ix_rel, 1)

                rope_copy(slab_at("qi", 0, l))
                rope_copy(slab_at("qi", 1, l))
                rope_copy(slab_at("k", 0, l))
                for n in range(4):
                    rope_copy(slab_at("q", n, l))
                    rectified(n)
                slab = slab_at("v", 0, l)
                done(slab)
                nc.scalar.activation(v2[:, :, :], lin[slab.bank][:, :, :], ACT.Copy).then_inc(s.bank_free[slab.bank], 1)
                act.wait_ge(s.dt_tr, l + 1)
                nc.scalar.activation(dt_tok_sb[:, :], tr[:, 0:4 * SH], ACT.Copy).then_inc(s.dt_tok, 1)

                def xbc_silu(n):
                    slab_at("xbc", n, l).wait_released(act)
                    nc.scalar.activation(xbc[:, 2 * n:2 * n + 2, :], acc[:, n % 2, :, :], ACT.Silu).then_inc(s.xbc_silu, 1)

                def xbc_conv(slab, n, j):
                    done(slab)
                    if n >= 2:
                        act.wait_ge(s.xbc_silu, 12 * l + n - 1)
                    for i in range(2):
                        ins = nc.scalar.activation(acc[:, j % 2, i, :], lin[slab.bank][:, i, :], ACT.Identity,
                                                   bias=pcol2(l, "ssd_b", 2 * n + i),
                                                   scale=pcol2(l, "ssd_w", 3 * XBC_CH + 2 * n + i))
                    ins.then_inc(s.xbc_t0, 1)
                    if n >= 1:
                        xbc_silu(n - 1)
                straight("xbc", xbc_conv, l)
                xbc_silu(COUNT["xbc"] - 1)

                def z_silu(n):
                    slab = slab_at("z", n, l)
                    done(slab)
                    nc.scalar.activation(zs[:, 2 * n:2 * n + 2, :], lin[slab.bank][:, :, :], ACT.Silu)\
                        .then_inc(s.bank_free[slab.bank], 1)

                def by_token(b):
                    t, quarter = XT_ORDER[b]
                    act.wait_ge(s.xt_tr, 8 * l + b + 1)
                    nc.scalar.activation(xtok[t][quarter], stat[:, :], ACT.Copy).then_inc(s.xt_copied, 1)

                for u in range(4):
                    t, kv = u // 2, u % 2
                    n = (t + 1) * P
                    act.wait_ge(s.da_max, 4 * l + u + 1)
                    for i in range(QPK):
                        ins = nc.scalar.activation(da_score[:, i, 0:n], da_score[:, i, 0:n],
                                                   ACT.Exp, bias=small[:, 16 + i:17 + i], accum_out=small[:, 24 + i:25 + i])
                    ins.then_inc(s.da_exp, 1)
                    z_silu(2 * u)
                    if u >= 1:
                        by_token(2 * u - 1)
                    act.wait_ge(s.da_tr, 4 * l + u + 1)
                    for st in range(t + 1):
                        nc.scalar.activation(pt[:, st, 0:4 * P], (tr, stat)[st][:, :], ACT.Copy).then_inc(s.da_pt, 1)
                    z_silu(2 * u + 1)
                    act.wait_ge(s.da_pv, 4 * l + u + 1)
                    if u >= 2:
                        act.wait_ge(s.a_lo, 4 * l + u - 1)
                    nc.scalar.activation(acc[:, u % 2, :, :], tr[:, :], ACT.Copy).then_inc(s.da_out, 1)
                    by_token(2 * u)
                by_token(7)

                def gate_sig(n):
                    act.wait_ge(s.ssd_ydone, XCH * l + 2 * n + 2)
                    slab = slab_at("gates", n, l)
                    nc.scalar.activation(gates[:, n, :, :], lin[slab.bank][:, :, :], ACT.Sigmoid)\
                        .then_inc(s.bank_free[slab.bank], 1)

                for m in range(XCH // 2):
                    for head in range(4 * m, 4 * m + 4):
                        i = head % 2
                        act.wait_ge(s.ssd_seg, SH * l + head + 1)
                        nc.scalar.activation(seg_e[:, i, :], seg[:, i, :], ACT.Exp).then_inc(s.ssd_exp, 1)
                    done(slab_at("gates", m, l))
                    if m % 2 == 1:
                        for n in range(max(0, m - 2), m):
                            gate_sig(n)

                def bn_square(g):
                    nc.scalar.activation(sq[:, 4 * (g % 2):4 * (g % 2) + 4, :], zs[:, 4 * g:4 * g + 4, :], ACT.Square)\
                        .then_inc(s.bn_sq, 1)

                def bn_round(g):
                    act.wait_ge(s.bn_chain, 2 * (SG * l + g) + 2)
                    part = h_hi[:, 4 * g:4 * g + 4, :] if g < 2 else hid_hi[:, 4 * g - 8:4 * g - 4, :]
                    nc.scalar.activation(part, zs[:, 4 * g:4 * g + 4, :], ACT.Copy).then_inc(s.bn_hi, 1)

                act.wait_ge(s.ssd_ydone, XCH * (l + 1))
                bn_square(0)
                bn_square(1)
                gate_sig(XCH // 2 - 1)
                for g in range(SG):
                    done(slab_at("pa", g, l))
                    act.wait_ge(s.bn_sum, SG * l + g + 1)
                    if g >= 2:
                        act.wait_ge(s.bn_chain, 2 * (SG * l + g - 1))
                    nc.scalar.activation(std[:, g % 2, 0:T], (tr, stat)[g % 2][:, 0:T], ACT.Sqrt, bias=eps[:, :])\
                        .then_inc(s.bn_std, 1)
                    if g + 2 < SG:
                        bn_square(g + 2)
                    if g in (1, 2):
                        bn_round(g - 1)
                bn_round(2)
                bn_round(3)

                def merge_round(slab, n, j):
                    if n < 6:
                        done(slab)
                    if n >= 4:
                        slab.wait_released(act)
                        nc.scalar.activation(h_hi[:, 2 * j:2 * j + 2, :], merged[:, 2 * j:2 * j + 2, :], ACT.Copy)\
                            .then_inc(s.merged_hi, 1)
                    if n >= 6:
                        done(slab)
                straight("ps", merge_round, l)
                residual("out", l)
                norm(5 + 2 * l)
                ffn(None, l)

            for l in range(2):
                layer(l)
            norm(8)

        @block.vector
        def _(dve):
            tt, stt, ts = nc.vector.tensor_tensor, nc.vector.scalar_tensor_tensor, nc.vector.tensor_scalar

            def norm(n, gain):
                dve.wait_ge(s.norm_std, n + 1)
                nc.vector.reciprocal(std[:, 0, 0:T], std[:, 0, 0:T]).then_inc(s.norm_rstd, 1)
                dve.wait_ge(s.norm_rstd, n + 1)
                for c in range(DC):
                    stt(sq[:, c, :], x[:, c, :], gain(c), std[:, 0, 0:T], ALU.mult, ALU.mult).then_inc(s.h_f32, 1)
                for c in range(DC // 2, DC):
                    dve.wait_ge(s.h_hi, DC * n + c + 1)
                    lo_part(nc.vector, h_lo[:, c, :], sq[:, c, :], h_hi[:, c, :]).then_inc(s.h_lo_v, 1)

            def weights(slab, later=0):
                target = slab.ahead()
                if target is not None:
                    target.number = target.number + later
                    split_lo(dve, target, 1)

            def softplus(chain, out, arg, mag, e, scratch):
                a, b = scratch
                chain.link(ts(a, e, 2.0, None, ALU.add))
                chain.link(nc.vector.reciprocal(b, a))
                chain.link(tt(e, e, b, ALU.mult))
                chain.link(tt(a, e, e, ALU.mult))
                chain.link(ts(b, a, 1.0 / 15.0, None, ALU.mult))
                for odd in (13, 11, 9, 7, 5, 3):
                    chain.link(stt(b, b, 1.0 / odd, a, ALU.add, ALU.mult))
                chain.link(stt(b, b, 1.0, e, ALU.add, ALU.mult))
                chain.link(ts(a, arg, 0.0, None, ALU.max))
                chain.link(stt(out, b, 2.0, a, ALU.mult, ALU.add))

            def add_residual(stage, l=None):
                pairs = x[:, :, :].rearrange("p (j i) t -> p j i t", i=2)

                def body(slab, n, j):
                    if n < COUNT[stage] - 2:
                        weights(slab)
                    slab.wait_done(dve)
                    if n >= 4:
                        slab_at(stage, n - 4, l).wait_released(dve)
                    elif stage[:3] == "dnB":
                        slab_at(stage.replace("B", "A"), n, l).wait_released(dve)
                    tt(pairs[:, j, :, :], pairs[:, j, :, :], lin[slab.bank][:, :, :], ALU.add)\
                        .then_inc(s.bank_free[slab.bank], 1)
                    if n >= COUNT[stage] - 2:
                        weights(slab)
                straight(stage, body, l)

            def older_taps(outs, ins_, taps, weight, sem, base, release=None):
                k = len(outs)
                for d in range(1, taps):
                    for i in range(k):
                        if d >= 2:
                            dve.wait_ge(sem, base + (d - 2) * k + i + 1)
                        ins = stt(outs[i][:, d:T], ins_[i][:, 0:T - d], weight(taps - 1 - d, i), outs[i][:, d:T],
                                  ALU.mult, ALU.add)
                        last = d == taps - 1 and i == k - 1
                        ins.then_inc(release if last and release is not None else sem, 1)
                return base + (taps - 1) * k

            def ffn(f, l=None):
                sfx, base = stage_ffn(f, l)

                def up(off):
                    def body(slab, n, j):
                        b = j % 2
                        bank = lin[slab.bank]
                        c = off + n
                        weights(slab)
                        if l is None:
                            dve.wait_ge(s.ffn_t0, base + c + 1)
                            older_taps([acc[:, b, 0, :]], [bank[:, 0, :]], FFN_TAPS,
                                       lambda k, i: pcol(f"fw{f}", k * FC + c), s.ffn_tap, 2 * (base + c))
                            dve.wait_ge(s.ffn_silu, base + c + 1)
                            value = bank[:, 1, :]
                        else:
                            dve.wait_ge(s.ffn2_t0, l * FC + c + 1)
                            added = older_taps([acc[:, b, 0, :], acc[:, b, 1, :]], [bank[:, 0, :], bank[:, 1, :]], FFN_TAPS,
                                               lambda k, i: pcol2(l, "fw", k * 2 * FC + i * FC + c), s.ffn2_tap,
                                               3 * (l * FC + c), s.bank_free[slab.bank])
                            dve.wait_ge(s.ffn2_silu, l * FC + c + 1)
                            slab.wait_released(dve)
                            value = acc[:, b, 1, :]
                        dve.wait_ge(s.hid_split, base + c + 1)
                        tt(prod[:, b, :], sil[:, b, :], value, ALU.mult)\
                            .then_inc(s.bank_free[slab.bank] if l is None else s.ffn2_prod, 1)
                    return body
                slabs(dve, "upA" + sfx, up(0), l)
                add_residual("dnA" + sfx, l)
                slabs(dve, "upB" + sfx, up(UP_A), l)
                add_residual("dnB" + sfx, l)

            dve.wait_ge(s.loaded, 80)
            dve.wait_ge(s.pads, 1)
            lam = par[:, PCOL["lam"]:PCOL["lam"] + NC4, :].rearrange("p c a -> p (c a)")
            chain = Chain(dve, s.lam_chain)
            for n in range(WSLOTS):
                split_lo(dve, Slab(s, n, 0), 1)
            norm(0, lambda c: pcol("mix_g0", c))

            def cf_u(slab, n, j):
                weights(slab)
                dve.wait_ge(s.cf_sig, n + 1)
                tt(u_pad[:, n, CF_TAPS - 1:], lin[slab.bank][:, 0, :], sq[:, n, :], ALU.mult)\
                    .then_inc(s.bank_free[slab.bank], 1)
            slabs(dve, "ev_cf", cf_u)
            stage_released(dve, "ev_cf")
            for c in range(NC4):
                ts(cf_acc[:, c, :], u_pad[:, c, CF_TAPS - 1:], pcol("cf_w", (CF_TAPS - 1) * NC4 + c), pcol("cf_b", c),
                   ALU.mult, ALU.add).then_inc(s.cf_tap, 1)
            with dve.Fori(0, (CF_TAPS - 1) // 3) as i:
                for d in range(3):
                    for c in range(NC4):
                        dve.wait_ge(s.cf_tap, (i * 3 + d) * NC4 + c + 1)
                        stt(cf_acc[:, c, :], u_pad[:, c, bass.ds(i * 3 + d, T)], pcol("cf_w", (i * 3 + d) * NC4 + c),
                            cf_acc[:, c, :], ALU.mult, ALU.add).then_inc(s.cf_tap, 1)
            stage_released(dve, "ev_sc")
            stage_released(dve, "ev_b")
            sc = Chain(dve, s.sc_chain)
            sc.link(tt(t_pad[:, :, SC_TAPS - 1:], sc_c[:, :, :], sc_x[:, :, :], ALU.mult))
            dve.wait_ge(s.ln_mean, 1)
            tt(diff[:, :, :], cf_acc[:, :, :], stat[:, 0:T].unsqueeze(1).to_broadcast([P, NC4, T]), ALU.subtract)\
                .then_inc(s.ln_diff, 1)
            for c in range(NC4):
                ins = ts(sc_acc[:, c, :], t_pad[:, c, 2:], pcol("sc_w", 2 * NC4 + c), None, ALU.mult)
            sc.link(ins)
            for k in (1, 0):
                for c in range(NC4):
                    ins = stt(sc_acc[:, c, :], t_pad[:, c, k:k + T], pcol("sc_w", k * NC4 + c), sc_acc[:, c, :],
                              ALU.mult, ALU.add)
                sc.link(ins)
            tt(sc_acc[:, :, :], sc_acc[:, :, :], sc_b[:, :, :], ALU.mult).then_inc(s.y_sc, 1)
            dve.wait_ge(s.ln_std, 1)
            nc.vector.reciprocal(std[:, 0, 0:T], std[:, 0, 0:T]).then_inc(s.ln_rstd, 1)
            dve.wait_ge(s.ln_rstd, 1)
            dve.wait_ge(s.ln_diff, 1)
            tt(diff[:, :, :], diff[:, :, :], std[:, 0, 0:T].unsqueeze(1).to_broadcast([P, NC4, T]), ALU.mult)\
                .then_inc(s.ln_scaled, 1)
            dve.wait_ge(s.y_sc_hi, 1)
            lo_part(nc.vector, hid_lo[:, 0:NC4, :], sc_acc[:, :, :], hid_hi[:, 0:NC4, :]).then_inc(s.y_sc_lo, 1)
            dve.wait_ge(s.u_ready, 1)
            lo_part(nc.vector, hid_lo[:, NC4:2 * NC4, :], sq[:, 0:NC4, :], hid_hi[:, NC4:2 * NC4, :]).then_inc(s.u_lo, 1)
            take_over(dve, "ev_out")
            add_residual("ev_out")
            norm(1, lambda c: pcol("ffn_g0", c))
            ffn(0)

            norm(2, lambda c: pcol("mix_g1", c))
            chain.link(stt(small[:, 4:8], lam, -1.0, lam, ALU.mult, ALU.max))
            ts(small[:, 12:16], lam, -1.0, None, ALU.mult)
            dve.wait_ge(s.lam_e, 1)
            softplus(chain, small[:, 4:8], small[:, 12:16], None, small[:, 8:12], (small[:, 58:62], small[:, 32:36]))
            chain.link(ts(small[:, 0:4], small[:, 4:8], -8.0, None, ALU.mult))
            assert chain.n == LAM_LINKS

            def lru_conv(slab, n, j):
                weights(slab)
                dve.wait_ge(s.lru_t0, n + 1)
                older_taps([lru_xc[:, n, :]], [lin[slab.bank][:, 0, :]], LRU_TAPS,
                           lambda k, i: pcol("lru_w", k * NC4 + n), s.lru_tap, 2 * n, s.bank_free[slab.bank])
            slabs(dve, "od_lru", lru_conv)

            def qk_norm(slab, n, j):
                weights(slab)
                dve.wait_ge(s.qk_std, n + 1)
                nc.vector.reciprocal(std[:, n % 2, :], std[:, n % 2, :]).then_inc(s.qk_chain, 1)
                dve.wait_ge(s.qk_chain, n + 1)
                stt(qn[:, n, :], lin[slab.bank][:, 0, :], pcol("q_g"), std[:, n % 2, 0:T], ALU.mult, ALU.mult)
                stt(kn[:, n, :], lin[slab.bank][:, 1, :], pcol("k_g"), std[:, n % 2, T:2 * T], ALU.mult, ALU.mult)\
                    .then_inc(s.bank_free[slab.bank], 1)
            slabs(dve, "od_qk", qk_norm)

            lc = Chain(dve, s.lru_chain)
            dve.wait_ge(s.lru_i, 1)
            stage_released(dve, "od_lru")
            lc.link(tt(lru_i[:, :, :], lru_i[:, :, :], lru_xc[:, :, :], ALU.mult))
            dve.wait_ge(s.lru_a, 1)
            lc.link(ts(lru_m[:, :, :], lru_th[:, :, :], -1.0, 1.0, ALU.mult, ALU.add))
            lc.link(nc.vector.reciprocal(lru_r[:, :, :], lru_m[:, :, :]))
            stt(lru_m[:, :, :], lru_th[:, :, :], -2.0, lru_r[:, :, :], ALU.mult, ALU.mult).then_inc(s.lru_m2, 1)
            dve.wait_ge(s.lru_mult, 1)
            lc.link(tt(lru_i[:, :, :], lru_i[:, :, :], lru_th[:, :, :], ALU.mult))
            for c in range(NC4):
                ins = nc.vector.tensor_tensor_scan(lru_hs[:, c, :], lru_a[:, c, :], lru_i[:, c, :], 0.0, ALU.mult, ALU.add)
            lc.link(ins)
            tt(lru_hs[:, :, :], lru_hs[:, :, :], lru_gate[:, :, :], ALU.mult).then_inc(s.lru_y, 1)

            ac = Chain(dve, s.at_chain)
            for u in range(2 * DIL_H):
                head, t = u // 2, u % 2
                n = (t + 1) * P
                dve.wait_ge(s.at_logits, u + 1)
                if u >= 2:
                    dve.wait_ge(s.at_tr, u - 1)
                sc3 = score[:, u % 2, 0:DIL_G * n].rearrange("p (g k) -> p g k", g=DIL_G)
                stt(sc3, logit[:, 0:DIL_G, 0:n], DIL_D ** -0.5,
                    dil[:, DIL_AT[t]:DIL_AT[t] + DIL_G * n].rearrange("p (g k) -> p g k", g=DIL_G), ALU.mult, ALU.add)\
                    .then_inc(s.at_masked, 1)
                dve.wait_ge(s.at_masked, u + 1)
                nc.vector.tensor_reduce(small[:, 16 + u:17 + u], score[:, u % 2, 0:DIL_G * n], AX_X, ALU.max, negate=True)\
                    .then_inc(s.at_max, 1)
                if u == 0:
                    dve.wait_ge(s.lru_y_hi, 1)
                    lo_part(nc.vector, hid_lo[:, 0:NC4, :], lru_hs[:, :, :], hid_hi[:, 0:NC4, :]).then_inc(s.lru_y_lo, 1)
                dve.wait_ge(s.at_exp, u + 1)
                ac.link(nc.vector.reciprocal(small[:, 32 + u:33 + u], small[:, 24 + u:25 + u]))
                ts(score[:, u % 2, 0:DIL_G * n], score[:, u % 2, 0:DIL_G * n], small[:, 32 + u:33 + u], None, ALU.mult)\
                    .then_inc(s.at_p, 1)
            dve.wait_ge(s.att_hi, 1)
            lo_part(nc.vector, hid_lo[:, NC4:NC4 + 2, :], acc[:, 0, :, :], hid_hi[:, NC4:NC4 + 2, :]).then_inc(s.att_lo, 1)
            take_over(dve, "od_out")
            add_residual("od_out")
            norm(3, lambda c: pcol("ffn_g1", c))
            ffn(1)

            def layer(l):
                norm(4 + 2 * l, lambda c: pcol2(l, "mix_g", c))
                rope_unit = [0]

                def rope(out, chunks, which):
                    r = rope_unit[0]
                    rope_unit[0] += 1
                    base = 8 * 2 * l + 2 * r
                    raw, part = rope_raw[:, r % 2, 0:chunks, :], rope_t[:, 0, 0:chunks, :]
                    cos, sin = (const(f"{f}_{which}", T).unsqueeze(1).to_broadcast([P, chunks, T])
                                for f in ("cos", "sin"))
                    dve.wait_ge(s.rope_rot, 8 * l + r + 1)
                    tt(out, raw, cos, ALU.mult).then_inc(s.rope_chain, 1)
                    tt(part, stat[:, 0:chunks * T].rearrange("p (c t) -> p c t", t=T), sin, ALU.mult)\
                        .then_inc(s.rope_chain, 1)
                    dve.wait_ge(s.rope_chain, base + 2)
                    tt(out, out, part, ALU.add).then_inc(s.rope_done, 1)

                rope(ki2[:, :, :], 1, "idx")
                dt, adt, cum = (dtb[0:SH, i, :] for i in range(3))
                arg, mag = dscr[0:SH, 2, :], dscr[0:SH, 3, :]
                Slab(s, AT2["kidt"], l * (PER_LAYER // RING)).wait_released(dve)
                stt(mag, arg, -1.0, arg, ALU.mult, ALU.max).then_inc(s.dt_abs, 1)
                dve.wait_ge(s.dt_e, l + 1)
                ch = Chain(dve, s.dt_chain, DT_LINKS * l)
                softplus(ch, dt, arg, None, mag, (adt, cum))
                dve.wait_ge(s.a_exp, l + 1)
                ch.link(ts(adt, dt, small[0:SH, 40:41], -1.0, ALU.mult, ALU.mult))
                ch.link(nc.vector.tensor_tensor_scan(cum, adt, adt, 0.0, ALU.add, ALU.min))
                assert ch.n == DT_LINKS

                ix = Chain(dve, s.ix_chain, IX_LINKS * l)

                def index_scores(t, half):
                    n = (t + 1) * P
                    row = ix_sc[:, 0, 0:n]
                    b = 2 * t + half
                    dve.wait_ge(s.ix_rel, 4 * l + b + 1)
                    for i in range(4):
                        head, rel = 4 * half + i, ix_rel[:, b, 2 * (i % 2) + i // 2, 0:n]
                        w = small[:, 42 + t * IH + head:43 + t * IH + head]
                        if head == 0:
                            ix.link(ts(row, rel, w, None, ALU.mult))
                        else:
                            ix.link(stt(row, rel, w, row, ALU.mult, ALU.add))
                    if half == 1:
                        ix.link(tt(row, row, const(f"causal{t}", n), ALU.add))

                def top_eights(t, rounds):
                    n = (t + 1) * P
                    for r in rounds:
                        now = ix_sc[:, 0, 0:n] if r == 0 else ix_w[:, (r - 1) % 2, 0:n]
                        ix.link(nc.vector.max(small[:, 0:8], now))
                        ix.link(nc.vector.match_replace(ix_w[:, r % 2, 0:n], small[:, 0:8], now, TAKEN))

                def selection(t):
                    n = (t + 1) * P
                    last = ix_w[:, (TOPK // 8 - 1) % 2, 0:n]
                    ix.link(ts(sel[:, t, 0:n], last, TAKEN / 2, NEG, ALU.is_gt, ALU.mult))
                    ix.link(tt(sel[:, t, 0:n], sel[:, t, 0:n], const(f"causal{t}", n), ALU.add))

                take_over(dve, "qi", l)
                for n in range(2):
                    weights(slab_at("qi", n, l))
                    rope(qi2[:, 2 * n:2 * n + 2, :], 2, "idx")
                weights(slab_at("k", 0, l))
                rope(k2[:, :, :], 2, "attn")
                weights(slab_at("q", 0, l))
                rounds = TOPK // 8
                for n in range(4):
                    rope(q2[:, 2 * n:2 * n + 2, :], 2, "attn")
                    weights(slab_at("q", n + 1, l) if n < 3 else slab_at("v", 0, l))
                    if n < 2:
                        index_scores(0, n)
                    elif n == 2:
                        top_eights(0, range(0, rounds // 2))
                    else:
                        top_eights(0, range(rounds // 2, rounds))
                        selection(0)

                def xbc_taps(slab, n, j):
                    b = j % 2
                    weights(slab)
                    dve.wait_ge(s.xbc_t0, 12 * l + n + 1)
                    older_taps([acc[:, b, i, :] for i in range(2)], [lin[slab.bank][:, i, :] for i in range(2)],
                               SSD_TAPS, lambda k, i: pcol2(l, "ssd_w", k * XBC_CH + 2 * n + i), s.xbc_tap,
                               5 * (12 * l + n), s.bank_free[slab.bank])
                    if n < 2:
                        index_scores(1, n)
                    elif n < 2 + rounds:
                        top_eights(1, range(n - 2, n - 1))
                    elif n == 2 + rounds:
                        selection(1)
                assert COUNT["xbc"] > 2 + rounds
                straight("xbc", xbc_taps, l)
                assert ix.n == IX_LINKS

                dc = Chain(dve, s.da_chain, 8 * l)
                for u in range(4):
                    t, kv = u // 2, u % 2
                    n = (t + 1) * P
                    dve.wait_ge(s.da_logits, 4 * l + u + 1)
                    if u >= 1:
                        dve.wait_ge(s.da_tr, 4 * l + u)
                    sc4 = da_score[:, :, 0:n]
                    for i in range(QPK):
                        ins = stt(sc4[:, i, :], logit[:, i, 0:n], HD ** -0.5, sel[:, t, 0:n], ALU.mult, ALU.add)
                    dc.link(ins)
                    nc.vector.tensor_reduce(small[:, 16:20], sc4, AX_X, ALU.max, negate=True).then_inc(s.da_max, 1)
                    dve.wait_ge(s.da_exp, 4 * l + u + 1)
                    dc.link(nc.vector.reciprocal(small[:, 32:36], small[:, 24:28]))
                    for i in range(QPK):
                        ins = ts(sc4[:, i, :], sc4[:, i, :], small[:, 32 + i:33 + i], None, ALU.mult)
                    ins.then_inc(s.da_p, 1)
                    weights(slab_at("z", 2 * u, l))
                    weights(slab_at("z", 2 * u + 1, l))

                dt_tok = dt_tok_sb[:, :].rearrange("p (i t h) -> p i t h", i=2, t=2)
                dve.wait_ge(s.dt_tok, l + 1)

                def ssd_seg(c, j, i):
                    head = 2 * c + i
                    dve.wait_ge(s.ssd_abc, XCH * l + c + 1)
                    for t, (lo, n) in enumerate(((0, T), (T, P))):
                        ins = ts(seg[:, i, lo:lo + n], logit[:, 2 * (j % 2) + i, T - n:T], dt_tok[:, 1, t, bass.ds(head, 1)],
                                 0.0, ALU.subtract, ALU.min)
                    ins.then_inc(s.ssd_seg, 1)

                def ssd_m(c, j, i):
                    head = 2 * c + i
                    dve.wait_ge(s.ssd_exp, SH * l + head + 1)
                    for t, (lo, n) in enumerate(((0, T), (T, P))):
                        ins = stt(m_buf[:, 2 * (j % 2) + i, lo:lo + n], seg_e[:, i, lo:lo + n],
                                  dt_tok[:, 0, t, bass.ds(head, 1)], cbm[:, lo:lo + n], ALU.mult, ALU.mult)
                    ins.then_inc(s.ssd_m, 1)

                def ssd_out(c, j):
                    dve.wait_ge(s.ssd_y, XCH * l + c + 1)
                    stt(y_raw[:, j % 2, :], xbc[:, c, :], pcol2(l, "ssd_d", c), (tr, stat)[j % 2][:, 0:T],
                        ALU.mult, ALU.add).then_inc(s.ssd_chain, 1)
                    dve.wait_ge(s.ssd_chain, XCH * l + c + 1)
                    tt(zs[:, c, :], y_raw[:, j % 2, :], zs[:, c, :], ALU.mult).then_inc(s.ssd_ydone, 1)

                def ssd_group(g, first):
                    dve.wait_ge(s.ssd_cb, SG * l + g + 1)
                    tt(cbm[:, 0:T], tr[:, 0:T], const("tril", T + P)[:, 0:T], ALU.mult)
                    tt(cbm[:, T:T + P], tr[:, T:T + P], const("tril", T + P)[:, T:], ALU.mult).then_inc(s.ssd_cbm, 1)
                    dve.wait_ge(s.ssd_cbm, SG * l + g + 1)
                    for j in range(4):
                        c = 4 * g + j
                        ssd_seg(c, j, 0)
                        ssd_seg(c, j, 1)
                        ssd_m(c, j, 0)
                        ssd_m(c, j, 1)
                        if j >= 1 or not first:
                            ssd_out(c - 1, j + 3)
                        if j % 2 == 1:
                            weights(slab_at("gates", j // 2, l), 2 * g)
                ssd_group(0, True)
                with dve.Fori(1, SG) as g:
                    ssd_group(g, False)
                ssd_out(XCH - 1, 3)

                def pa(slab, n):
                    weights(slab)
                    slab.wait_done(dve)
                    tt(merged[:, 2 * n:2 * n + 2, :], lin[slab.bank][:, :, :], gates[:, 2 * n:2 * n + 2, 0, :], ALU.mult)\
                        .then_inc(s.bank_free[slab.bank], 1)

                def bn_rest(g):
                    dve.wait_ge(s.bn_hi, SG * l + g + 1)
                    part = (slice(None), slice(4 * (g % 2), 4 * (g % 2) + 4), slice(None))
                    lo, hi = (h_lo, h_hi) if g < 2 else (hid_lo, hid_hi)
                    lo_part(nc.vector, lo[part], zs[:, 4 * g:4 * g + 4, :], hi[part]).then_inc(s.bn_lo, 1)

                for g in range(SG):
                    pa(slab_at("pa", g, l), g)
                    dve.wait_ge(s.bn_std, SG * l + g + 1)
                    nc.vector.reciprocal(std[:, g % 2, 0:T], std[:, g % 2, 0:T]).then_inc(s.bn_chain, 1)
                    dve.wait_ge(s.bn_chain, 2 * (SG * l + g) + 1)
                    for c in range(4 * g, 4 * g + 4):
                        ins = stt(zs[:, c, :], zs[:, c, :], pcol2(l, "ssd_norm", c), std[:, g % 2, 0:T], ALU.mult, ALU.mult)
                    ins.then_inc(s.bn_chain, 1)
                    if g in (1, 2):
                        bn_rest(g - 1)
                bn_rest(2)
                bn_rest(3)
                stage_released(dve, "pa", l)

                def merged_rest(j):
                    dve.wait_ge(s.merged_hi, 4 * l + j + 1)
                    pair_of = (slice(None), slice(2 * j, 2 * j + 2), slice(None))
                    lo_part(nc.vector, h_lo[pair_of], merged[pair_of], h_hi[pair_of]).then_inc(s.merged_lo, 1)

                pc = Chain(dve, s.ps_chain, 8 * l)

                def ps(slab, n, j):
                    if n < 6:
                        weights(slab)
                    slab.wait_done(dve)
                    if n >= 4:
                        slab_at("ps", n - 4, l).wait_released(dve)
                    part = acc[:, n % 2, :, :]
                    pc.link(tt(part, lin[slab.bank][:, :, :], gates[:, 2 * j:2 * j + 2, 1, :], ALU.mult))
                    tt(merged[:, 2 * j:2 * j + 2, :], merged[:, 2 * j:2 * j + 2, :], part, ALU.add)\
                        .then_inc(s.bank_free[slab.bank], 1)
                    if n >= 5:
                        merged_rest(j - 1)
                    if n >= 6:
                        weights(slab)
                straight("ps", ps, l)
                merged_rest(3)
                add_residual("out", l)
                norm(5 + 2 * l, lambda c: pcol2(l, "ffn_g", c))
                ffn(None, l)

            for l in range(2):
                layer(l)
            dve.wait_ge(s.norm_std, 9)
            nc.vector.reciprocal(std[:, 0, 0:T], std[:, 0, 0:T]).then_inc(s.norm_rstd, 1)
            dve.wait_ge(s.norm_rstd, 9)
            for half in range(2):
                for c in range(half * DC // 2, (half + 1) * DC // 2):
                    ins = stt(sq[:, c, :], x[:, c, :], pcol("final_g", c), std[:, 0, 0:T], ALU.mult, ALU.mult)
                ins.then_inc(s.final, 1)


def constants():
    c = np.zeros((P, NCONST), np.float32)
    dil = np.zeros((P, NDIL), np.float32)

    def put(name, a):
        c[:a.shape[0], CCOL[name]:CCOL[name] + a.shape[1]] = a

    put("ident", np.eye(P))
    put("mean1024", np.full((P, P), 1 / 1024))
    put("mean512", np.full((P, P), 1 / 512))
    put("mean64", np.kron(np.eye(2), np.full((64, 64), 1 / 64)))
    for name, dim, heads in (("attn", HD, 1), ("idx", ID, 2)):
        rot = dim // ROPE_FRACTION
        half = rot // 2
        inv = np.float32(ROPE_THETA) ** (-np.arange(0, rot, 2, dtype=np.float32) / np.float32(rot))
        ang = np.arange(T, dtype=np.float32)[None, :] * inv.astype(np.float32)[:, None]
        swap, cos, sin = np.zeros((dim, dim)), np.ones((dim, T), np.float32), np.zeros((dim, T), np.float32)
        for i in range(half):
            swap[i, i + half] = swap[i + half, i] = 1
        cos[0:half] = cos[half:rot] = np.cos(ang)
        sin[0:half], sin[half:rot] = -np.sin(ang), np.sin(ang)
        put(f"swap_{name}", np.kron(np.eye(heads), swap))
        put(f"cos_{name}", np.tile(cos, (heads, 1)))
        put(f"sin_{name}", np.tile(sin, (heads, 1)))
    q, k = np.arange(T)[:, None], np.arange(T)[None, :]
    for t in range(2):
        rows, n = slice(t * P, (t + 1) * P), (t + 1) * P
        seen = [(k <= q) & (q - k <= w) & ((q - k) % d == 0) for w, d in DIL]
        dil[:, DIL_AT[t]:DIL_AT[t] + DIL_G * n] = np.concatenate([np.where(m, 0.0, NEG)[rows, :n] for m in seen], axis=1)
        put(f"causal{t}", np.where(k <= q, 0.0, NEG)[rows, :n])
    after = (k >= q).astype(np.float32)
    put("tril", np.concatenate([after[0:P, :], after[P:, P:]], axis=1))
    return c, dil


def slab_of(w, cols, chunks=None):
    kc = w.shape[0] // P
    w = w.reshape(kc, P, w.shape[1])
    return np.stack([np.ascontiguousarray(w[:, :, c].transpose(1, 0, 2)).reshape(P, -1) for c in cols])


def tile(n, at=0):
    return np.arange(at + n * P, at + n * P + P)


def pair(a, b, at=0, at_b=None):
    return np.concatenate([tile(a, at), tile(b, at if at_b is None else at_b)])


def pairs(n, at=0):
    return [pair(2 * j, 2 * j + 1, at) for j in range(n // 2)]


def down_slabs(w, groups):
    out = []
    for c0, n in groups:
        part = slab_of(w[c0 * P:(c0 + n) * P], pairs(DC))
        out.append(np.pad(part, ((0, 0), (0, 0), (0, KC * 256 - part.shape[2]))))
    return np.concatenate(out)


def by_channel(a):
    a = a.reshape(-1, a.shape[-1] // P, P)
    return a.transpose(2, 0, 1).reshape(P, -1)


def column(a):
    return np.pad(a.reshape(-1, 1), ((0, P - a.size), (0, 0)))


_OUT = (1, T, D)


def kernel(**inputs):
    import concourse.bacc as bacc
    from concourse.bass_utils import run_bass_kernel_spmd

    i = {k: np.asarray(v) for k, v in inputs.items()}
    arrays = {"x": np.ascontiguousarray(i["x"][0].T.reshape(DC, P, T).transpose(1, 0, 2))}
    arrays["consts"], arrays["dil"] = constants()
    ev, od = i["ev_w_in"][0], i["od_w_in"][0]
    arrays["ev_cf"] = slab_of(ev, [pair(c, c, 3 * SC, 3 * SC + CF) for c in range(NC4)])
    arrays["ev_sc"] = slab_of(ev, [pair(c, c, SC, 2 * SC) for c in range(NC4)])
    arrays["ev_b"] = slab_of(ev, pairs(NC4))
    arrays["ev_out"] = slab_of(i["ev_w_out"][0], pairs(DC))
    arrays["od_lru"] = slab_of(od, [pair(c, c, 0, LRU) for c in range(NC4)])
    arrays["od_qk"] = slab_of(od, [pair(c, c, 2 * LRU, 2 * LRU + DIL_W) for c in range(DIL_W // P)])
    arrays["od_v"] = slab_of(od, pairs(DIL_W // P, 2 * LRU + 2 * DIL_W))
    arrays["od_out"] = slab_of(i["od_w_out"][0], pairs(DC))
    for f in range(2):
        both = np.concatenate([i["ffn_w_gate"][f], i["ffn_w_up"][f]], axis=1)
        arrays[f"upA{f}"], arrays[f"upB{f}"] = (slab_of(both, [pair(c, c, 0, FF) for c in part]) for part in UP_CHUNKS)
        arrays[f"dnA{f}"] = down_slabs(i["ffn_w_down"][f], DOWN_GROUPS[0:1])
        arrays[f"dnB{f}"] = down_slabs(i["ffn_w_down"][f], DOWN_GROUPS[1:])
    at = np.cumsum((0,) + IN_SPLITS)
    stages = {name: [] for name, _ in SECOND}
    for l in range(2):
        w = i["w_in_2"][l]
        ki = np.arange(at[4], at[5])
        kidt = slab_of(np.concatenate([w, np.zeros((D, 256 - P - SH), np.float32)], axis=1),
                       [np.concatenate([ki, ki, np.arange(at[8], at[9]), np.arange(w.shape[1], w.shape[1] + 256 - P - SH)])])
        stages["kidt"].append(kidt)
        stages["wi"].append(slab_of(w, [np.arange(at[5], at[6])]))
        stages["qi"].append(slab_of(w, pairs(4, at[3])))
        stages["q"].append(slab_of(w, pairs(8, at[0])))
        stages["k"].append(slab_of(w, pairs(2, at[1])))
        stages["v"].append(slab_of(w, pairs(2, at[2])))
        stages["xbc"].append(slab_of(w, pairs(XBC_CH, at[7])))
        stages["z"].append(slab_of(w, pairs(XCH, at[6])))
        stages["gates"].append(slab_of(w, [pair(m, m, at[9], at[10]) for m in range(DC)]))
        stages["pa"].append(slab_of(i["w_proj_attn_2"][l], pairs(DC)))
        stages["ps"].append(down_slabs(i["w_proj_ssd_2"][l], ((0, 8), (8, 8))))
        stages["out"].append(slab_of(i["w_out_2"][l], pairs(DC)))
        for part, name in zip(UP_CHUNKS, ("upA", "upB")):
            stages[name].append(slab_of(i["ffn_w_up_2"][l], [pair(c, c, 0, FF) for c in part]))
        stages["dnA"].append(down_slabs(i["ffn_w_down_2"][l], DOWN_GROUPS[0:1]))
        stages["dnB"].append(down_slabs(i["ffn_w_down_2"][l], DOWN_GROUPS[1:]))
    for name, parts in stages.items():
        arrays[name] = np.concatenate(parts)

    first = [i["mix_norm_g"][0], i["ffn_norm_g"][0], i["mix_norm_g"][1], i["ffn_norm_g"][1], i["ev_sc_conv_w"][0],
             i["ev_cf_conv_w"][0], i["ev_cf_conv_b"][0], i["ev_cf_ln_g"][0], i["ev_cf_ln_b"][0], i["od_lru_conv_w"][0],
             i["od_lru_conv_b"][0], i["od_lru_ba"][0], i["od_lru_bx"][0], i["od_lru_lam"][0],
             np.tile(i["od_q_norm_g"][0], 2), np.tile(i["od_k_norm_g"][0], 2), i["ffn_conv_w"][0], i["ffn_conv_b"][0],
             i["ffn_conv_w"][1], i["ffn_conv_b"][1], i["norm_final_w_2"]]
    cols = [by_channel(a) for a in first]
    for l in range(2):
        cols += [by_channel(i[n][l]) for n in ("norm_mix_w_2", "norm_ffn_w_2", "ssd_conv_w_2", "ssd_conv_b_2", "ssd_norm_w_2")]
        cols.append(by_channel(np.repeat(i["ssd_d_2"][l], XI // SH)))
        cols += [column(i["ssd_dt_bias_2"][l]), column(i["ssd_a_log_2"][l])]
        cols += [by_channel(i["ffn_conv_w_2"][l]), by_channel(i["ffn_conv_b_2"][l])]
    arrays["params"] = np.ascontiguousarray(np.concatenate(cols, axis=1))
    assert arrays["params"].shape == (P, NPARAM)
    gate_w = np.zeros((P, 2 * NC4, P), np.float32)
    for n, w in enumerate((i["od_lru_wa"][0], i["od_lru_wx"][0])):
        for head in range(8):
            lo = 64 * (head % 2)
            gate_w[lo:lo + 64, NC4 * n + head // 2, lo:lo + 64] = w[head]
    arrays["gate_w"] = gate_w

    nc = bacc.Bacc("TRN2", target_bir_lowering=False, num_devices=1)
    arrays = {f"in_{k}": np.ascontiguousarray(a, dtype=np.float32) for k, a in arrays.items()}
    dram = {k[3:]: nc.dram_tensor(k, a.shape, F32, kind="ExternalInput").ap() for k, a in arrays.items()}
    dram["result"] = nc.dram_tensor("out_0", (P, DC, T), F32, kind="ExternalOutput").ap()
    build(nc, dram)
    got = run_bass_kernel_spmd(nc, [arrays], core_ids=[0]).results[0]["out_0"]
    return np.ascontiguousarray(got.transpose(1, 0, 2).reshape(D, T).T).reshape(_OUT)
```

```python
from contextlib import ExitStack

import numpy as np

import concourse.bass as bass
from concourse import mybir

F32 = mybir.dt.float32
F32R = mybir.dt.float32r
ALU = mybir.AluOpType
ACT = mybir.ActivationFunctionType
AX_X = mybir.AxisListType.X

P = 128
T = 256
D = 1024
DC = D // P
RING = 4
WSLOTS = 2
KC = 8
EPS = 1e-6
NEG = -1.0e30
TAKEN = -3.0e38

SC = CF = LRU = 512
NC4 = SC // P
SC_TAPS, CF_TAPS, LRU_TAPS, FFN_TAPS = 3, 31, 4, 3
CF_PE_TAPS = 6
CF_SUMS = CF_TAPS * NC4 - 2 * CF_PE_TAPS + 1
DIL = ((128, 1), (512, 4), (2048, 16))
DIL_G, DIL_H, DIL_D = 3, 4, 64
DIL_W = DIL_G * DIL_H * DIL_D
FF = 2816
FC = FF // P
DOWN_GROUPS = ((0, 8), (8, 8), (16, 6))
HID = 14
UP_CHUNKS = range(HID), range(HID, FC)
UP_A, UP_B = HID, FC - HID

NH, HD, NKV = 8, 128, 2
QPK = NH // NKV
IH, ID = 8, 64
TOPK = min(256, T // 4)
XI = 2048
XCH = XI // P
SH, SG, SN = 32, 4, 128
XBC = XI + 2 * SG * SN
XBC_CH = XBC // P
SSD_TAPS = 4
ROPE_THETA, ROPE_FRACTION = 500000.0, 4
IN_SPLITS = (NH * HD, NKV * HD, NKV * HD, IH * ID, ID, IH, XI, XBC, SH, D, D)

FIRST = [("ev_cf", 4), ("ev_sc", 4), ("ev_b", 2), ("ev_out", 4),
         ("upA0", UP_A), ("dnA0", 4), ("upB0", UP_B), ("dnB0", 8),
         ("od_lru", 4), ("od_qk", 6), ("od_v", 3), ("od_out", 4),
         ("upA1", UP_A), ("dnA1", 4), ("upB1", UP_B), ("dnB1", 8)]
SECOND = [("kidtwi", 1), ("qi", 2), ("k", 1), ("q", 4), ("v", 1), ("xbc", 12), ("z", 8),
          ("gates", 8), ("pa", 4), ("ps", 8), ("out", 4),
          ("upA", UP_A), ("dnA", 4), ("upB", UP_B), ("dnB", 8)]


def starts(stages, at):
    where = {}
    for name, n in stages:
        where[name] = at
        at += n
    return where, at


AT, SECOND_AT = starts(FIRST, 0)
AT2, END2 = starts(SECOND, SECOND_AT)
PER_LAYER = END2 - SECOND_AT
SLABS = SECOND_AT + 2 * PER_LAYER
WIDTH = {"od_out": 6 * 256}
COUNT = dict(FIRST + SECOND)


def columns(parts):
    where, at = {}, 0
    for name, n in parts:
        where[name] = at
        at += n
    return where, at


PCOL, P_FIRST = columns([
    ("mix_g0", DC), ("ffn_g0", DC), ("mix_g1", DC), ("ffn_g1", DC), ("sc_w", SC_TAPS * NC4),
    ("cf_w", CF_TAPS * NC4), ("cf_b", NC4), ("ln_g", NC4), ("ln_b", NC4), ("lru_w", LRU_TAPS * NC4),
    ("lru_b", NC4), ("lru_ba", NC4), ("lru_bx", NC4), ("lam", NC4), ("q_g", 1), ("k_g", 1),
    ("fw0", FFN_TAPS * FC), ("fb0", FC), ("fw1", FFN_TAPS * FC), ("fb1", FC), ("final_g", DC)])
PCOL2, P_LAYER = columns([
    ("mix_g", DC), ("ffn_g", DC), ("ssd_w", SSD_TAPS * XBC_CH), ("ssd_b", XBC_CH), ("ssd_norm", XCH),
    ("ssd_d", XCH), ("dt_bias", 1), ("a_log", 1), ("fw", FFN_TAPS * 2 * FC), ("fb", 2 * FC)])
NPARAM = P_FIRST + 2 * P_LAYER

CCOL, NCONST = columns([
    ("ident", P), ("mean1024", P), ("mean512", P), ("mean64", P), ("swap_attn", P), ("swap_idx", P),
    ("cos_attn", T), ("sin_attn", T), ("cos_idx", T), ("sin_idx", T),
    ("causal0", P), ("causal1", T), ("tril", T + P)])
DIL_AT = (0, DIL_G * P)
NDIL = DIL_G * (P + T)


class Semaphores:
    pass


class Slab:

    def __init__(self, sems, first, turns):
        self.sems, self.first, self.turns = sems, first, turns
        self.bank, self.slot = first % RING, first % WSLOTS
        self.use = turns + first // RING
        self.number = turns * RING + first
        self.fixed = isinstance(turns, int)

    def ahead(self):
        if self.fixed and self.number + WSLOTS >= SLABS:
            return None
        return Slab(self.sems, self.first + WSLOTS, self.turns)

    def wait_raw_free(self, eng):
        if not self.fixed or self.number >= WSLOTS:
            eng.wait_ge(self.sems.w_lo_a, self.number - WSLOTS + 1)
            eng.wait_ge(self.sems.w_lo_b, self.number - WSLOTS + 1)

    def wait_landed(self, eng):
        eng.wait_ge(self.sems.w_landed[self.slot], (self.turns * (RING // WSLOTS) + self.first // WSLOTS + 1) * 16)

    def wait_hi(self, eng, half):
        eng.wait_ge(self.sems.w_hi, 2 * self.number + half + 1)

    def wait_split(self, eng):
        eng.wait_ge(self.sems.w_lo_a, self.number + 1)
        eng.wait_ge(self.sems.w_lo_b, self.number + 1)

    def wait_bank_free(self, eng):
        if not self.fixed or self.number >= RING:
            eng.wait_ge(self.sems.bank_free[self.bank], self.use)

    def wait_done(self, eng):
        eng.wait_ge(self.sems.lin_done, self.number + 1)

    def wait_released(self, eng):
        eng.wait_ge(self.sems.bank_free[self.bank], self.use + 1)


def each_slab(sems, eng, first, count, turns, body, peel=0):
    whole = count // RING if count >= 2 * RING else 0
    for n in range(peel * RING if whole else 0):
        body(Slab(sems, first + n, turns), n, n % RING)
    if whole:
        with eng.Fori(peel, whole) as i:
            for j in range(RING):
                body(Slab(sems, first + j, turns + i), i * RING + j, j)
    for n in range(whole * RING, count):
        body(Slab(sems, first + n, turns), n, n % RING)


class Chain:

    def __init__(self, eng, sem, base=0):
        self.eng, self.sem, self.base, self.n = eng, sem, base, 0

    def link(self, ins):
        self.n += 1
        ins.then_inc(self.sem, 1)
        self.eng.wait_ge(self.sem, self.base + self.n)





SOFTPLUS_LINKS = 14
LAM_LINKS = SOFTPLUS_LINKS + 2
DT_LINKS = SOFTPLUS_LINKS + 2
IX_LINKS = 2 * (IH + 1 + 2 * (TOPK // 8) + 2)


def build(nc, dram):
    ctx = ExitStack()
    with ctx:
        def sb(name, shape, dtype=F32):
            return ctx.enter_context(nc.sbuf_tensor(name, shape, dtype))

        def psum(name, shape):
            return ctx.enter_context(nc.psum_tensor(name, shape, F32))

        def sem(name):
            return ctx.enter_context(nc.semaphore(name))

        s = Semaphores()
        s.x_loaded = [sem(f"x_loaded{j}") for j in range(4)]
        s.loaded = sem("loaded")
        s.loaded_later = sem("loaded_later")
        s.pads = sem("pads")
        s.lin_done = sem("lin_done")
        s.norm_sq = sem("norm_sq")
        s.norm_pre = sem("norm_pre")
        s.norm_sum = sem("norm_sum")
        s.norm_std = sem("norm_std")
        s.norm_rstd = sem("norm_rstd")
        s.h_f32 = sem("h_f32")
        s.h_hi = sem("h_hi")
        s.h_lo_p = sem("h_lo_p")
        s.h_lo_v = sem("h_lo_v")
        s.w_hi = sem("w_hi")
        s.w_lo_a = sem("w_lo_a")
        s.w_lo_b = sem("w_lo_b")
        s.ffn_prod = sem("ffn_prod")
        s.hid_hi = sem("hid_hi")
        s.hid_split = sem("hid_split")
        s.y_sc_hi = sem("y_sc_hi")
        s.y_sc_lo = sem("y_sc_lo")
        s.u_lo = sem("u_lo")
        s.lru_y_hi = sem("lru_y_hi")
        s.lru_y_lo = sem("lru_y_lo")
        s.att_hi = sem("att_hi")
        s.att_lo = sem("att_lo")
        s.a_hi = sem("a_hi")
        s.a_lo = sem("a_lo")
        s.bn_hi = sem("bn_hi")
        s.bn_lo = sem("bn_lo")
        s.merged_hi = sem("merged_hi")
        s.merged_lo = sem("merged_lo")
        s.cf_sig = sem("cf_sig")
        s.cf_tap = sem("cf_tap")
        s.cf_diag = sem("cf_diag")
        s.cf_pe = sem("cf_pe")
        s.ln_mean = sem("ln_mean")
        s.ln_diff = sem("ln_diff")
        s.ln_sq = sem("ln_sq")
        s.ln_var = sem("ln_var")
        s.ln_std = sem("ln_std")
        s.ln_rstd = sem("ln_rstd")
        s.ln_scaled = sem("ln_scaled")
        s.u_ready = sem("u_ready")
        s.sc_chain = sem("sc_chain")
        s.y_sc = sem("y_sc")
        s.ffn_t0 = sem("ffn_t0")
        s.ffn_tap = sem("ffn_tap")
        s.ffn_silu = sem("ffn_silu")
        s.ffn2_t0 = sem("ffn2_t0")
        s.ffn2_tap = sem("ffn2_tap")
        s.ffn2_silu = sem("ffn2_silu")
        s.lru_t0 = sem("lru_t0")
        s.lru_tap = sem("lru_tap")
        s.lru_r = sem("lru_r")
        s.lru_i = sem("lru_i")
        s.lru_gates = sem("lru_gates")
        s.lru_a = sem("lru_a")
        s.lru_m2 = sem("lru_m2")
        s.lru_mult = sem("lru_mult")
        s.lru_chain = sem("lru_chain")
        s.lru_y = sem("lru_y")
        s.lam_chain = sem("lam_chain")
        s.lam_e = sem("lam_e")
        s.qk_sq = sem("qk_sq")
        s.qk_sum = sem("qk_sum")
        s.qk_std = sem("qk_std")
        s.qk_chain = sem("qk_chain")
        s.at_logits = sem("at_logits")
        s.at_masked = sem("at_masked")
        s.at_max = sem("at_max")
        s.at_exp = sem("at_exp")
        s.at_chain = sem("at_chain")
        s.at_p = sem("at_p")
        s.at_tr = sem("at_tr")
        s.at_pt = sem("at_pt")
        s.at_pv = sem("at_pv")
        s.at_out = sem("at_out")
        s.rope_rot = sem("rope_rot")
        s.rope_chain = sem("rope_chain")
        s.rope_done = sem("rope_done")
        s.dt_abs = sem("dt_abs")
        s.dt_e = sem("dt_e")
        s.dt_chain = sem("dt_chain")
        s.dt_tr = sem("dt_tr")
        s.dt_tok = sem("dt_tok")
        s.xbc_t0 = sem("xbc_t0")
        s.xbc_tap = sem("xbc_tap")
        s.xbc_silu = sem("xbc_silu")
        s.wi_tr = sem("wi_tr")
        s.wi_copied = sem("wi_copied")
        s.ix_mm = sem("ix_mm")
        s.ix_rel = sem("ix_rel")
        s.ix_chain = sem("ix_chain")
        s.da_logits = sem("da_logits")
        s.da_masked = sem("da_masked")
        s.da_max = sem("da_max")
        s.da_exp = sem("da_exp")
        s.da_chain = sem("da_chain")
        s.da_p = sem("da_p")
        s.da_tr = sem("da_tr")
        s.da_pt = sem("da_pt")
        s.da_pv = sem("da_pv")
        s.da_out = sem("da_out")
        s.xt_tr = sem("xt_tr")
        s.xt_copied = sem("xt_copied")
        s.a_exp = sem("a_exp")
        s.cum_hi = sem("cum_hi")
        s.cum_lo = sem("cum_lo")
        s.ident_r = sem("ident_r")
        s.ssd_cb = sem("ssd_cb")
        s.ssd_cbm = sem("ssd_cbm")
        s.ssd_abc = sem("ssd_abc")
        s.ssd_seg = sem("ssd_seg")
        s.ssd_exp = sem("ssd_exp")
        s.ssd_m = sem("ssd_m")
        s.ssd_y = sem("ssd_y")
        s.ssd_raw = sem("ssd_raw")
        s.ssd_ydone = sem("ssd_ydone")
        s.bn_sq = sem("bn_sq")
        s.bn_pre = sem("bn_pre")
        s.bn_sum = sem("bn_sum")
        s.bn_std = sem("bn_std")
        s.bn_chain = sem("bn_chain")
        s.ps_chain = sem("ps_chain")
        s.final = sem("final")
        s.out_written = sem("out_written")
        s.w_landed = [sem(f"w_landed{i}") for i in range(WSLOTS)]
        s.bank_free = [sem(f"bank_free{i}") for i in range(RING)]

        x = sb("x", [P, DC, T])
        h_hi = sb("h_hi", [P, DC, T], F32R)
        h_lo = sb("h_lo", [P, DC, T], F32R)
        sq = sb("sq", [P, DC, T])
        hid_hi = sb("hid_hi", [P, HID, T], F32R)
        hid_lo = sb("hid_lo", [P, HID, T], F32R)
        w_raw = [sb(f"w_raw{i}", [P, KC * 256]) for i in range(WSLOTS)]
        w_hi = [sb(f"w_hi{i}", [P, KC * 256], F32R) for i in range(WSLOTS)]
        w_lo = [sb(f"w_lo{i}", [P, KC * 256], F32R) for i in range(WSLOTS)]
        arena = sb("arena", [P, 74 * T])
        par = sb("par", [P, NPARAM, 1])
        cst = sb("cst", [P, NCONST])
        std = sb("std", [P, 2, 2 * T])
        eps = sb("eps", [P, 1])
        acc = sb("acc", [P, 2, 2, T])
        sil = std[:, :, T:2 * T]
        score = arena[:, 57 * T:65 * T].rearrange("p (b n) -> p b n", b=2)
        cum_hi = sb("cum_hi", [SH, T], F32R)
        cum_lo = sb("cum_lo", [SH, T], F32R)
        ident_r = sb("ident_r", [SH, SH], F32R)
        dt_tok_sb = sb("dt_tok_sb", [P, 4 * SH])
        dt_tok = dt_tok_sb[:, :].rearrange("p (i t h) -> p i t h", i=2, t=2)
        small = sb("small", [P, 64])
        sqf = sq[:, :, :].rearrange("p c t -> p (c t)")

        lin = [psum(f"lin{i}", [P, 2, T]) for i in range(RING)]
        stat = psum("stat", [P, 2 * T])
        logit = psum("logit", [P, 4, T])
        tr = psum("tr", [P, 2 * T])

        def cut(at, chunks):
            return arena[:, at * T:(at + chunks) * T].rearrange("p (c t) -> p c t", t=T)

        gx = cut(0, 8)
        zz = cut(36, 8).rearrange("p (b c) t -> p b c t", b=4)
        prod = cut(34, 2)
        pt = sq[:, 0:4, :].rearrange("p (b c) t -> p b (c t)", b=2)

        u_pad = arena[:, 0:NC4 * (T + 30)].rearrange("p (c t) -> p c t", c=NC4)
        t_pad = arena[:, 5 * T:5 * T + NC4 * (T + 2)].rearrange("p (c t) -> p c t", c=NC4)
        cf_acc, sc_c, sc_x, sc_b, diff, sc_acc = (cut(10 + 4 * i, 4) for i in range(6))
        cf_diag = arena[:, 44 * T:44 * T + 2 * CF_PE_TAPS * P].rearrange("p (k c n) -> p k c n", c=2, n=P)
        lru_xc, lru_gate, lru_r, lru_i, lru_a, lru_th, lru_m, lru_hs = (cut(4 * i, 4) for i in range(8))
        qn, kn = cut(32, 6), cut(38, 6)
        vt = arena[:, 44 * T:50 * T].rearrange("p (t n) -> p t n", t=2)
        qk_sq = cut(50, 4).rearrange("p (b c) t -> p b (c t)", b=2)
        pt1 = (sqf[:, 0:6 * P], arena[:, 54 * T:57 * T])
        gate_w = arena[:, 65 * T:69 * T].rearrange("p (c n) -> p c n", n=P)
        dil = arena[:, 69 * T:69 * T + NDIL]
        q2, k2, v2, qi2, ki2 = cut(0, 8), cut(8, 2), cut(10, 2), cut(12, 4), cut(16, 1)
        xbc = cut(17, XBC_CH)
        zs = cut(41, XCH)
        ix_rel = zs.rearrange("p (b c) t -> p b c t", b=4)
        xtok = [[arena[:, at * T:(at + 2) * T] for at in tile_at] for tile_at in ((12, 14, 8, 10), (57, 59, 61, 63))]
        gates = arena[:, 17 * T:33 * T].rearrange("p (m g t) -> p m g t", g=2, t=T)
        merged = cut(57, 8)
        ix_sc, ix_w = cut(65, 1), cut(66, 2)
        sel = cut(69, 2)
        dtb = cut(71, 3)
        m_buf = arena[:, 0:6 * T].rearrange("p (b c) -> p b c", b=4)
        cbm = arena[:, 6 * T:6 * T + T + P]
        rope_raw = sq[:, 0:4, :].rearrange("p (b c) t -> p b c t", b=2)
        rope_t = sq[:, 4:8, :].rearrange("p (b c) t -> p b c t", b=2)
        dscr = sq[:, 4:8, :]
        da_score = (sq[:, 4:8, :], cut(65, 4))
        seg = sqf[:, 0:3 * T].rearrange("p (b c) -> p b c", b=2)
        seg_e = sqf[:, 3 * T:6 * T].rearrange("p (b c) -> p b c", b=2)
        y_raw = sq[:, 6:8, :]

        ident = cst[:, CCOL["ident"]:CCOL["ident"] + P]

        def const(name, n=P):
            return cst[:, CCOL[name]:CCOL[name] + n]

        def pcol(name, n=0):
            return par[:, PCOL[name] + n, :]

        def pcol2(l, name, n=0):
            return par[:, P_FIRST + PCOL2[name] + l * P_LAYER + n, :]

        def slab_at(stage, n, l=None):
            return Slab(s, AT[stage] + n if l is None else AT2[stage] + l * PER_LAYER + n, 0)

        def slabs(eng, stage, body, l=None, peel=0):
            each_slab(s, eng, slab_at(stage, 0, l).number, COUNT[stage], 0, body, peel)

        def straight(stage, body, l=None):
            for n in range(COUNT[stage]):
                body(slab_at(stage, n, l), n, n % RING)

        at_bank = [lin[slab_at("od_out", n).bank] for n in (2, 3)]
        XT_ORDER = ((1, 0), (0, 0), (1, 1), (0, 1), (1, 2), (1, 3), (0, 2), (0, 3))
        half_slab = KC * 256 // 2

        def split_lo(eng, slab, half):
            if slab is None:
                return
            slab.wait_hi(eng, half)
            part = slice(half * half_slab, (half + 1) * half_slab)
            eng.tensor_tensor(w_lo[slab.slot][:, part], w_raw[slab.slot][:, part], w_hi[slab.slot][:, part].bitcast(F32),
                              ALU.subtract).then_inc((s.w_lo_a, s.w_lo_b)[half], 1)

        def take_over(eng, stage, l=None):
            eng.wait_ge(s.w_lo_b, slab_at(stage, 0, l).ahead().number)

        def lo_part(eng, lo, whole, hi):
            return eng.tensor_tensor(lo, whole, hi.bitcast(F32), ALU.subtract)

        MERGED = (8, 9, 10, 11, 12, 13, 0, 1)
        ffn_number = {"0": 0, "1": 1}

        def stage_ffn(f, l):
            return ("", FC * (2 + l)) if l is not None else (str(f), FC * ffn_number[str(f)])

        def stage_released(eng, stage, l=None):
            for n in range(max(0, COUNT[stage] - RING), COUNT[stage]):
                slab_at(stage, n, l).wait_released(eng)

        block = ctx.enter_context(nc.Block())

        @block.sync
        def _(sp):
            def stream(stage, l=None):
                width = WIDTH.get(stage, KC * 256)

                def body(slab, n, j):
                    slab.wait_raw_free(sp)
                    at = n if l is None else l * COUNT[stage] + n
                    sp.dma_start(w_raw[slab.slot][:, 0:width], dram[stage][at, :, :])\
                        .then_inc(s.w_landed[slab.slot], 16)
                slabs(sp, stage, body, l)

            for j in range(4):
                sp.dma_start(x[:, 2 * j:2 * j + 2, :], dram["x"][:, 2 * j:2 * j + 2, :]).then_inc(s.x_loaded[j], 16)
            for stage, _n in FIRST:
                stream(stage)
            for l in range(2):
                for stage, _n in SECOND:
                    stream(stage, l)
            for half in range(2):
                sp.wait_ge(s.final, half + 1)
                part = slice(half * DC // 2, (half + 1) * DC // 2)
                sp.dma_start(dram["result"][:, part, :], sq[:, part, :]).then_inc(s.out_written, 16)
            sp.wait_ge(s.out_written, 32)

        @block.gpsimd
        def _(pool):
            def norm_lo(n, chunks, whole):
                for c in chunks:
                    pool.wait_ge(s.h_hi, DC * n + c + 1)
                    pool.wait_ge(s.h_f32, DC * n + c + 1)
                    lo_part(pool, h_lo[:, c, :], whole[:, c, :], h_hi[:, c, :]).then_inc(s.h_lo_p, 1)

            def add_squares(n, j):
                pool.wait_ge(s.norm_sq, 4 * n + j + 1)
                if j == 2:
                    pool.wait_ge(s.norm_pre, 2 * n + 1)
                pool.tensor_tensor(sq[:, 0:2, :], sq[:, 0:2, :], sq[:, 2 * j:2 * j + 2, :], ALU.add).then_inc(s.norm_pre, 1)

            def residual(stage, n, l=None):
                mixer = stage[:3] != "dnB"
                for k in range(COUNT[stage]):
                    j = k - (COUNT[stage] - 4)
                    if mixer:
                        split_lo(pool, slab_at(stage, k, l).ahead(), 0)
                        if j < 2:
                            norm_lo(n, (2 * j, 2 * j + 1), gx)
                    if j == 2:
                        add_squares(n, 1)
                        add_squares(n, 2)
                    if not mixer:
                        if j == 3 and n < 8:
                            norm_lo(n, range(DC // 2), sq)
                        split_lo(pool, slab_at(stage, k, l).ahead(), 0)

            def weights(stage, l=None, both=False):
                def body(slab, n, j):
                    split_lo(pool, slab.ahead(), 0)
                    if both:
                        split_lo(pool, slab.ahead(), 1)
                if both:
                    take_over(pool, stage, l)
                slabs(pool, stage, body, l)

            def ffn(f, n, l=None):
                sfx, base = stage_ffn(f, l)

                def up(off):
                    def body(slab, n, j):
                        split_lo(pool, slab.ahead(), 0)
                        pool.wait_ge(s.ffn_prod, base + off + n + 1)
                        slot = n
                        pool.tensor_copy(hid_hi[:, slot, :], prod[:, j % 2, :]).then_inc(s.hid_hi, 1)
                        pool.wait_ge(s.hid_hi, base + off + n + 1)
                        lo_part(pool, hid_lo[:, slot, :], prod[:, j % 2, :], hid_hi[:, slot, :]).then_inc(s.hid_split, 1)
                    return body
                slabs(pool, "upA" + sfx, up(0), l)
                weights("dnA" + sfx, l)
                slabs(pool, "upB" + sfx, up(UP_A), l)
                residual("dnB" + sfx, n, l)

            nc.gpsimd.memset(eps[:, :], EPS)
            nc.gpsimd.memset(u_pad[:, :, 0:CF_TAPS - 1], 0.0)
            nc.gpsimd.memset(t_pad[:, :, 0:SC_TAPS - 1], 0.0).then_inc(s.pads, 1)
            for b in range(2):
                nc.gpsimd.memset(prod[:, b, :], 0.0).then_inc(s.hid_split, 1)
            add_squares(0, 1)
            add_squares(0, 2)
            for n in range(WSLOTS):
                split_lo(pool, Slab(s, n, 0), 0)
            norm_lo(0, range(DC // 2), sq)
            for stage in ("ev_cf", "ev_sc", "ev_b"):
                weights(stage, both=True)
            residual("ev_out", 1)
            ffn(0, 2)
            weights("od_lru")
            weights("od_qk", both=True)
            weights("od_v", both=True)
            residual("od_out", 3)
            ffn(1, 4)
            for l in range(2):
                weights("kidtwi", l, both=True)
                weights("qi", l, both=True)
                for stage in ("k", "q", "v", "xbc"):
                    weights(stage, l)
                pool.wait_ge(s.cum_hi, l + 1)
                lo_part(pool, cum_lo[:, :], dtb[0:SH, 2, :], cum_hi[:, :]).then_inc(s.cum_lo, 1)
                for u in range(4):
                    split_lo(pool, slab_at("z", 2 * u, l).ahead(), 0)
                    split_lo(pool, slab_at("z", 2 * u + 1, l).ahead(), 0)
                    t, kv = u // 2, u % 2
                    out = (slice(None), slice(kv * QPK, (kv + 1) * QPK), slice(t * P, t * P + P))
                    raw = acc[:, u % 2, :, :].rearrange("p c (a b) -> p (c a) b", b=P)
                    pool.wait_ge(s.da_out, 4 * l + u + 1)
                    pool.tensor_copy(hid_hi[out], raw).then_inc(s.a_hi, 1)
                    pool.wait_ge(s.a_hi, 4 * l + u + 1)
                    lo_part(pool, hid_lo[out], raw, hid_hi[out]).then_inc(s.a_lo, 1)
                def ssd_gate(c, j):
                    pool.wait_ge(s.ssd_raw, XCH * l + c + 1)
                    pool.tensor_tensor(zs[:, c, :], y_raw[:, j % 2, :], zs[:, c, :], ALU.mult).then_inc(s.ssd_ydone, 1)

                def gates_weights(slab, n, j):
                    if not (isinstance(n, int) and n == 0):
                        ssd_gate(2 * n - 1, 1)
                    ssd_gate(2 * n, 0)
                    split_lo(pool, slab.ahead(), 0)
                    split_lo(pool, slab.ahead(), 1)
                take_over(pool, "gates", l)
                slabs(pool, "gates", gates_weights, l, 1)

                def bn_add(g):
                    pool.wait_ge(s.bn_sq, SG * l + g + 1)
                    at = 4 * (g % 2)
                    pool.tensor_tensor(sq[:, at:at + 2, :], sq[:, at:at + 2, :], sq[:, at + 2:at + 4, :], ALU.add)\
                        .then_inc(s.bn_pre, 1)

                bn_add(0)
                bn_add(1)
                for g in range(SG):
                    split_lo(pool, slab_at("pa", g, l).ahead(), 0)
                    if g + 2 < SG:
                        bn_add(g + 2)
                weights("ps", l)
                residual("out", 5 + 2 * l, l)
                ffn(None, 6 + 2 * l, l)

        @block.tensor
        def _(pe):
            def passes(out, lhs, rhs, first, last):
                nc.tensor.matmul(out, lhs[0], rhs[0], start=first, stop=False)
                nc.tensor.matmul(out, lhs[0], rhs[1], start=False, stop=False)
                return nc.tensor.matmul(out, lhs[1], rhs[0], start=False, stop=last)

            def operand(pair, chunks=range(KC)):
                return [(pair[0][:, c, :], pair[1][:, c, :]) for c in chunks]

            h_op = operand((h_hi, h_lo))
            hid = (hid_hi, hid_lo)

            def slab_products(slab, rhs, waits=(None, None)):
                slab.wait_split(pe)
                slab.wait_bank_free(pe)
                wait_chunk, wait_rest = waits
                for half in range(2):
                    out = lin[slab.bank][:, half, :]
                    w = [tuple(part[slab.slot][:, k * 256 + half * P:k * 256 + half * P + P] for part in (w_hi, w_lo))
                         for k in range(len(rhs))]
                    last = len(rhs) - 1
                    if half == 0 and wait_rest is not None:
                        for k, chunk in enumerate(rhs):
                            wait_chunk(k)
                            nc.tensor.matmul(out, w[k][0], chunk[0], start=(k == 0), stop=False)
                            nc.tensor.matmul(out, w[k][1], chunk[0], start=False, stop=False)
                        for k, chunk in enumerate(rhs):
                            wait_rest(k)
                            mm = nc.tensor.matmul(out, w[k][0], chunk[1], start=False, stop=(k == last))
                    else:
                        for k, chunk in enumerate(rhs):
                            if half == 0 and wait_chunk is not None:
                                wait_chunk(k)
                            mm = passes(out, w[k], chunk, k == 0, k == last)
                mm.then_inc(s.lin_done, 1)

            def slab_tokens(slab):
                slab.wait_split(pe)
                slab.wait_bank_free(pe)
                for t in range(2):
                    for k in range(KC):
                        tokens = tuple(part[:, k, t * P:t * P + P] for part in (h_hi, h_lo))
                        cols = slice(k * 256, (k + 1) * 256)
                        mm = passes(lin[slab.bank][:, t, :], tokens, (w_hi[slab.slot][:, cols], w_lo[slab.slot][:, cols]),
                                    k == 0, k == KC - 1)
                mm.then_inc(s.lin_done, 1)

            no_waits = (None, None)

            def products(stage, rhs, l=None, waits=no_waits):
                slabs(pe, stage, lambda slab, n, j: slab_products(slab, rhs, waits if isinstance(n, int) and n == 0 else no_waits),
                      l, 0 if waits is no_waits else 1)

            def norm_mean(n):
                for k in (0, 1, 6, 7):
                    if k == 0:
                        pe.wait_ge(s.norm_pre, 2 * n + 2)
                    if k == 6:
                        pe.wait_ge(s.norm_sq, 4 * n + 4)
                    mm = nc.tensor.matmul(stat[:, 0:T], const("mean1024"), sq[:, k, :], start=(k == 0), stop=(k == DC - 1))
                mm.then_inc(s.norm_sum, 1)

            def late_products(slab_list, rhs, early, wait_chunk):
                last = len(rhs) - 1
                for slab in slab_list:
                    slab.wait_split(pe)
                    slab.wait_bank_free(pe)
                    for part in ((range(early),) if len(slab_list) > 1 else (range(early), range(early, last + 1))):
                        late_part(slab, rhs, part, last, wait_chunk)
                if len(slab_list) > 1:
                    for slab in slab_list:
                        late_part(slab, rhs, range(early, last + 1), last, wait_chunk)

            def late_part(slab, rhs, chunks, last, wait_chunk, halves=(0, 1)):
                for half in halves:
                    for k in chunks:
                        if half == 0:
                            wait_chunk(k)
                        w = tuple(part[slab.slot][:, k * 256 + half * P:k * 256 + half * P + P] for part in (w_hi, w_lo))
                        mm = passes(lin[slab.bank][:, half, :], w, rhs[k], k == 0 and half == 0, k == last and half == 1)
                if last in chunks:
                    mm.then_inc(s.lin_done, 1)

            def closing(slab_list, rhs, n, waits=no_waits):
                for j, slab in enumerate(slab_list):
                    slab_products(slab, rhs, waits if j == 0 else no_waits)
                if n is not None:
                    norm_mean(n)

            def normed(n):
                def wait_hi(k):
                    pe.wait_ge(s.h_hi, DC * n + k + 1)

                def wait_lo(k):
                    half = DC // 2
                    if k < half:
                        pe.wait_ge(s.h_lo_p, half * n + k + 1)
                    else:
                        pe.wait_ge(s.h_lo_v, half * n + k - half + 1)
                return wait_hi, wait_lo

            def ffn(f, n, l=None):
                sfx, base = stage_ffn(f, l)
                ups = 2 + base

                def up(slab, k, j):
                    if not (isinstance(k, int) and k == 0):
                        slab_products(slab, h_op)
                        return
                    wait_hi, wait_lo = normed(n)

                    def wait_chunk(c):
                        wait_hi(c)
                        wait_lo(c)
                    late_products([slab], h_op, DC - 2, wait_chunk)
                    norm_mean(n)
                slabs(pe, "upA" + sfx, up, l, 1)

                def group(g, stage, at):
                    c0, chunks = DOWN_GROUPS[g]
                    rhs = operand(hid, [c % HID for c in range(c0, c0 + chunks)])
                    return [slab_at(stage + sfx, at + j, l) for j in range(4)], rhs, \
                        (lambda k: pe.wait_ge(s.hid_split, ups + c0 + k + 1), None)

                slab_list, rhs, waits = group(0, "dnA", 0)
                for j, slab in enumerate(slab_list):
                    slab_products(slab, rhs, waits if j == 0 else no_waits)
                products("upB" + sfx, h_op, l)
                slab_list, rhs, waits = group(1, "dnB", 0)
                for j, slab in enumerate(slab_list):
                    slab_products(slab, rhs, waits if j == 0 else no_waits)
                slab_list, rhs, waits = group(2, "dnB", 4)
                closing(slab_list, rhs, n + 1, waits)

            pe.wait_ge(s.loaded, 32)
            norm_mean(0)
            products("ev_cf", h_op, waits=normed(0))
            products("ev_sc", h_op)
            products("ev_b", h_op)
            pe.wait_ge(s.loaded_later, 64)
            stage_released(pe, "ev_cf")
            pe.wait_ge(s.cf_diag, CF_PE_TAPS)
            for c in range(2):
                for k in range(CF_PE_TAPS):
                    mm = nc.tensor.matmul(logit[:, c, :], cf_diag[:, k, c, :], u_pad[:, 2 + c, k:k + T],
                                          start=(k == 0), stop=(k == CF_PE_TAPS - 1))
            mm.then_inc(s.cf_pe, 1)
            for k in range(NC4):
                if k % 2 == 0:
                    pe.wait_ge(s.cf_tap, 2 * CF_TAPS if k == 0 else CF_SUMS)
                mm = nc.tensor.matmul(stat[:, 0:T], const("mean512"), cf_acc[:, k, :],
                                      start=(k == 0), stop=(k == NC4 - 1))
            mm.then_inc(s.ln_mean, 1)
            pe.wait_ge(s.ln_sq, 1)
            for k in range(NC4):
                mm = nc.tensor.matmul(stat[:, T:2 * T], const("mean512"), sq[:, k, :],
                                      start=(k == 0), stop=(k == NC4 - 1))
            mm.then_inc(s.ln_var, 1)
            late_products([slab_at("ev_out", 0)], operand(hid), NC4,
                          lambda k: pe.wait_ge(s.y_sc_lo if k < NC4 else s.u_lo, 1))
            closing([slab_at("ev_out", j) for j in range(1, 4)], operand(hid), None)
            ffn(0, 1)

            products("od_lru", h_op, waits=normed(2))

            def qk_mean(n):
                pe.wait_ge(s.qk_sq, n + 1)
                if n >= 1:
                    pe.wait_ge(s.qk_std, n)
                nc.tensor.matmul(stat[:, :], const("mean64"), qk_sq[:, n % 2, :],
                                 start=True, stop=True).then_inc(s.qk_sum, 1)

            def lru_gate(i):
                for c in range(NC4):
                    mm = nc.tensor.matmul(logit[:, c, :], gate_w[:, i * NC4 + c, :], lru_xc[:, c, :], start=True, stop=True)
                mm.then_inc(s.lru_gates, 1)

            for n in range(COUNT["od_qk"]):
                slab_products(slab_at("od_qk", n), h_op)
                if n >= 1:
                    qk_mean(n - 1)
                if n == 1:
                    stage_released(pe, "od_lru")
                    lru_gate(0)
                if n == 3:
                    pe.wait_ge(s.lru_r, 1)
                    lru_gate(1)

            out_0, out_operand, OUT_LAST = slab_at("od_out", 0), operand(hid, range(6)), 5

            def wait_out_chunk(k):
                pe.wait_ge(s.lru_y_lo if k < NC4 else s.att_lo, 1)

            def at_logits(u):
                head, t = u // 2, u % 2
                lo = 64 * (head % 2)
                if u >= 1:
                    pe.wait_ge(s.at_masked, u)
                for g in range(DIL_G):
                    c = (g * DIL_H + head) // 2
                    mm = nc.tensor.matmul(logit[:, g, 0:(t + 1) * P], qn[lo:lo + 64, c, t * P:t * P + P],
                                          kn[lo:lo + 64, c, 0:(t + 1) * P], start=True, stop=True)
                mm.then_inc(s.at_logits, 1)

            slab_tokens(slab_at("od_v", 0))
            qk_mean(COUNT["od_qk"] - 1)
            slab_tokens(slab_at("od_v", 1))
            pe.wait_ge(s.lru_i, 1)
            stage_released(pe, "od_qk")
            at_logits(0)
            slab_tokens(slab_at("od_v", 2))
            at_logits(1)
            stage_released(pe, "od_v")
            for u in range(2 * DIL_H):
                head, t = u // 2, u % 2
                lo = 64 * (head % 2)
                nb = DIL_G * (t + 1)
                if u + 2 < 2 * DIL_H:
                    at_logits(u + 2)
                if 1 <= u <= 4:
                    if u == 1:
                        out_0.wait_split(pe)
                        out_0.wait_bank_free(pe)
                    half, k = (u - 1) // 2, (u - 1) % 2 * (NC4 // 2)
                    late_part(out_0, out_operand, range(k, k + NC4 // 2), OUT_LAST, wait_out_chunk, (half,))
                pe.wait_ge(s.at_p, u + 1)
                if u == 0:
                    pe.wait_ge(s.qk_std, COUNT["od_qk"])
                for b in range(nb):
                    where = tr[:, b * P:b * P + P] if b < 4 else stat[:, T + (b - 4) * P:T + (b - 3) * P]
                    g, st = b // (t + 1), b % (t + 1)
                    at = g * (t + 1) * P + st * P
                    mm = nc.tensor.transpose(where, score[:, u % 2, at:at + P], ident)
                mm.then_inc(s.at_tr, 1)
                pe.wait_ge(s.at_pt, u + 1)
                if u >= 2:
                    pe.wait_ge(s.at_out, u - 1)
                for b in range(nb):
                    g, st = b // (t + 1), b % (t + 1)
                    v_at = (g * DIL_H + head) * DIL_D
                    mm = nc.tensor.matmul(at_bank[u % 2][lo:lo + 64, 0, 0:P], vt[:, st, v_at:v_at + DIL_D],
                                          pt1[u % 2][:, b * P:b * P + P], start=(b == 0), stop=(b == nb - 1))
                mm.then_inc(s.at_pv, 1)
            late_part(out_0, out_operand, range(NC4, OUT_LAST + 1), OUT_LAST, wait_out_chunk)
            closing([slab_at("od_out", j) for j in range(1, 4)], out_operand, None)
            ffn(1, 3)

            def layer(l):
                rope_unit = [0]

                def swap(which, n, stage, at=0):
                    r = rope_unit[0]
                    rope_unit[0] += 1
                    slab_at(stage, at, l).wait_released(pe)
                    if r >= 1:
                        pe.wait_ge(s.rope_done, 8 * l + r)
                    nc.tensor.matmul(stat[:, 0:n], const(which),
                                     rope_raw[:, r % 2, :, :].rearrange("p c t -> p (c t)")[:, 0:n],
                                     start=True, stop=True).then_inc(s.rope_rot, 1)

                products("kidtwi", h_op, l, normed(4 + 2 * l))

                def index_products(b):
                    t, half = b // 2, b % 2
                    if b >= 1:
                        pe.wait_ge(s.ix_rel, 4 * l + b)
                    for i in range(4):
                        head = 4 * half + i
                        lo = 64 * (head % 2)
                        mm = nc.tensor.matmul(logit[:, 2 * (i % 2) + i // 2, 0:(t + 1) * P],
                                              qi2[lo:lo + 64, head // 2, t * P:t * P + P],
                                              ki2[lo:lo + 64, 0, 0:(t + 1) * P], start=True, stop=True)
                    mm.then_inc(s.ix_mm, 1)

                slab_products(slab_at("qi", 0, l), h_op)
                swap("swap_idx", T, "kidtwi")
                for t in range(2):
                    mm = nc.tensor.transpose(tr[:, t * IH:(t + 1) * IH], dscr[SH:SH + IH, 2, t * P:t * P + P],
                                             ident[SH:SH + IH, SH:SH + IH])
                mm.then_inc(s.wi_tr, 1)
                slab_products(slab_at("qi", 1, l), h_op)
                swap("swap_idx", 2 * T, "qi", 0)
                slab_products(slab_at("k", 0, l), h_op)
                swap("swap_idx", 2 * T, "qi", 1)
                for n in range(4):
                    slab_products(slab_at("q", n, l), h_op)
                    if n == 0:
                        swap("swap_attn", 2 * T, "k")
                    else:
                        swap("swap_attn", 2 * T, "q", n - 1)
                    index_products(n)
                slab_tokens(slab_at("v", 0, l))
                swap("swap_attn", 2 * T, "q", 3)

                def da_logits(u):
                    t, kv = u // 2, u % 2
                    n = (t + 1) * P
                    for i in range(QPK):
                        mm = nc.tensor.matmul(logit[:, i, 0:n], q2[:, kv * QPK + i, t * P:t * P + P],
                                              k2[:, kv, 0:n], start=True, stop=True)
                    mm.then_inc(s.da_logits, 1)

                def dt_by_token():
                    pe.wait_ge(s.dt_chain, DT_LINKS * (l + 1))
                    pe.wait_ge(s.wi_copied, l + 1)
                    for i, row in enumerate((0, 2)):
                        for t in range(2):
                            mm = nc.tensor.transpose(tr[:, (2 * i + t) * SH:(2 * i + t + 1) * SH],
                                                     dtb[0:SH, row, t * P:t * P + P], ident[0:SH, 0:SH])
                    mm.then_inc(s.dt_tr, 1)

                def xbc_slab(slab, n, j):
                    slab_products(slab, h_op)
                    if isinstance(n, int) and n == 0:
                        dt_by_token()
                        pe.wait_ge(s.rope_done, 8 * l + 8)
                        pe.wait_ge(s.ix_rel, 4 * l + 4)
                        da_logits(0)
                slabs(pe, "xbc", xbc_slab, l, 1)

                def by_token(b):
                    t, quarter = XT_ORDER[b]
                    if b == 0:
                        pe.wait_ge(s.xbc_silu, 12 * (l + 1))
                    else:
                        pe.wait_ge(s.xt_copied, 8 * l + b)
                    for i in range(4):
                        mm = nc.tensor.transpose(stat[:, i * P:i * P + P], xbc[:, 4 * quarter + i, t * P:t * P + P], ident)
                    mm.then_inc(s.xt_tr, 1)

                for u in range(4):
                    t, kv = u // 2, u % 2
                    if u < 3:
                        pe.wait_ge(s.da_masked, 4 * l + u + 1)
                        da_logits(u + 1)
                    pe.wait_ge(s.da_p, 4 * l + u + 1)
                    if u == 0:
                        pe.wait_ge(s.dt_tok, l + 1)
                    else:
                        pe.wait_ge(s.da_out, 4 * l + u)
                    if t == 1:
                        pe.wait_ge(s.xt_copied, 8 * l + 2 * u)
                    for st in range(t + 1):
                        for i in range(QPK):
                            mm = nc.tensor.transpose((tr, stat)[st][:, i * P:i * P + P],
                                                     da_score[u % 2][:, i, st * P:st * P + P], ident)
                    mm.then_inc(s.da_tr, 1)
                    slab_products(slab_at("z", 2 * u, l), h_op)
                    pe.wait_ge(s.da_pt, 6 * l + (1, 2, 4, 6)[u])
                    for st in range(t + 1):
                        mm = nc.tensor.matmul(tr[:, :], v2[:, st, kv * P:kv * P + P], pt[:, st, 0:4 * P],
                                              start=(st == 0), stop=(st == t))
                    mm.then_inc(s.da_pv, 1)
                    by_token(2 * u)
                    slab_products(slab_at("z", 2 * u + 1, l), h_op)
                    by_token(2 * u + 1)

                def running_sums(c):
                    if c >= 2:
                        pe.wait_ge(s.ssd_seg, SH * l + 2 * c - 2)
                    for i in range(2):
                        head = ident_r[:, 2 * c + i:2 * c + i + 1].to_broadcast([SH, P])
                        out = logit[:, 2 * (c % 2) + i, :]
                        nc.tensor.matmul(out, head, cum_hi[:, :], start=True, stop=False)
                        mm = nc.tensor.matmul(out, head, cum_lo[:, :], start=False, stop=True)
                    mm.then_inc(s.ssd_abc, 1)

                pe.wait_ge(s.ident_r, 1)
                pe.wait_ge(s.cum_lo, l + 1)
                running_sums(0)
                pe.wait_ge(s.da_out, 4 * l + 4)
                for c in range(XCH):
                    where = (tr, stat)[c % 2]

                    def bank_read():
                        if c >= 2:
                            pe.wait_ge(s.ssd_raw, XCH * l + c - 1)
                    if c % 4 == 0:
                        g = c // 4
                        bank_read()
                        nc.tensor.matmul(where[:, 0:T], xbc[:, XCH + g, 0:P], xbc[:, XCH + SG + g, :],
                                         start=True, stop=True)
                        nc.tensor.matmul(where[:, T:T + P], xbc[:, XCH + g, P:T], xbc[:, XCH + SG + g, P:T],
                                         start=True, stop=True).then_inc(s.ssd_cb, 1)
                    if c + 1 < XCH:
                        running_sums(c + 1)
                    if c % 2 == 0:
                        slab_products(slab_at("gates", c // 2, l), h_op)
                    if c == 0:
                        pe.wait_ge(s.xt_copied, 8 * l + 8)
                    bank_read()
                    for head in (2 * c, 2 * c + 1):
                        lo = 64 * (head % 2)
                        pe.wait_ge(s.ssd_m, SH * l + head + 1)
                        by_tok = [xtok[t][head // 8][:, head % 8 * 64:head % 8 * 64 + 64] for t in range(2)]
                        nc.tensor.matmul(where[lo:lo + 64, 0:T], by_tok[0], m_buf[:, head % 4, 0:T], start=True, stop=False)
                        mm = nc.tensor.matmul(where[lo:lo + 64, P:T], by_tok[1], m_buf[:, head % 4, T:T + P],
                                              start=False, stop=True)
                    mm.then_inc(s.ssd_y, 1)
                pe.wait_ge(s.a_lo, 4 * (l + 1))
                for g in range(SG):
                    slab_products(slab_at("pa", g, l), operand(hid))
                    pe.wait_ge(s.bn_pre, SG * l + g + 1)
                    for k in range(2):
                        mm = nc.tensor.matmul((tr, stat)[g % 2][:, 0:T], const("mean512"),
                                              sq[:, 4 * (g % 2) + k, :], start=(k == 0), stop=(k == 1))
                    mm.then_inc(s.bn_sum, 1)
                for n in range(8):
                    slab_products(slab_at("ps", n, l), (h_op, operand(hid))[n // 4],
                                  (lambda k: pe.wait_ge(s.bn_lo, SG * l + 2 * (n // 4) + k // 4 + 1), None)
                                  if n % 4 == 0 else no_waits)
                late_products([slab_at("out", 0, l)], operand(hid, MERGED), DC - 2,
                              lambda k: pe.wait_ge(s.merged_lo, 4 * l + k // 2 + 1))
                closing([slab_at("out", j, l) for j in range(1, 4)], operand(hid, MERGED), None)
                ffn(None, 5 + 2 * l, l)

            for l in range(2):
                layer(l)

        @block.scalar
        def _(act):
            def weights_hi(slab):
                if slab is None:
                    return
                slab.wait_landed(act)
                for half in range(2):
                    part = slice(half * half_slab, (half + 1) * half_slab)
                    nc.scalar.activation(w_hi[slab.slot][:, part], w_raw[slab.slot][:, part], ACT.Copy).then_inc(s.w_hi, 1)

            def done(slab):
                slab.wait_done(act)
                weights_hi(slab.ahead())

            def square(j):
                nc.scalar.activation(sq[:, 2 * j:2 * j + 2, :], x[:, 2 * j:2 * j + 2, :], ACT.Square).then_inc(s.norm_sq, 1)

            def root_table():
                nc.scalar.activation(small[:, 63:64], eps[:, :], ACT.Sqrt)

            def norm_root(n):
                act.wait_ge(s.norm_sum, n + 1)
                nc.scalar.activation(std[:, 0, 0:T], stat[:, 0:T], ACT.Sqrt, bias=eps[:, :]).then_inc(s.norm_std, 1)

            def norm(n):
                for c in range(DC):
                    act.wait_ge(s.h_f32, DC * n + c + 1)
                    nc.scalar.activation(h_hi[:, c, :], sq[:, c, :], ACT.Copy).then_inc(s.h_hi, 1)

            def residual(stage, n, gain=None, l=None):
                first = COUNT[stage] - 4
                for k in range(COUNT[stage]):
                    slab, j = slab_at(stage, k, l), k - first
                    if j < 2 or (j == 2 and gain is not None):
                        done(slab)
                    if j >= 0:
                        slab.wait_released(act)
                        if gain is not None:
                            for out, ready in ((h_hi, s.h_hi), (gx, s.h_f32)):
                                for c in (2 * j, 2 * j + 1):
                                    nc.scalar.activation(out[:, c, :], x[:, c, :], ACT.Identity, scale=gain(c)).then_inc(ready, 1)
                        square(j)
                    if j == 2 and gain is None:
                        done(slab)
                    if j == 2:
                        root_table()
                if gain is None:
                    norm_root(n)
                    done(slab)
                    if n < 8:
                        norm(n)
                else:
                    done(slab)
                    norm_root(n)

            def ffn(f, n, l=None):
                sfx, base = stage_ffn(f, l)

                def up(off):
                    def body(slab, n, j):
                        b = j % 2
                        done(slab)
                        slab.wait_released(act)
                        c = off + n
                        if l is None:
                            nc.scalar.activation(acc[:, b, 0, :], zz[:, j, 0, :], ACT.Identity,
                                                 bias=pcol(f"fb{f}", c), scale=pcol(f"fw{f}", 2 * FC + c)).then_inc(s.ffn_t0, 1)
                            act.wait_ge(s.ffn_tap, 2 * (base + c) + 2)
                            nc.scalar.activation(sil[:, b, :], acc[:, b, 0, :], ACT.Silu).then_inc(s.ffn_silu, 1)
                        else:
                            for i in range(2):
                                ins = nc.scalar.activation(acc[:, b, i, :], zz[:, j, i, :], ACT.Identity,
                                                           bias=pcol2(l, "fb", i * FC + c),
                                                           scale=pcol2(l, "fw", 2 * 2 * FC + i * FC + c))
                            ins.then_inc(s.ffn2_t0, 1)
                            act.wait_ge(s.ffn2_tap, 4 * (l * FC + c) + 3)
                            nc.scalar.activation(sil[:, b, :], acc[:, b, 0, :], ACT.Silu).then_inc(s.ffn2_silu, 1)
                    return body
                slabs(act, "upA" + sfx, up(0), l)
                straight("dnA" + sfx, lambda slab, k, j: done(slab), l)
                slabs(act, "upB" + sfx, up(UP_A), l)
                residual("dnB" + sfx, n, None, l)

            first, rest = slice(CCOL["mean1024"], CCOL["mean1024"] + P), slice(CCOL["mean1024"] + P, NCONST)
            assert CCOL["mean1024"] == P
            act.dma_start(cst[:, first], dram["consts"][:, first]).then_inc(s.loaded, 16)
            act.dma_start(par[:, :, :], dram["params"].rearrange("p (n a) -> p n a", a=1)).then_inc(s.loaded, 16)
            act.wait_ge(s.pads, 1)

            root_table()
            for j in range(4):
                act.wait_ge(s.x_loaded[j], 16)
                square(j)
            act.dma_start(cst[:, rest], dram["consts"][:, rest]).then_inc(s.loaded_later, 16)
            act.dma_start(cst[:, 0:P], dram["consts"][:, 0:P]).then_inc(s.loaded_later, 16)
            act.dma_start(gate_w[:, :, :], dram["gate_w"]).then_inc(s.loaded_later, 16)
            act.dma_start(dil, dram["dil"]).then_inc(s.loaded_later, 16)
            act.wait_ge(s.loaded, 32)
            weights_hi(Slab(s, 0, 0))
            norm_root(0)
            norm(0)
            weights_hi(Slab(s, 1, 0))

            def cf_gate(slab, n, j):
                done(slab)
                nc.scalar.activation(sq[:, n, :], lin[slab.bank][:, 1, :], ACT.Sigmoid).then_inc(s.cf_sig, 1)
            slabs(act, "ev_cf", cf_gate)

            def tap_diagonals(taps):
                for k in taps:
                    for c in range(2):
                        ins = nc.scalar.activation(cf_diag[:, k, c, :], ident, ACT.Copy,
                                                   scale=pcol("cf_w", k * NC4 + 2 + c))
                    ins.then_inc(s.cf_diag, 1)
            act.wait_ge(s.loaded_later, 64)
            tap_diagonals(range(CF_PE_TAPS // 2))

            def sc_copy(slab, n, j):
                done(slab)
                nc.scalar.activation(sc_c[:, n, :], lin[slab.bank][:, 0, :], ACT.Copy)
                nc.scalar.activation(sc_x[:, n, :], lin[slab.bank][:, 1, :], ACT.Copy).then_inc(s.bank_free[slab.bank], 1)
            slabs(act, "ev_sc", sc_copy)
            tap_diagonals(range(CF_PE_TAPS // 2, CF_PE_TAPS))

            def b_copy(slab, n, j):
                done(slab)
                nc.scalar.activation(sc_b[:, 2 * n:2 * n + 2, :], lin[slab.bank][:, :, :], ACT.Copy)\
                    .then_inc(s.bank_free[slab.bank], 1)
            slabs(act, "ev_b", b_copy)
            act.wait_ge(s.ln_diff, 1)
            nc.scalar.activation(sq[:, 0:NC4, :], diff[:, :, :], ACT.Square).then_inc(s.ln_sq, 1)
            act.wait_ge(s.ln_var, 1)
            nc.scalar.activation(std[:, 0, 0:T], stat[:, T:2 * T], ACT.Sqrt, bias=eps[:, :]).then_inc(s.ln_std, 1)
            act.wait_ge(s.y_sc, 1)
            nc.scalar.activation(hid_hi[:, 0:NC4, :], sc_acc[:, :, :], ACT.Copy).then_inc(s.y_sc_hi, 1)
            act.wait_ge(s.ln_scaled, 1)
            for c in range(NC4):
                for out in (sq[:, c, :], hid_hi[:, NC4 + c, :]):
                    ins = nc.scalar.activation(out, diff[:, c, :], ACT.Silu, bias=pcol("ln_b", c), scale=pcol("ln_g", c))
            ins.then_inc(s.u_ready, 1)
            residual("ev_out", 1, lambda c: pcol("ffn_g0", c))
            ffn(0, 2)

            act.wait_ge(s.lam_chain, 1)
            nc.scalar.activation(small[:, 8:12], small[:, 4:8], ACT.Exp, scale=-1.0).then_inc(s.lam_e, 1)

            def lru_in(slab, n, j):
                done(slab)
                nc.scalar.activation(lru_gate[:, n, :], lin[slab.bank][:, 1, :], ACT.Gelu_apprx_tanh)
                nc.scalar.activation(lru_xc[:, n, :], lin[slab.bank][:, 0, :], ACT.Identity,
                                     bias=pcol("lru_b", n), scale=pcol("lru_w", 3 * NC4 + n)).then_inc(s.lru_t0, 1)
            slabs(act, "od_lru", lru_in)

            def qk_square(slab, n, j):
                done(slab)
                if n >= 2:
                    act.wait_ge(s.qk_sum, n - 1)
                nc.scalar.activation(qk_sq[:, n % 2, :], lin[slab.bank][:, :, :].rearrange("p c t -> p (c t)"),
                                     ACT.Square).then_inc(s.qk_sq, 1)
                if n >= 1:
                    qk_root(n - 1)

            def qk_root(n):
                act.wait_ge(s.qk_sum, n + 1)
                if n >= 2:
                    slab_at("od_qk", n - 2).wait_released(act)
                nc.scalar.activation(std[:, n % 2, :], stat[:, :], ACT.Sqrt, bias=eps[:, :]).then_inc(s.qk_std, 1)
            for n in range(COUNT["od_qk"]):
                qk_square(slab_at("od_qk", n), n, n % RING)
                if n == 2:
                    act.wait_ge(s.lru_gates, 1)
                    for c in range(NC4):
                        ins = nc.scalar.activation(lru_r[:, c, :], logit[:, c, :], ACT.Sigmoid, bias=pcol("lru_ba", c))
                    ins.then_inc(s.lru_r, 1)
                if n == 4:
                    act.wait_ge(s.lru_gates, 2)
                    for c in range(NC4):
                        ins = nc.scalar.activation(lru_i[:, c, :], logit[:, c, :], ACT.Sigmoid, bias=pcol("lru_bx", c))
                    ins.then_inc(s.lru_i, 1)
                    act.wait_ge(s.lru_r, 1)
                    act.wait_ge(s.lam_chain, LAM_LINKS)
                    for func, out in ((ACT.Tanh, lru_th), (ACT.Exp, lru_a)):
                        for c in range(NC4):
                            ins = nc.scalar.activation(out[:, c, :], lru_r[:, c, :], func, scale=small[:, c:c + 1])
                    ins.then_inc(s.lru_a, 1)

            def v_copy(n):
                slab = slab_at("od_v", n)
                done(slab)
                nc.scalar.activation(vt[:, :, n * 256:(n + 1) * 256], lin[slab.bank][:, :, :], ACT.Copy)\
                    .then_inc(s.bank_free[slab.bank], 1)
            v_copy(0)
            qk_root(COUNT["od_qk"] - 1)
            act.wait_ge(s.lru_m2, 1)
            nc.scalar.activation(lru_th[:, :, :], lru_m[:, :, :], ACT.Sqrt, scale=-1.0).then_inc(s.lru_mult, 1)
            v_copy(1)

            def at_exp(u):
                n = DIL_G * (u % 2 + 1) * P
                act.wait_ge(s.at_max, u + 1)
                nc.scalar.activation(score[:, u % 2, 0:n], score[:, u % 2, 0:n], ACT.Exp,
                                     bias=small[:, 16 + u:17 + u], accum_out=small[:, 24 + u:25 + u]).then_inc(s.at_exp, 1)

            at_exp(0)
            act.wait_ge(s.lru_y, 1)
            nc.scalar.activation(hid_hi[:, 0:NC4, :], lru_hs[:, :, :], ACT.Copy).then_inc(s.lru_y_hi, 1)
            v_copy(2)
            at_exp(1)
            for u in range(2 * DIL_H):
                head, t = u // 2, u % 2
                lo = 64 * (head % 2)
                n = DIL_G * (t + 1) * P
                act.wait_ge(s.at_tr, u + 1)
                first = min(n, 4 * P)
                ins = nc.scalar.activation(pt1[u % 2][:, 0:first], tr[:, 0:first], ACT.Copy)
                if n > first:
                    ins = nc.scalar.activation(pt1[u % 2][:, first:n], stat[:, T:T + n - first], ACT.Copy)
                ins.then_inc(s.at_pt, 1)
                act.wait_ge(s.at_pv, u + 1)
                nc.scalar.activation(acc[lo:lo + 64, 0, head // 2, t * P:t * P + P], at_bank[u % 2][lo:lo + 64, 0, 0:P],
                                     ACT.Copy).then_inc(s.at_out, 1)
                if u + 2 < 2 * DIL_H:
                    at_exp(u + 2)
            act.wait_ge(s.at_out, 2 * DIL_H)
            nc.scalar.activation(hid_hi[:, NC4:NC4 + 2, :], acc[:, 0, :, :], ACT.Copy).then_inc(s.att_hi, 1)
            residual("od_out", 3, lambda c: pcol("ffn_g1", c))
            ffn(1, 4)

            act.wait_ge(s.loaded_later, 64)
            nc.scalar.activation(ident_r[:, :], ident[0:SH, 0:SH], ACT.Copy).then_inc(s.ident_r, 1)

            def layer(l):
                rope_unit = [0]

                def raw_copy(slab, chunks):
                    r = rope_unit[0]
                    rope_unit[0] += 1
                    if r >= 2:
                        act.wait_ge(s.rope_done, 8 * l + r - 1)
                    return nc.scalar.activation(rope_raw[:, r % 2, 0:chunks, :], lin[slab.bank][:, 0:chunks, :], ACT.Copy)

                slab = slab_at("kidtwi", 0, l)
                done(slab)
                raw_copy(slab, 1)
                nc.scalar.activation(dscr[0:SH + IH, 2, :], lin[slab.bank][0:SH + IH, 1, :], ACT.Identity,
                                     bias=pcol2(l, "dt_bias")[0:SH + IH, :]).then_inc(s.bank_free[slab.bank], 1)
                nc.scalar.activation(small[0:SH, 40:41], pcol2(l, "a_log")[0:SH, :], ACT.Exp).then_inc(s.a_exp, 1)
                act.wait_ge(s.dt_abs, l + 1)
                nc.scalar.activation(dscr[0:SH, 3, :], dscr[0:SH, 3, :], ACT.Exp, scale=-1.0).then_inc(s.dt_e, 1)

                def rope_copy(slab):
                    done(slab)
                    raw_copy(slab, 2).then_inc(s.bank_free[slab.bank], 1)

                def rectified(b):
                    n = (b // 2 + 1) * P
                    act.wait_ge(s.ix_mm, 4 * l + b + 1)
                    nc.scalar.activation(ix_rel[:, b, :, 0:n], logit[:, :, 0:n], ACT.Relu).then_inc(s.ix_rel, 1)

                rope_copy(slab_at("qi", 0, l))
                act.wait_ge(s.wi_tr, l + 1)
                nc.scalar.activation(small[:, 42:58], tr[:, 0:2 * IH], ACT.Copy).then_inc(s.wi_copied, 1)
                rope_copy(slab_at("qi", 1, l))
                rope_copy(slab_at("k", 0, l))
                for n in range(4):
                    rope_copy(slab_at("q", n, l))
                    rectified(n)
                slab = slab_at("v", 0, l)
                done(slab)
                nc.scalar.activation(v2[:, :, :], lin[slab.bank][:, :, :], ACT.Copy).then_inc(s.bank_free[slab.bank], 1)
                act.wait_ge(s.dt_tr, l + 1)
                nc.scalar.activation(dt_tok_sb[:, :], tr[:, 0:4 * SH], ACT.Copy).then_inc(s.dt_tok, 1)
                act.wait_ge(s.dt_chain, DT_LINKS * (l + 1))
                nc.scalar.activation(cum_hi[:, :], dtb[0:SH, 2, :], ACT.Copy).then_inc(s.cum_hi, 1)

                def da_exp(u):
                    n = (u // 2 + 1) * P
                    act.wait_ge(s.da_max, 4 * l + u + 1)
                    for i in range(QPK):
                        ins = nc.scalar.activation(da_score[u % 2][:, i, 0:n], da_score[u % 2][:, i, 0:n], ACT.Exp,
                                                   bias=small[:, 16 + i:17 + i], accum_out=small[:, 24 + i:25 + i])
                    ins.then_inc(s.da_exp, 1)

                def xbc_silu(n):
                    slab_at("xbc", n, l).wait_released(act)
                    nc.scalar.activation(xbc[:, 2 * n:2 * n + 2, :], acc[:, n % 2, :, :], ACT.Silu).then_inc(s.xbc_silu, 1)

                def xbc_conv(slab, n, j):
                    done(slab)
                    if n >= 2:
                        act.wait_ge(s.xbc_silu, 12 * l + n - 1)
                    for i in range(2):
                        ins = nc.scalar.activation(acc[:, j % 2, i, :], lin[slab.bank][:, i, :], ACT.Identity,
                                                   bias=pcol2(l, "ssd_b", 2 * n + i),
                                                   scale=pcol2(l, "ssd_w", 3 * XBC_CH + 2 * n + i))
                    ins.then_inc(s.xbc_t0, 1)
                    if n >= 1:
                        xbc_silu(n - 1)
                    if n == 5:
                        da_exp(0)
                straight("xbc", xbc_conv, l)
                xbc_silu(COUNT["xbc"] - 1)

                def z_silu(slab, n):
                    nc.scalar.activation(zs[:, 2 * n:2 * n + 2, :], lin[slab.bank][:, :, :], ACT.Silu)\
                        .then_inc(s.bank_free[slab.bank], 1)

                def by_token(b):
                    t, quarter = XT_ORDER[b]
                    act.wait_ge(s.xt_tr, 8 * l + b + 1)
                    nc.scalar.activation(xtok[t][quarter], stat[:, :], ACT.Copy).then_inc(s.xt_copied, 1)

                for u in range(4):
                    t = u // 2
                    act.wait_ge(s.da_tr, 4 * l + u + 1)
                    for st in range(t + 1):
                        nc.scalar.activation(pt[:, st, 0:4 * P], (tr, stat)[st][:, :], ACT.Copy).then_inc(s.da_pt, 1)
                    if u < 3:
                        da_exp(u + 1)
                    slab = slab_at("z", 2 * u, l)
                    done(slab)
                    z_silu(slab, 2 * u)
                    act.wait_ge(s.da_pv, 4 * l + u + 1)
                    if u >= 2:
                        act.wait_ge(s.a_lo, 4 * l + u - 1)
                    nc.scalar.activation(acc[:, u % 2, :, :], tr[:, :], ACT.Copy).then_inc(s.da_out, 1)
                    by_token(2 * u)
                    slab = slab_at("z", 2 * u + 1, l)
                    slab.wait_done(act)
                    z_silu(slab, 2 * u + 1)
                    by_token(2 * u + 1)
                    weights_hi(slab.ahead())

                def gate_sig(n):
                    act.wait_ge(s.ssd_raw, XCH * l + 2 * n + 2)
                    slab = slab_at("gates", n, l)
                    nc.scalar.activation(gates[:, n, :, :], lin[slab.bank][:, :, :], ACT.Sigmoid)\
                        .then_inc(s.bank_free[slab.bank], 1)

                for m in range(XCH // 2):
                    for head in range(4 * m, 4 * m + 4):
                        i = head % 2
                        act.wait_ge(s.ssd_seg, SH * l + head + 1)
                        nc.scalar.activation(seg_e[:, i, :], seg[:, i, :], ACT.Exp).then_inc(s.ssd_exp, 1)
                    done(slab_at("gates", m, l))
                    if m % 2 == 1:
                        for n in range(max(0, m - 2), m):
                            gate_sig(n)

                def bn_square(g):
                    nc.scalar.activation(sq[:, 4 * (g % 2):4 * (g % 2) + 4, :], zs[:, 4 * g:4 * g + 4, :], ACT.Square)\
                        .then_inc(s.bn_sq, 1)

                def bn_round(g):
                    act.wait_ge(s.bn_chain, 2 * (SG * l + g) + 2)
                    part = h_hi[:, 4 * g:4 * g + 4, :] if g < 2 else hid_hi[:, 4 * g - 8:4 * g - 4, :]
                    nc.scalar.activation(part, zs[:, 4 * g:4 * g + 4, :], ACT.Copy).then_inc(s.bn_hi, 1)

                act.wait_ge(s.ssd_ydone, XCH * (l + 1))
                bn_square(0)
                bn_square(1)
                gate_sig(XCH // 2 - 1)
                for g in range(SG):
                    done(slab_at("pa", g, l))
                    act.wait_ge(s.bn_sum, SG * l + g + 1)
                    if g >= 2:
                        act.wait_ge(s.bn_chain, 2 * (SG * l + g - 1))
                    nc.scalar.activation(std[:, g % 2, 0:T], (tr, stat)[g % 2][:, 0:T], ACT.Sqrt, bias=eps[:, :])\
                        .then_inc(s.bn_std, 1)
                    if g + 2 < SG:
                        bn_square(g + 2)
                    if g in (1, 2):
                        bn_round(g - 1)
                bn_round(2)
                bn_round(3)

                def merge_round(slab, n, j):
                    if n < 6:
                        done(slab)
                    if n >= 4:
                        slab.wait_released(act)
                        at = MERGED[2 * j]
                        nc.scalar.activation(hid_hi[:, at:at + 2, :], merged[:, 2 * j:2 * j + 2, :], ACT.Copy)\
                            .then_inc(s.merged_hi, 1)
                    if n >= 6:
                        done(slab)
                straight("ps", merge_round, l)
                residual("out", 5 + 2 * l, lambda c: pcol2(l, "ffn_g", c), l)
                ffn(None, 6 + 2 * l, l)

            for l in range(2):
                layer(l)

        @block.vector
        def _(dve):
            tt, stt, ts = nc.vector.tensor_tensor, nc.vector.scalar_tensor_tensor, nc.vector.tensor_scalar

            def norm(n, gain, stage=None, l=None):
                norm_root(n)
                for c in range(DC):
                    stt(sq[:, c, :], x[:, c, :], gain(c), std[:, 0, 0:T], ALU.mult, ALU.mult).then_inc(s.h_f32, 1)
                norm_lo(n, range(DC // 2, DC), sq)
                if stage is not None:
                    weights(slab_at(stage, COUNT[stage] - 1, l))

            def weights(slab):
                split_lo(dve, slab.ahead(), 1)

            def softplus(chain, out, arg, mag, e, scratch):
                a, b = scratch
                chain.link(ts(a, e, 2.0, None, ALU.add))
                chain.link(nc.vector.reciprocal(b, a))
                chain.link(tt(e, e, b, ALU.mult))
                chain.link(tt(a, e, e, ALU.mult))
                chain.link(ts(b, a, 1.0 / 15.0, None, ALU.mult))
                for odd in (13, 11, 9, 7, 5, 3):
                    chain.link(stt(b, b, 1.0 / odd, a, ALU.add, ALU.mult))
                chain.link(stt(b, b, 1.0, e, ALU.add, ALU.mult))
                chain.link(ts(a, arg, 0.0, None, ALU.max))
                chain.link(stt(out, b, 2.0, a, ALU.mult, ALU.add))

            def norm_lo(n, chunks, whole):
                for c in chunks:
                    dve.wait_ge(s.h_hi, DC * n + c + 1)
                    dve.wait_ge(s.h_f32, DC * n + c + 1)
                    lo_part(nc.vector, h_lo[:, c, :], whole[:, c, :], h_hi[:, c, :]).then_inc(s.h_lo_v, 1)

            def norm_root(n):
                dve.wait_ge(s.norm_std, n + 1)
                nc.vector.reciprocal(std[:, 0, 0:T], std[:, 0, 0:T]).then_inc(s.norm_rstd, 1)
                dve.wait_ge(s.norm_rstd, n + 1)

            def add_residual(stage, l=None, n=None):
                pairs = x[:, :, :].rearrange("p (j i) t -> p j i t", i=2)
                late = 2 if stage[:3] != "dnA" else 0

                def body(slab, k, j):
                    if k < COUNT[stage] - late:
                        weights(slab)
                    slab.wait_done(dve)
                    if k >= 4:
                        slab_at(stage, k - 4, l).wait_released(dve)
                    elif stage[:3] == "dnB":
                        slab_at(stage.replace("B", "A"), k, l).wait_released(dve)
                    tt(pairs[:, j, :, :], pairs[:, j, :, :], lin[slab.bank][:, :, :], ALU.add)\
                        .then_inc(s.bank_free[slab.bank], 1)
                    if n is not None and j >= 2:
                        if j == 2:
                            weights(slab)
                        norm_lo(n, (2 * j, 2 * j + 1), gx)
                        if j == 3:
                            weights(slab)
                straight(stage, body, l)
                if late and n is None:
                    weights(slab_at(stage, COUNT[stage] - 2, l))
                if n is not None:
                    norm_root(n)

            def older_taps(outs, ins_, taps, weight, sem, base, release=None):
                k = len(outs)
                for d in range(1, taps):
                    for i in range(k):
                        if d >= 2:
                            dve.wait_ge(sem, base + (d - 2) * k + i + 1)
                        ins = stt(outs[i][:, d:T], ins_[i][:, 0:T - d], weight(taps - 1 - d, i), outs[i][:, d:T],
                                  ALU.mult, ALU.add)
                        last = d == taps - 1 and i == k - 1
                        ins.then_inc(release if last and release is not None else sem, 1)
                return base + (taps - 1) * k

            def ffn(f, l=None):
                sfx, base = stage_ffn(f, l)

                def up(off):
                    def body(slab, n, j):
                        b = j % 2
                        c = off + n
                        slab.wait_done(dve)
                        tt(zz[:, j, :, :], lin[slab.bank][:, :, :], std[:, 0, 0:T].unsqueeze(1).to_broadcast([P, 2, T]),
                           ALU.mult).then_inc(s.bank_free[slab.bank], 1)
                        weights(slab)
                        if l is None:
                            dve.wait_ge(s.ffn_t0, base + c + 1)
                            older_taps([acc[:, b, 0, :]], [zz[:, j, 0, :]], FFN_TAPS,
                                       lambda k, i: pcol(f"fw{f}", k * FC + c), s.ffn_tap, 2 * (base + c))
                            dve.wait_ge(s.ffn_silu, base + c + 1)
                            value = zz[:, j, 1, :]
                        else:
                            dve.wait_ge(s.ffn2_t0, l * FC + c + 1)
                            added = older_taps([acc[:, b, 0, :], acc[:, b, 1, :]], [zz[:, j, 0, :], zz[:, j, 1, :]], FFN_TAPS,
                                               lambda k, i: pcol2(l, "fw", k * 2 * FC + i * FC + c), s.ffn2_tap,
                                               4 * (l * FC + c))
                            dve.wait_ge(s.ffn2_silu, l * FC + c + 1)
                            dve.wait_ge(s.ffn2_tap, added)
                            value = acc[:, b, 1, :]
                        dve.wait_ge(s.hid_split, base + c + 1)
                        tt(prod[:, b, :], sil[:, b, :], value, ALU.mult).then_inc(s.ffn_prod, 1)
                    return body
                slabs(dve, "upA" + sfx, up(0), l)
                add_residual("dnA" + sfx, l)
                slabs(dve, "upB" + sfx, up(UP_A), l)
                add_residual("dnB" + sfx, l)

            for j in range(4):
                dve.wait_ge(s.x_loaded[j], 16)
            dve.wait_ge(s.loaded, 32)
            dve.wait_ge(s.pads, 1)
            lam = par[:, PCOL["lam"]:PCOL["lam"] + NC4, :].rearrange("p c a -> p (c a)")
            chain = Chain(dve, s.lam_chain)
            split_lo(dve, Slab(s, 0, 0), 1)
            norm(0, lambda c: pcol("mix_g0", c))
            split_lo(dve, Slab(s, 1, 0), 1)

            def cf_u(n):
                slab = slab_at("ev_cf", n)
                dve.wait_ge(s.cf_sig, n + 1)
                tt(u_pad[:, n, CF_TAPS - 1:], lin[slab.bank][:, 0, :], sq[:, n, :], ALU.mult)\
                    .then_inc(s.bank_free[slab.bank], 1)

            for c0 in (0, 2):
                if c0 == 0:
                    cf_u(0)
                    cf_u(1)
                for c in (c0, c0 + 1):
                    slab_at("ev_cf", c).wait_released(dve)
                    ts(cf_acc[:, c, :], u_pad[:, c, CF_TAPS - 1:], pcol("cf_w", (CF_TAPS - 1) * NC4 + c), pcol("cf_b", c),
                       ALU.mult, ALU.add).then_inc(s.cf_tap, 1)
                turns = (CF_TAPS - 1) // 3
                first = 0 if c0 == 0 else CF_PE_TAPS
                before = CF_TAPS * c0 - 2 * first
                for part in ((range(0, turns // 2), range(turns // 2, turns)) if c0 == 0 else (range(first // 3, turns),)):
                    with dve.Fori(part.start, part.stop) as i:
                        for d in range(3):
                            for c in (c0, c0 + 1):
                                dve.wait_ge(s.cf_tap, before + (i * 3 + d) * 2 + c - c0 + 1)
                                stt(cf_acc[:, c, :], u_pad[:, c, bass.ds(i * 3 + d, T)], pcol("cf_w", (i * 3 + d) * NC4 + c),
                                    cf_acc[:, c, :], ALU.mult, ALU.add).then_inc(s.cf_tap, 1)
                    if c0 == 0 and part.start == 0:
                        cf_u(2)
                        cf_u(3)
            dve.wait_ge(s.cf_tap, CF_SUMS - 1)
            dve.wait_ge(s.cf_pe, 1)
            tt(cf_acc[:, 2:NC4, :], cf_acc[:, 2:NC4, :], logit[:, 0:2, :], ALU.add).then_inc(s.cf_tap, 1)
            stage_released(dve, "ev_sc")
            stage_released(dve, "ev_b")
            sc = Chain(dve, s.sc_chain)
            sc.link(tt(t_pad[:, :, SC_TAPS - 1:], sc_c[:, :, :], sc_x[:, :, :], ALU.mult))
            dve.wait_ge(s.ln_mean, 1)
            tt(diff[:, :, :], cf_acc[:, :, :], stat[:, 0:T].unsqueeze(1).to_broadcast([P, NC4, T]), ALU.subtract)\
                .then_inc(s.ln_diff, 1)
            for c in range(NC4):
                ins = ts(sc_acc[:, c, :], t_pad[:, c, 2:], pcol("sc_w", 2 * NC4 + c), None, ALU.mult)
            sc.link(ins)
            for k in (1, 0):
                for c in range(NC4):
                    ins = stt(sc_acc[:, c, :], t_pad[:, c, k:k + T], pcol("sc_w", k * NC4 + c), sc_acc[:, c, :],
                              ALU.mult, ALU.add)
                sc.link(ins)
            tt(sc_acc[:, :, :], sc_acc[:, :, :], sc_b[:, :, :], ALU.mult).then_inc(s.y_sc, 1)
            dve.wait_ge(s.ln_std, 1)
            nc.vector.reciprocal(std[:, 0, 0:T], std[:, 0, 0:T]).then_inc(s.ln_rstd, 1)
            dve.wait_ge(s.ln_rstd, 1)
            dve.wait_ge(s.ln_diff, 1)
            tt(diff[:, :, :], diff[:, :, :], std[:, 0, 0:T].unsqueeze(1).to_broadcast([P, NC4, T]), ALU.mult)\
                .then_inc(s.ln_scaled, 1)
            dve.wait_ge(s.y_sc_hi, 1)
            lo_part(nc.vector, hid_lo[:, 0:NC4, :], sc_acc[:, :, :], hid_hi[:, 0:NC4, :]).then_inc(s.y_sc_lo, 1)
            dve.wait_ge(s.u_ready, 1)
            lo_part(nc.vector, hid_lo[:, NC4:2 * NC4, :], sq[:, 0:NC4, :], hid_hi[:, NC4:2 * NC4, :]).then_inc(s.u_lo, 1)
            take_over(dve, "ev_out")
            add_residual("ev_out", None, 1)
            ffn(0)

            norm(2, lambda c: pcol("mix_g1", c), "dnB0")
            dve.wait_ge(s.loaded_later, 64)
            chain.link(stt(small[:, 4:8], lam, -1.0, lam, ALU.mult, ALU.max))
            ts(small[:, 12:16], lam, -1.0, None, ALU.mult)
            dve.wait_ge(s.lam_e, 1)
            softplus(chain, small[:, 4:8], small[:, 12:16], None, small[:, 8:12], (small[:, 58:62], small[:, 32:36]))
            chain.link(ts(small[:, 0:4], small[:, 4:8], -8.0, None, ALU.mult))
            assert chain.n == LAM_LINKS

            def lru_conv(slab, n, j):
                weights(slab)
                dve.wait_ge(s.lru_t0, n + 1)
                older_taps([lru_xc[:, n, :]], [lin[slab.bank][:, 0, :]], LRU_TAPS,
                           lambda k, i: pcol("lru_w", k * NC4 + n), s.lru_tap, 2 * n, s.bank_free[slab.bank])
            slabs(dve, "od_lru", lru_conv)

            def qk_norm(n):
                slab = slab_at("od_qk", n)
                dve.wait_ge(s.qk_std, n + 1)
                nc.vector.reciprocal(std[:, n % 2, :], std[:, n % 2, :]).then_inc(s.qk_chain, 1)
                dve.wait_ge(s.qk_chain, n + 1)
                stt(qn[:, n, :], lin[slab.bank][:, 0, :], pcol("q_g"), std[:, n % 2, 0:T], ALU.mult, ALU.mult)
                stt(kn[:, n, :], lin[slab.bank][:, 1, :], pcol("k_g"), std[:, n % 2, T:2 * T], ALU.mult, ALU.mult)\
                    .then_inc(s.bank_free[slab.bank], 1)
            lc = Chain(dve, s.lru_chain)
            for n in range(COUNT["od_qk"]):
                qk_norm(n)
                if n == 3:
                    dve.wait_ge(s.lru_i, 1)
                    stage_released(dve, "od_lru")
                    lc.link(tt(lru_i[:, :, :], lru_i[:, :, :], lru_xc[:, :, :], ALU.mult))
                    dve.wait_ge(s.lru_a, 1)
                    lc.link(tt(lru_m[:, :, :], lru_a[:, :, :], lru_a[:, :, :], ALU.mult))
                    stt(lru_m[:, :, :], lru_m[:, :, :], 1.0, lru_th[:, :, :], ALU.add, ALU.mult).then_inc(s.lru_m2, 1)

            def at_mask(u):
                t = u % 2
                n = (t + 1) * P
                dve.wait_ge(s.at_logits, u + 1)
                if u >= 2:
                    dve.wait_ge(s.at_tr, u - 1)
                sc3 = score[:, u % 2, 0:DIL_G * n].rearrange("p (g k) -> p g k", g=DIL_G)
                stt(sc3, logit[:, 0:DIL_G, 0:n], DIL_D ** -0.5,
                    dil[:, DIL_AT[t]:DIL_AT[t] + DIL_G * n].rearrange("p (g k) -> p g k", g=DIL_G), ALU.mult, ALU.add)\
                    .then_inc(s.at_masked, 1)
                dve.wait_ge(s.at_masked, u + 1)
                nc.vector.tensor_reduce(small[:, 16 + u:17 + u], score[:, u % 2, 0:DIL_G * n], AX_X, ALU.max, negate=True)\
                    .then_inc(s.at_max, 1)

            ac = Chain(dve, s.at_chain)
            at_mask(0)
            dve.wait_ge(s.lru_mult, 1)
            lc.link(tt(lru_i[:, :, :], lru_i[:, :, :], lru_th[:, :, :], ALU.mult))
            for c in range(NC4):
                ins = nc.vector.tensor_tensor_scan(lru_hs[:, c, :], lru_a[:, c, :], lru_i[:, c, :], 0.0, ALU.mult, ALU.add)
            lc.link(ins)
            tt(lru_hs[:, :, :], lru_hs[:, :, :], lru_gate[:, :, :], ALU.mult).then_inc(s.lru_y, 1)
            for u in range(2 * DIL_H):
                n = (u % 2 + 1) * P
                dve.wait_ge(s.at_exp, u + 1)
                ac.link(nc.vector.reciprocal(small[:, 32 + u:33 + u], small[:, 24 + u:25 + u]))
                ts(score[:, u % 2, 0:DIL_G * n], score[:, u % 2, 0:DIL_G * n], small[:, 32 + u:33 + u], None, ALU.mult)\
                    .then_inc(s.at_p, 1)
                if u == 0:
                    at_mask(1)
                if u + 2 < 2 * DIL_H:
                    at_mask(u + 2)
                if u == 0:
                    dve.wait_ge(s.lru_y_hi, 1)
                    lo_part(nc.vector, hid_lo[:, 0:NC4, :], lru_hs[:, :, :], hid_hi[:, 0:NC4, :]).then_inc(s.lru_y_lo, 1)
            dve.wait_ge(s.att_hi, 1)
            lo_part(nc.vector, hid_lo[:, NC4:NC4 + 2, :], acc[:, 0, :, :], hid_hi[:, NC4:NC4 + 2, :]).then_inc(s.att_lo, 1)
            take_over(dve, "od_out")
            add_residual("od_out", None, 3)
            ffn(1)

            def layer(l):
                if l == 0:
                    norm(4, lambda c: pcol2(0, "mix_g", c), "dnB1")
                else:
                    norm(4 + 2 * l, lambda c: pcol2(l, "mix_g", c), "dnB", l - 1)
                rope_unit = [0]

                def rope(out, chunks, which):
                    r = rope_unit[0]
                    rope_unit[0] += 1
                    base = 8 * 2 * l + 2 * r
                    raw, part = rope_raw[:, r % 2, 0:chunks, :], rope_t[:, 0, 0:chunks, :]
                    cos, sin = (const(f"{f}_{which}", T).unsqueeze(1).to_broadcast([P, chunks, T])
                                for f in ("cos", "sin"))
                    dve.wait_ge(s.rope_rot, 8 * l + r + 1)
                    tt(out, raw, cos, ALU.mult).then_inc(s.rope_chain, 1)
                    tt(part, stat[:, 0:chunks * T].rearrange("p (c t) -> p c t", t=T), sin, ALU.mult)\
                        .then_inc(s.rope_chain, 1)
                    dve.wait_ge(s.rope_chain, base + 2)
                    tt(out, out, part, ALU.add).then_inc(s.rope_done, 1)

                rope(ki2[:, :, :], 1, "idx")
                dt, adt, cum = (dtb[0:SH, i, :] for i in range(3))
                arg, mag = dscr[0:SH, 2, :], dscr[0:SH, 3, :]
                slab_at("kidtwi", 0, l).wait_released(dve)
                stt(mag, arg, -1.0, arg, ALU.mult, ALU.max).then_inc(s.dt_abs, 1)
                dve.wait_ge(s.dt_e, l + 1)
                ch = Chain(dve, s.dt_chain, DT_LINKS * l)
                softplus(ch, dt, arg, None, mag, (adt, cum))
                dve.wait_ge(s.a_exp, l + 1)
                ch.link(ts(adt, dt, small[0:SH, 40:41], -1.0, ALU.mult, ALU.mult))
                ch.link(nc.vector.tensor_tensor_scan(cum, adt, adt, 0.0, ALU.add, ALU.min))
                assert ch.n == DT_LINKS

                ix = Chain(dve, s.ix_chain, IX_LINKS * l)
                dve.wait_ge(s.wi_copied, l + 1)

                def index_scores(t, half):
                    n = (t + 1) * P
                    row = ix_sc[:, 0, 0:n]
                    b = 2 * t + half
                    dve.wait_ge(s.ix_rel, 4 * l + b + 1)
                    for i in range(4):
                        head, rel = 4 * half + i, ix_rel[:, b, 2 * (i % 2) + i // 2, 0:n]
                        w = small[:, 42 + t * IH + head:43 + t * IH + head]
                        if head == 0:
                            ix.link(ts(row, rel, w, None, ALU.mult))
                        else:
                            ix.link(stt(row, rel, w, row, ALU.mult, ALU.add))
                    if half == 1:
                        ix.link(tt(row, row, const(f"causal{t}", n), ALU.add))

                def top_eights(t, rounds):
                    n = (t + 1) * P
                    for r in rounds:
                        now = ix_sc[:, 0, 0:n] if r == 0 else ix_w[:, (r - 1) % 2, 0:n]
                        ix.link(nc.vector.max(small[:, 0:8], now))
                        ix.link(nc.vector.match_replace(ix_w[:, r % 2, 0:n], small[:, 0:8], now, TAKEN))

                def selection(t):
                    n = (t + 1) * P
                    last = ix_w[:, (TOPK // 8 - 1) % 2, 0:n]
                    ix.link(ts(sel[:, t, 0:n], last, TAKEN / 2, NEG, ALU.is_gt, ALU.mult))
                    ix.link(tt(sel[:, t, 0:n], sel[:, t, 0:n], const(f"causal{t}", n), ALU.add))

                for n in range(2):
                    rope(qi2[:, 2 * n:2 * n + 2, :], 2, "idx")
                take_over(dve, "k", l)
                weights(slab_at("k", 0, l))
                rope(k2[:, :, :], 2, "attn")
                weights(slab_at("q", 0, l))
                rounds = TOPK // 8
                for n in range(4):
                    rope(q2[:, 2 * n:2 * n + 2, :], 2, "attn")
                    weights(slab_at("q", n + 1, l) if n < 3 else slab_at("v", 0, l))
                    if n < 2:
                        index_scores(0, n)
                    elif n == 2:
                        top_eights(0, range(0, rounds // 2))
                    else:
                        top_eights(0, range(rounds // 2, rounds))
                        selection(0)

                def da_mask(u):
                    t = u // 2
                    n = (t + 1) * P
                    dve.wait_ge(s.da_logits, 4 * l + u + 1)
                    if u >= 2:
                        dve.wait_ge(s.da_tr, 4 * l + u - 1)
                    sc4 = da_score[u % 2][:, :, 0:n]
                    for i in range(QPK):
                        ins = stt(sc4[:, i, :], logit[:, i, 0:n], HD ** -0.5, sel[:, t, 0:n], ALU.mult, ALU.add)
                    ins.then_inc(s.da_masked, 1)
                    dve.wait_ge(s.da_masked, 4 * l + u + 1)
                    nc.vector.tensor_reduce(small[:, 16:20], sc4, AX_X, ALU.max, negate=True).then_inc(s.da_max, 1)

                dc = Chain(dve, s.da_chain, 4 * l)

                def da_probs(u):
                    sc4 = da_score[u % 2][:, :, 0:(u // 2 + 1) * P]
                    dve.wait_ge(s.da_exp, 4 * l + u + 1)
                    dc.link(nc.vector.reciprocal(small[:, 32:36], small[:, 24:28]))
                    for i in range(QPK):
                        ins = ts(sc4[:, i, :], sc4[:, i, :], small[:, 32 + i:33 + i], None, ALU.mult)
                    ins.then_inc(s.da_p, 1)

                def xbc_taps(slab, n, j):
                    b = j % 2
                    weights(slab)
                    dve.wait_ge(s.xbc_t0, 12 * l + n + 1)
                    older_taps([acc[:, b, i, :] for i in range(2)], [lin[slab.bank][:, i, :] for i in range(2)],
                               SSD_TAPS, lambda k, i: pcol2(l, "ssd_w", k * XBC_CH + 2 * n + i), s.xbc_tap,
                               5 * (12 * l + n), s.bank_free[slab.bank])
                    if n < 2:
                        index_scores(1, n)
                    elif n < 2 + rounds:
                        top_eights(1, range(n - 2, n - 1))
                    elif n == 2 + rounds:
                        selection(1)
                    if n == 3:
                        da_mask(0)
                    if n == 7:
                        da_probs(0)
                assert COUNT["xbc"] > 2 + rounds
                straight("xbc", xbc_taps, l)
                assert ix.n == IX_LINKS

                for u in range(4):
                    if u < 3:
                        da_mask(u + 1)
                    weights(slab_at("z", 2 * u, l))
                    if u < 3:
                        da_probs(u + 1)
                    weights(slab_at("z", 2 * u + 1, l))

                dve.wait_ge(s.dt_tok, l + 1)

                def ssd_seg(c, j, i):
                    head = 2 * c + i
                    dve.wait_ge(s.ssd_abc, XCH * l + c + 1)
                    for t, (lo, n) in enumerate(((0, T), (T, P))):
                        ins = ts(seg[:, i, lo:lo + n], logit[:, 2 * (j % 2) + i, T - n:T], dt_tok[:, 1, t, bass.ds(head, 1)],
                                 0.0, ALU.subtract, ALU.min)
                    ins.then_inc(s.ssd_seg, 1)

                def ssd_m(c, j, i):
                    head = 2 * c + i
                    dve.wait_ge(s.ssd_exp, SH * l + head + 1)
                    for t, (lo, n) in enumerate(((0, T), (T, P))):
                        ins = stt(m_buf[:, 2 * (j % 2) + i, lo:lo + n], seg_e[:, i, lo:lo + n],
                                  dt_tok[:, 0, t, bass.ds(head, 1)], cbm[:, lo:lo + n], ALU.mult, ALU.mult)
                    ins.then_inc(s.ssd_m, 1)

                def ssd_out(c, j):
                    if not (isinstance(c, int) and c < 2):
                        dve.wait_ge(s.ssd_ydone, XCH * l + c - 1)
                    dve.wait_ge(s.ssd_y, XCH * l + c + 1)
                    stt(y_raw[:, j % 2, :], xbc[:, c, :], pcol2(l, "ssd_d", c), (tr, stat)[j % 2][:, 0:T],
                        ALU.mult, ALU.add).then_inc(s.ssd_raw, 1)

                def ssd_group(g, first):
                    dve.wait_ge(s.ssd_cb, SG * l + g + 1)
                    tt(cbm[:, 0:T], tr[:, 0:T], const("tril", T + P)[:, 0:T], ALU.mult)
                    tt(cbm[:, T:T + P], tr[:, T:T + P], const("tril", T + P)[:, T:], ALU.mult).then_inc(s.ssd_cbm, 1)
                    dve.wait_ge(s.ssd_cbm, SG * l + g + 1)
                    for j in range(4):
                        c = 4 * g + j
                        ssd_seg(c, j, 0)
                        ssd_seg(c, j, 1)
                        ssd_m(c, j, 0)
                        ssd_m(c, j, 1)
                        if j >= 1 or not first:
                            ssd_out(c - 1, j + 3)
                ssd_group(0, True)
                with dve.Fori(1, SG) as g:
                    ssd_group(g, False)
                ssd_out(XCH - 1, 3)
                dve.wait_ge(s.ssd_raw, XCH * (l + 1))
                dve.wait_ge(s.ssd_ydone, XCH * (l + 1) - 1)
                tt(zs[:, XCH - 1, :], y_raw[:, 1, :], zs[:, XCH - 1, :], ALU.mult).then_inc(s.ssd_ydone, 1)
                take_over(dve, "pa", l)

                def pa(slab, n):
                    weights(slab)
                    slab.wait_done(dve)
                    tt(merged[:, 2 * n:2 * n + 2, :], lin[slab.bank][:, :, :], gates[:, 2 * n:2 * n + 2, 0, :], ALU.mult)\
                        .then_inc(s.bank_free[slab.bank], 1)

                def bn_rest(g):
                    dve.wait_ge(s.bn_hi, SG * l + g + 1)
                    part = (slice(None), slice(4 * (g % 2), 4 * (g % 2) + 4), slice(None))
                    lo, hi = (h_lo, h_hi) if g < 2 else (hid_lo, hid_hi)
                    lo_part(nc.vector, lo[part], zs[:, 4 * g:4 * g + 4, :], hi[part]).then_inc(s.bn_lo, 1)

                for g in range(SG):
                    pa(slab_at("pa", g, l), g)
                    dve.wait_ge(s.bn_std, SG * l + g + 1)
                    nc.vector.reciprocal(std[:, g % 2, 0:T], std[:, g % 2, 0:T]).then_inc(s.bn_chain, 1)
                    dve.wait_ge(s.bn_chain, 2 * (SG * l + g) + 1)
                    for c in range(4 * g, 4 * g + 4):
                        ins = stt(zs[:, c, :], zs[:, c, :], pcol2(l, "ssd_norm", c), std[:, g % 2, 0:T], ALU.mult, ALU.mult)
                    ins.then_inc(s.bn_chain, 1)
                    if g in (1, 2):
                        bn_rest(g - 1)
                bn_rest(2)
                bn_rest(3)
                stage_released(dve, "pa", l)

                def merged_rest(j):
                    dve.wait_ge(s.merged_hi, 4 * l + j + 1)
                    at = MERGED[2 * j]
                    lo_part(nc.vector, hid_lo[:, at:at + 2, :], merged[:, 2 * j:2 * j + 2, :], hid_hi[:, at:at + 2, :])\
                        .then_inc(s.merged_lo, 1)

                pc = Chain(dve, s.ps_chain, 8 * l)

                def ps(slab, n, j):
                    if n < 6:
                        weights(slab)
                    slab.wait_done(dve)
                    if n >= 4:
                        slab_at("ps", n - 4, l).wait_released(dve)
                    part = acc[:, n % 2, :, :]
                    pc.link(tt(part, lin[slab.bank][:, :, :], gates[:, 2 * j:2 * j + 2, 1, :], ALU.mult))
                    tt(merged[:, 2 * j:2 * j + 2, :], merged[:, 2 * j:2 * j + 2, :], part, ALU.add)\
                        .then_inc(s.bank_free[slab.bank], 1)
                    if n >= 5:
                        merged_rest(j - 1)
                    if n >= 6:
                        weights(slab)
                straight("ps", ps, l)
                merged_rest(3)
                add_residual("out", l, 5 + 2 * l)
                ffn(None, l)

            for l in range(2):
                layer(l)
            dve.wait_ge(s.norm_std, 9)
            nc.vector.reciprocal(std[:, 0, 0:T], std[:, 0, 0:T]).then_inc(s.norm_rstd, 1)
            dve.wait_ge(s.norm_rstd, 9)
            for half in range(2):
                for c in range(half * DC // 2, (half + 1) * DC // 2):
                    ins = stt(sq[:, c, :], x[:, c, :], pcol("final_g", c), std[:, 0, 0:T], ALU.mult, ALU.mult)
                ins.then_inc(s.final, 1)


def constants():
    c = np.zeros((P, NCONST), np.float32)
    dil = np.zeros((P, NDIL), np.float32)

    def put(name, a):
        c[:a.shape[0], CCOL[name]:CCOL[name] + a.shape[1]] = a

    put("ident", np.eye(P))
    put("mean1024", np.full((P, P), 1 / 1024))
    put("mean512", np.full((P, P), 1 / 512))
    put("mean64", np.kron(np.eye(2), np.full((64, 64), 1 / 64)))
    for name, dim, heads in (("attn", HD, 1), ("idx", ID, 2)):
        rot = dim // ROPE_FRACTION
        half = rot // 2
        inv = np.float32(ROPE_THETA) ** (-np.arange(0, rot, 2, dtype=np.float32) / np.float32(rot))
        ang = np.arange(T, dtype=np.float32)[None, :] * inv.astype(np.float32)[:, None]
        swap, cos, sin = np.zeros((dim, dim)), np.ones((dim, T), np.float32), np.zeros((dim, T), np.float32)
        for i in range(half):
            swap[i, i + half] = swap[i + half, i] = 1
        cos[0:half] = cos[half:rot] = np.cos(ang)
        sin[0:half], sin[half:rot] = -np.sin(ang), np.sin(ang)
        put(f"swap_{name}", np.kron(np.eye(heads), swap))
        put(f"cos_{name}", np.tile(cos, (heads, 1)))
        put(f"sin_{name}", np.tile(sin, (heads, 1)))
    q, k = np.arange(T)[:, None], np.arange(T)[None, :]
    for t in range(2):
        rows, n = slice(t * P, (t + 1) * P), (t + 1) * P
        seen = [(k <= q) & (q - k <= w) & ((q - k) % d == 0) for w, d in DIL]
        dil[:, DIL_AT[t]:DIL_AT[t] + DIL_G * n] = np.concatenate([np.where(m, 0.0, NEG)[rows, :n] for m in seen], axis=1)
        put(f"causal{t}", np.where(k <= q, 0.0, NEG)[rows, :n])
    after = (k >= q).astype(np.float32)
    put("tril", np.concatenate([after[0:P, :], after[P:, P:]], axis=1))
    return c, dil


def slab_of(w, cols, chunks=None):
    kc = w.shape[0] // P
    w = w.reshape(kc, P, w.shape[1])
    return np.stack([np.ascontiguousarray(w[:, :, c].transpose(1, 0, 2)).reshape(P, -1) for c in cols])


def tile(n, at=0):
    return np.arange(at + n * P, at + n * P + P)


def pair(a, b, at=0, at_b=None):
    return np.concatenate([tile(a, at), tile(b, at if at_b is None else at_b)])


def pairs(n, at=0):
    return [pair(2 * j, 2 * j + 1, at) for j in range(n // 2)]


def down_slabs(w, groups):
    out = []
    for c0, n in groups:
        part = slab_of(w[c0 * P:(c0 + n) * P], pairs(DC))
        out.append(np.pad(part, ((0, 0), (0, 0), (0, KC * 256 - part.shape[2]))))
    return np.concatenate(out)


def by_channel(a):
    a = a.reshape(-1, a.shape[-1] // P, P)
    return a.transpose(2, 0, 1).reshape(P, -1)


def column(a):
    return np.pad(a.reshape(-1, 1), ((0, P - a.size), (0, 0)))


_OUT = (1, T, D)


def kernel(**inputs):
    import concourse.bacc as bacc
    from concourse.bass_utils import run_bass_kernel_spmd

    i = {k: np.asarray(v) for k, v in inputs.items()}
    arrays = {"x": np.ascontiguousarray(i["x"][0].T.reshape(DC, P, T).transpose(1, 0, 2))}
    arrays["consts"], arrays["dil"] = constants()
    ev, od = i["ev_w_in"][0], i["od_w_in"][0]
    arrays["ev_cf"] = slab_of(ev, [pair(c, c, 3 * SC, 3 * SC + CF) for c in range(NC4)])
    arrays["ev_sc"] = slab_of(ev, [pair(c, c, SC, 2 * SC) for c in range(NC4)])
    arrays["ev_b"] = slab_of(ev, pairs(NC4))
    arrays["ev_out"] = slab_of(i["ev_w_out"][0], pairs(DC))
    arrays["od_lru"] = slab_of(od, [pair(c, c, 0, LRU) for c in range(NC4)])
    arrays["od_qk"] = slab_of(od, [pair(c, c, 2 * LRU, 2 * LRU + DIL_W) for c in range(DIL_W // P)])
    arrays["od_v"] = slab_of(od, pairs(DIL_W // P, 2 * LRU + 2 * DIL_W))
    arrays["od_out"] = slab_of(i["od_w_out"][0], pairs(DC))
    for f in range(2):
        both = np.concatenate([i["ffn_w_gate"][f], i["ffn_w_up"][f]], axis=1)
        arrays[f"upA{f}"], arrays[f"upB{f}"] = (slab_of(both, [pair(c, c, 0, FF) for c in part]) for part in UP_CHUNKS)
        arrays[f"dnA{f}"] = down_slabs(i["ffn_w_down"][f], DOWN_GROUPS[0:1])
        arrays[f"dnB{f}"] = down_slabs(i["ffn_w_down"][f], DOWN_GROUPS[1:])
    at = np.cumsum((0,) + IN_SPLITS)
    stages = {name: [] for name, _ in SECOND}
    for l in range(2):
        w = i["w_in_2"][l]
        ki = np.arange(at[4], at[5])
        dt, wi = np.arange(at[8], at[9]), np.arange(at[5], at[6])
        unused = 256 - P - SH - IH
        stages["kidtwi"].append(slab_of(np.concatenate([w, np.zeros((D, unused), np.float32)], axis=1),
                                        [np.concatenate([ki, ki, dt, wi, w.shape[1] + np.arange(unused)])]))
        stages["qi"].append(slab_of(w, pairs(4, at[3])))
        stages["q"].append(slab_of(w, pairs(8, at[0])))
        stages["k"].append(slab_of(w, pairs(2, at[1])))
        stages["v"].append(slab_of(w, pairs(2, at[2])))
        stages["xbc"].append(slab_of(w, pairs(XBC_CH, at[7])))
        stages["z"].append(slab_of(w, pairs(XCH, at[6])))
        stages["gates"].append(slab_of(w, [pair(m, m, at[9], at[10]) for m in range(DC)]))
        stages["pa"].append(slab_of(i["w_proj_attn_2"][l], pairs(DC)))
        stages["ps"].append(down_slabs(i["w_proj_ssd_2"][l], ((0, 8), (8, 8))))
        stages["out"].append(slab_of(i["w_out_2"][l], pairs(DC)))
        for part, name in zip(UP_CHUNKS, ("upA", "upB")):
            stages[name].append(slab_of(i["ffn_w_up_2"][l], [pair(c, c, 0, FF) for c in part]))
        stages["dnA"].append(down_slabs(i["ffn_w_down_2"][l], DOWN_GROUPS[0:1]))
        stages["dnB"].append(down_slabs(i["ffn_w_down_2"][l], DOWN_GROUPS[1:]))
    for name, parts in stages.items():
        arrays[name] = np.concatenate(parts)

    first = [i["mix_norm_g"][0], i["ffn_norm_g"][0], i["mix_norm_g"][1], i["ffn_norm_g"][1], i["ev_sc_conv_w"][0],
             i["ev_cf_conv_w"][0], i["ev_cf_conv_b"][0], i["ev_cf_ln_g"][0], i["ev_cf_ln_b"][0], i["od_lru_conv_w"][0],
             i["od_lru_conv_b"][0], i["od_lru_ba"][0], i["od_lru_bx"][0], i["od_lru_lam"][0],
             np.tile(i["od_q_norm_g"][0], 2), np.tile(i["od_k_norm_g"][0], 2), i["ffn_conv_w"][0], i["ffn_conv_b"][0],
             i["ffn_conv_w"][1], i["ffn_conv_b"][1], i["norm_final_w_2"]]
    cols = [by_channel(a) for a in first]
    for l in range(2):
        cols += [by_channel(i[n][l]) for n in ("norm_mix_w_2", "norm_ffn_w_2", "ssd_conv_w_2", "ssd_conv_b_2", "ssd_norm_w_2")]
        cols.append(by_channel(np.repeat(i["ssd_d_2"][l], XI // SH)))
        cols += [column(i["ssd_dt_bias_2"][l]), column(i["ssd_a_log_2"][l])]
        cols += [by_channel(i["ffn_conv_w_2"][l]), by_channel(i["ffn_conv_b_2"][l])]
    arrays["params"] = np.ascontiguousarray(np.concatenate(cols, axis=1))
    assert arrays["params"].shape == (P, NPARAM)
    gate_w = np.zeros((P, 2 * NC4, P), np.float32)
    for n, w in enumerate((i["od_lru_wa"][0], i["od_lru_wx"][0])):
        for head in range(8):
            lo = 64 * (head % 2)
            gate_w[lo:lo + 64, NC4 * n + head // 2, lo:lo + 64] = w[head]
    arrays["gate_w"] = gate_w

    nc = bacc.Bacc("TRN2", target_bir_lowering=False, num_devices=1)
    arrays = {f"in_{k}": np.ascontiguousarray(a, dtype=np.float32) for k, a in arrays.items()}
    dram = {k[3:]: nc.dram_tensor(k, a.shape, F32, kind="ExternalInput").ap() for k, a in arrays.items()}
    dram["result"] = nc.dram_tensor("out_0", (P, DC, T), F32, kind="ExternalOutput").ap()
    build(nc, dram)
    got = run_bass_kernel_spmd(nc, [arrays], core_ids=[0]).results[0]["out_0"]
    return np.ascontiguousarray(got.transpose(1, 0, 2).reshape(D, T).T).reshape(_OUT)
```
